# Optimizing a Trainium2 kernel written in Bass

```python
import math
import jax, jax.numpy as jnp
from jax import lax
import numpy as np

D_MODEL = 1024
BATCH = 1
SEQ = 256
DEPTH = 2

HEAD_DIM = 64
N_HEADS_A = 4
N_HEADS_B = 6
N_HEADS_C = 6
WIDTH_A = N_HEADS_A * HEAD_DIM
WIDTH_B = N_HEADS_B * HEAD_DIM
WIDTH_C = N_HEADS_C * HEAD_DIM
MIX_WIDTH = WIDTH_A + WIDTH_B + WIDTH_C
DIFF_DIM = HEAD_DIM // 2
ROPE_THETA = 500000.0
ROPE_FRACTION = 4
Q_BLOCK = 128
DILATED_CONFIGS = ((128, 1), (512, 4), (2048, 16))
SW_BLOCK = 64
GRID_W = 64
NA_ROWS_MAX = 8
NA_COLS = 16
D_FF_DENSE = 2816
N_EXPERTS = 8
TOP_K = 2
D_FF_EXPERT = 3584
N_DENSE = (DEPTH + 1) // 2
N_MOE = DEPTH // 2
DEEPNORM_ALPHA = (2 * DEPTH) ** 0.25
DEEPNORM_BETA = (8 * DEPTH) ** -0.25
LN_EPS = 1e-5
NEG = -1e30

kernel_name = 'hybrid_diff_dilated_natten_moe_encoder'

def layer_norm(x, g, b):
    xf = x.astype(jnp.float32)
    mu = jnp.mean(xf, axis=-1, keepdims=True)
    var = jnp.mean(jnp.square(xf - mu), axis=-1, keepdims=True)
    y = (xf - mu) * lax.rsqrt(var + LN_EPS) * g.astype(jnp.float32) + b.astype(jnp.float32)
    return y.astype(x.dtype)

def rms_norm(x, g):
    xf = x.astype(jnp.float32)
    y = xf * lax.rsqrt(jnp.mean(xf * xf, axis=-1, keepdims=True) + LN_EPS) * g.astype(jnp.float32)
    return y.astype(x.dtype)

def rope_tables(seq, rot_dim):
    inv = ROPE_THETA ** (-jnp.arange(0, rot_dim, 2, dtype=jnp.float32) / rot_dim)
    ang = jnp.arange(seq, dtype=jnp.float32)[:, None] * inv[None, :]
    return jnp.cos(ang), jnp.sin(ang)

def apply_partial_rope(x, cos, sin):
    half = cos.shape[-1]
    c = cos.astype(x.dtype)
    s = sin.astype(x.dtype)
    x1, x2, xp = x[..., :half], x[..., half:2 * half], x[..., 2 * half:]
    return jnp.concatenate([x1 * c - x2 * s, x2 * c + x1 * s, xp], axis=-1)

def diff_attention(q, k, v, lam, lam_init, norm_g):
    B, H, _, S, dq = q.shape
    nb = S // Q_BLOCK
    qb = q.reshape(B, H, 2, nb, Q_BLOCK, dq).transpose(3, 0, 1, 2, 4, 5)
    scale = dq ** -0.5

    def block(q_blk):
        s = jnp.einsum('bhmqd,bhmkd->bhmqk', q_blk, k).astype(jnp.float32) * scale
        p = jax.nn.softmax(s, axis=-1)
        pd = p[:, :, 0] - lam * p[:, :, 1]
        return jnp.einsum('bhqk,bhkd->bhqd', pd.astype(v.dtype), v)

    o = lax.map(block, qb)
    o = o.transpose(1, 2, 0, 3, 4).reshape(B, H, S, v.shape[-1])
    return rms_norm(o, norm_g) * (1.0 - lam_init)

def dilated_branch(q, k, v, window, dilation):
    B, H, S, dh = q.shape
    half = window // (2 * dilation)
    assert half <= SW_BLOCK
    L = S // dilation
    nb = -(-L // SW_BLOCK)
    Lp = nb * SW_BLOCK

    def by_residue(t):
        return t.reshape(B, H, L, dilation, dh).transpose(0, 1, 3, 2, 4)

    pad0 = ((0, 0), (0, 0), (0, 0))
    qs = jnp.pad(by_residue(q), pad0 + ((0, Lp - L), (0, 0)))
    ks = jnp.pad(by_residue(k), pad0 + ((SW_BLOCK, Lp - L + SW_BLOCK), (0, 0)))
    vs = jnp.pad(by_residue(v), pad0 + ((SW_BLOCK, Lp - L + SW_BLOCK), (0, 0)))
    qb = qs.reshape(B, H, dilation, nb, SW_BLOCK, dh)

    def band(t):
        tb = t.reshape(B, H, dilation, nb + 2, SW_BLOCK, dh)
        return jnp.concatenate([tb[:, :, :, j:j + nb] for j in range(3)], axis=-2)

    kb, vb = band(ks), band(vs)
    qpos = np.arange(nb)[:, None] * SW_BLOCK + np.arange(SW_BLOCK)[None, :]
    kpos = (np.arange(nb)[:, None] - 1) * SW_BLOCK + np.arange(3 * SW_BLOCK)[None, :]
    delta = kpos[:, None, :] - qpos[:, :, None]
    mask = (np.abs(delta) <= half) & (kpos[:, None, :] >= 0) & (kpos[:, None, :] < L)
    s = jnp.einsum('bhrnqd,bhrnkd->bhrnqk', qb, kb).astype(jnp.float32) * dh ** -0.5
    s = jnp.where(mask, s, NEG)
    lse = jax.nn.logsumexp(s, axis=-1)
    p = jnp.exp(s - lse[..., None])
    o = jnp.einsum('bhrnqk,bhrnkd->bhrnqd', p.astype(v.dtype), vb)
    o = o.reshape(B, H, dilation, Lp, dh)[:, :, :, :L].transpose(0, 1, 3, 2, 4).reshape(B, H, S, dh)
    lse = lse.reshape(B, H, dilation, Lp)[:, :, :, :L].transpose(0, 1, 3, 2).reshape(B, H, S)
    return o, lse

def dilated_attention(q, k, v):
    outs, lses = [], []
    for window, dilation in DILATED_CONFIGS:
        o, lse = dilated_branch(q, k, v, window, dilation)
        outs.append(o)
        lses.append(lse)
    wts = jax.nn.softmax(jnp.stack(lses, axis=0), axis=0)
    return jnp.einsum('gbhs,gbhsd->bhsd', wts.astype(v.dtype), jnp.stack(outs, axis=0))

def neighbourhood_attention(q, k, v, rpb):
    B, H, S, dh = q.shape
    rows = S // GRID_W
    kh = min(NA_ROWS_MAX, rows)
    kw = NA_COLS
    r = np.arange(rows)
    row_start = np.clip(r - kh // 2, 0, rows - kh)
    key_rows = row_start[:, None] + np.arange(kh)[None, :]
    tok = (key_rows[:, :, None] * GRID_W + np.arange(GRID_W)[None, None, :]).reshape(rows, kh * GRID_W)
    kg = jnp.take(k, tok, axis=2)
    vg = jnp.take(v, tok, axis=2)
    qg = q.reshape(B, H, rows, GRID_W, dh)
    c = np.arange(GRID_W)
    col_start = np.clip(c - kw // 2, 0, GRID_W - kw)
    kcol = np.tile(np.arange(GRID_W), kh)
    valid = (kcol[None, :] >= col_start[:, None]) & (kcol[None, :] < col_start[:, None] + kw)
    ridx = np.repeat(key_rows, GRID_W, axis=1) - r[:, None] + NA_ROWS_MAX - 1
    cidx = np.clip(kcol[None, :] - c[:, None] + kw - 1, 0, 2 * kw - 2)
    bias = rpb[:, ridx[:, None, :], cidx[None, :, :]].astype(jnp.float32)
    bias = jnp.where(valid[None, None], bias, NEG)
    s = jnp.einsum('bhrqd,bhrkd->bhrqk', qg, kg).astype(jnp.float32) * dh ** -0.5 + bias[None]
    p = jax.nn.softmax(s, axis=-1)
    o = jnp.einsum('bhrqk,bhrkd->bhrqd', p.astype(v.dtype), vg)
    return o.reshape(B, H, S, dh)

def hybrid_mixer(x, w_in, w_out, beta_mix, diff_lambda, diff_norm_g, na_rpb, lam_init, rope_a, rope_b):
    B, S, _ = x.shape
    proj = x @ w_in
    pa, pb, pc = jnp.split(proj, [3 * WIDTH_A, 3 * WIDTH_A + 3 * WIDTH_B], axis=-1)

    def heads(t, n):
        return t.reshape(B, S, n, HEAD_DIM).transpose(0, 2, 1, 3)

    def diff_heads(t):
        return t.reshape(B, S, N_HEADS_A, 2, DIFF_DIM).transpose(0, 2, 3, 1, 4)

    qa, ka, va = jnp.split(pa, 3, axis=-1)
    qa = apply_partial_rope(diff_heads(qa), *rope_a)
    ka = apply_partial_rope(diff_heads(ka), *rope_a)
    lam_p = diff_lambda.astype(jnp.float32)
    lam = jnp.exp(jnp.sum(lam_p[0] * lam_p[1])) - jnp.exp(jnp.sum(lam_p[2] * lam_p[3])) + lam_init
    oa = diff_attention(qa, ka, heads(va, N_HEADS_A), lam, lam_init, diff_norm_g)

    qb, kb, vb = jnp.split(pb, 3, axis=-1)
    qb = apply_partial_rope(heads(qb, N_HEADS_B), *rope_b)
    kb = apply_partial_rope(heads(kb, N_HEADS_B), *rope_b)
    ob = dilated_attention(qb, kb, heads(vb, N_HEADS_B))

    qc, kc, vc = jnp.split(pc, 3, axis=-1)
    oc = neighbourhood_attention(heads(qc, N_HEADS_C), heads(kc, N_HEADS_C), heads(vc, N_HEADS_C), na_rpb)

    merged = jnp.concatenate([oa, ob, oc], axis=1).transpose(0, 2, 1, 3).reshape(B, S, MIX_WIDTH)
    return (merged * beta_mix) @ w_out

def swiglu(x, w_gate, w_up, w_down):
    return (jax.nn.silu(x @ w_gate) * (x @ w_up)) @ w_down

def moe_swiglu(x, w_router, w_gate, w_up, w_down):
    logits = (x @ w_router).astype(jnp.float32)
    top_v, top_i = lax.top_k(logits, TOP_K)
    gates = jax.nn.softmax(top_v, axis=-1)
    combine = jnp.sum(jax.nn.one_hot(top_i, N_EXPERTS, dtype=jnp.float32) * gates[..., None], axis=-2)
    out = jnp.zeros_like(x)
    for e in range(N_EXPERTS):
        out = out + combine[..., e:e + 1].astype(x.dtype) * swiglu(x, w_gate[e], w_up[e], w_down[e])
    return out

def setup_inputs(seed: int = 0) -> dict:
    key = jax.random.key(seed)
    ks = jax.random.split(key, 18)
    D = D_MODEL
    f32 = jnp.float32

    def nrm(k, shape, scale):
        return jax.random.normal(k, shape, f32) * scale

    col_scale = np.ones(3 * MIX_WIDTH, np.float32)
    off = 0
    for w in (WIDTH_A, WIDTH_B, WIDTH_C):
        col_scale[off + 2 * w: off + 3 * w] = DEEPNORM_BETA
        off += 3 * w
    return {
        'x': nrm(ks[0], (BATCH, SEQ, D), 1.0),
        'w_in': nrm(ks[1], (DEPTH, D, 3 * MIX_WIDTH), D ** -0.5) * jnp.asarray(col_scale),
        'w_out': nrm(ks[2], (DEPTH, MIX_WIDTH, D), MIX_WIDTH ** -0.5 * DEEPNORM_BETA),
        'beta_mix': 1.0 + nrm(ks[3], (DEPTH, MIX_WIDTH), 0.02),
        'diff_lambda': nrm(ks[4], (DEPTH, 4, DIFF_DIM), 0.1),
        'diff_norm_g': 1.0 + nrm(ks[5], (DEPTH, HEAD_DIM), 0.02),
        'na_rpb': nrm(ks[6], (DEPTH, N_HEADS_C, 2 * NA_ROWS_MAX - 1, 2 * NA_COLS - 1), 0.02),
        'ln1_g': 1.0 + nrm(ks[7], (DEPTH, D), 0.02),
        'ln1_b': nrm(ks[8], (DEPTH, D), 0.02),
        'ln2_g': 1.0 + nrm(ks[9], (DEPTH, D), 0.02),
        'ln2_b': nrm(ks[10], (DEPTH, D), 0.02),
        'ffn_w_gate': nrm(ks[11], (N_DENSE, D, D_FF_DENSE), D ** -0.5),
        'ffn_w_up': nrm(ks[12], (N_DENSE, D, D_FF_DENSE), D ** -0.5),
        'ffn_w_down': nrm(ks[13], (N_DENSE, D_FF_DENSE, D), D_FF_DENSE ** -0.5 * DEEPNORM_BETA),
        'moe_w_router': nrm(ks[14], (N_MOE, D, N_EXPERTS), D ** -0.5),
        'moe_w_gate': nrm(ks[15], (N_MOE, N_EXPERTS, D, D_FF_EXPERT), D ** -0.5),
        'moe_w_up': nrm(ks[16], (N_MOE, N_EXPERTS, D, D_FF_EXPERT), D ** -0.5),
        'moe_w_down': nrm(ks[17], (N_MOE, N_EXPERTS, D_FF_EXPERT, D), D_FF_EXPERT ** -0.5 * DEEPNORM_BETA),
    }

def reference(x, w_in, w_out, beta_mix, diff_lambda, diff_norm_g, na_rpb, ln1_g, ln1_b, ln2_g, ln2_b,
              ffn_w_gate, ffn_w_up, ffn_w_down, moe_w_router, moe_w_gate, moe_w_up, moe_w_down):
    S = x.shape[1]
    rope_a = rope_tables(S, DIFF_DIM // ROPE_FRACTION)
    rope_b = rope_tables(S, HEAD_DIM // ROPE_FRACTION)
    for l in range(DEPTH):
        lam_init = 0.8 - 0.6 * math.exp(-0.3 * l)
        mix = hybrid_mixer(x, w_in[l], w_out[l], beta_mix[l], diff_lambda[l], diff_norm_g[l], na_rpb[l],
                           lam_init, rope_a, rope_b)
        x = layer_norm(DEEPNORM_ALPHA * x + mix, ln1_g[l], ln1_b[l])
        if l % 2 == 0:
            j = l // 2
            f = swiglu(x, ffn_w_gate[j], ffn_w_up[j], ffn_w_down[j])
        else:
            j = l // 2
            f = moe_swiglu(x, moe_w_router[j], moe_w_gate[j], moe_w_up[j], moe_w_down[j])
        x = layer_norm(DEEPNORM_ALPHA * x + f, ln2_g[l], ln2_b[l])
    return x


_drawn_inputs = setup_inputs


def setup_inputs(seed=0):
    import zlib

    import numpy as np

    out = dict(_drawn_inputs(seed))
    spreads = {}
    factors = {'beta_mix': 7.239, 'diff_lambda': 3.895, 'diff_norm_g': 8.0, 'na_rpb': 64.0}
    for name, (base, spread) in spreads.items():
        noise = np.random.default_rng([zlib.crc32(name.encode()), seed]).standard_normal(out[name].shape)
        drawn = base * np.exp(spread * noise) if base else spread * noise
        out[name] = __import__('jax').numpy.asarray(drawn.astype(out[name].dtype))
    for name, factor in factors.items():
        out[name] = (out[name] * factor).astype(out[name].dtype)
    return out
```

```python
from contextlib import ExitStack
import math

import numpy as np
import concourse.bass as bass
from concourse import mybir

P = 128
D = 1024
SEQ = 256
NT = SEQ // P
KT = D // P
DEPTH = 2
HD = 64
HA, HB, HC = 4, 6, 6
WA, WB, WC = HA * HD, HB * HD, HC * HD
QKV = 3 * D
DIFF = HD // 2
GRID_W, NA_ROWS, NA_COLS = 64, 8, 16
ROWS = SEQ // GRID_W
F_DENSE, F_EXP, NE = 2816, 3584, 8
ALPHA = (2 * DEPTH) ** 0.25
EPS = 1e-5
NEG = -1e30
CW = 512

F32 = mybir.dt.float32
F32R = mybir.dt.float32r
I32 = mybir.dt.int32
ALU = mybir.AluOpType
ACT = mybir.ActivationFunctionType
AX = mybir.AxisListType

QA, KA, VA = 0, WA, 2 * WA
QB, KB, VB = 3 * WA, 3 * WA + WB, 3 * WA + 2 * WB
QC, KC, VC = 3 * (WA + WB), 3 * (WA + WB) + WC, 3 * (WA + WB) + 2 * WC
QK_TILES = ([c for c in range(QA, VA, P)] + [c for c in range(QB, VB, P)] + [c for c in range(QC, VC, P)])
MERGED_TILES = ([QA + c for c in range(0, WA, P)] + [QB + c for c in range(0, WB, P)]
                + [QC + c for c in range(0, WC, P)])

NR = 6
NH = 3
UNIT = 2048
IN_CHUNKS = QKV // CW
U_IN = 2 * IN_CHUNKS
U_OUT = D // 256
FFN_W = [CW] * (F_DENSE // CW) + [F_DENSE % CW]
U_FFN_COL = [2] * (F_DENSE // CW) + [1]
U_FFN = 2 * sum(U_FFN_COL) + F_DENSE // 256
BASE_IN = [0, U_IN + U_OUT + U_FFN]
BASE_OUT = [b + U_IN for b in BASE_IN]
BASE_FFN = BASE_OUT[0] + U_OUT
BASE_MOE = BASE_OUT[1] + U_OUT
MOE_W = [CW] * (F_EXP // CW)
MOE_COL = [2] * len(MOE_W)
U_MOE = 2 * sum(MOE_COL) + F_EXP // 256
assert U_MOE % NR == 0 and U_MOE % NH == 0 and F_DENSE % CW == 256

TABLE = {}
_at = 0
for _name, _w in (("ident", P), ("iota", P), ("before", P), ("ones", P), ("lower", NE * NE),
                  ("bias_b", NT * SEQ), ("mask_c", GRID_W), ("cos_a", NT * 8), ("sin_a", NT * 4),
                  ("cos_b", NT * 16), ("sin_b", NT * 8), ("minus_half", NT)):
    TABLE[_name] = (_at, _w)
    _at += _w
TABLE_W = _at


def shape_table():
    t = np.zeros((P, TABLE_W), np.float32)

    def put(name, a):
        o, w = TABLE[name]
        t[:, o:o + w] = np.asarray(a, np.float32).reshape(P, w)

    p = np.arange(P)
    put("ident", np.eye(P))
    put("iota", np.tile(p, (P, 1)))
    put("before", p[:, None] < p[None, :])
    put("ones", np.ones((P, P)))
    e = np.arange(NE)
    put("lower", np.tile((e[None, :] < e[:, None]).reshape(1, -1), (P, 1)))
    q = np.arange(SEQ)
    d = np.abs(q[:, None] - q[None, :])
    count = np.zeros((SEQ, SEQ))
    for window, dil in ((128, 1), (512, 4), (2048, 16)):
        count += (d % dil == 0) & (d // dil <= window // (2 * dil))
    bias = np.where(count > 0, np.log(np.maximum(count, 1)), NEG)
    put("bias_b", bias.reshape(NT, P, SEQ).transpose(1, 0, 2))
    c = np.arange(GRID_W)
    start = np.clip(c - NA_COLS // 2, 0, GRID_W - NA_COLS)
    ok = (c[None, :] >= start[:, None]) & (c[None, :] < start[:, None] + NA_COLS)
    put("mask_c", np.tile(np.where(ok, 0.0, NEG), (P // GRID_W, 1)))
    for name, rot in (("a", DIFF // 4), ("b", HD // 4)):
        inv = (np.float32(500000.0) ** (-np.arange(0, rot, 2, dtype=np.float32) / np.float32(rot))).astype(np.float32)
        ang = (np.arange(SEQ, dtype=np.float32)[:, None] * inv[None, :]).astype(np.float32)
        cos = np.cos(ang.astype(np.float64)).reshape(NT, P, rot // 2).transpose(1, 0, 2)
        sin = np.sin(ang.astype(np.float64)).reshape(NT, P, rot // 2).transpose(1, 0, 2)
        put("cos_" + name, np.concatenate([cos, cos], axis=-1))
        put("sin_" + name, sin)
    put("minus_half", np.full((P, NT), -0.5))
    return t


def encoder(nc, x, w_in, w_out, beta_mix, diff_lambda, diff_norm_g, na_rpb, ln1_g, ln1_b, ln2_g, ln2_b,
            ffn_w_gate, ffn_w_up, ffn_w_down, moe_w_router, moe_w_gate, moe_w_up, moe_w_down, table, out):
    ctx = ExitStack()
    with ctx:
        def sb(name, shape, dt=F32, scope=None):
            return (scope or ctx).enter_context(nc.sbuf_tensor(name, shape, dt))

        def sem(name):
            return ctx.enter_context(nc.semaphore(name))

        raw = sb("raw", [P, NR, UNIT])
        w_hi = sb("w_hi", [P, NH, UNIT], F32R)
        w_lo = sb("w_lo", [P, NH, UNIT], F32R)
        xtok = sb("xtok", [P, NT, D])
        xT_hi = sb("xT_hi", [P, KT, SEQ], F32R)
        xT_lo = sb("xT_lo", [P, KT, SEQ], F32R)
        rows = sb("rows", [P, 3, D])
        tab = sb("tab", [P, TABLE_W])
        gain_a = sb("gain_a", [P, DEPTH, HD])
        lam_in = sb("lam_in", [P, DEPTH, 4, DIFF])
        router = sb("router", [P, KT, NE])
        router_hi = sb("router_hi", [P, KT, NE], F32R)
        router_lo = sb("router_lo", [P, KT, NE], F32R)
        stats = sb("stats", [P, NT, 12])
        mean_var = sb("mean_var", [P, NT, 2])
        var_eps = sb("var_eps", [P, NT])
        rstd = sb("rstd", [P, NT])
        lam_prod = sb("lam_prod", [P, 2, DIFF])
        lam_sum = sb("lam_sum", [P, 2])
        lam_exp = sb("lam_exp", [P, 2])
        lam_neg = sb("lam_neg", [P, 1])
        with ExitStack() as s:
            proj = sb("proj", [P, NT, QKV], scope=s)
            qkT = sb("qkT", [P, len(QK_TILES), SEQ], scope=s)
            bias_c = sb("bias_c", [P, HC, 6, GRID_W], scope=s)
            score = sb("score", [P, 2, 2, SEQ], scope=s)
            prob = sb("prob", [P, 2, 2, SEQ], scope=s)
            prob_d = sb("prob_d", [P, 2, SEQ], scope=s)
            probT = sb("probT", [P, 2, 4, P], scope=s)
            rope_cos = score[:].rearrange("p a b (g w) -> p a b g w", w=16)
            rope_sin = prob[:].rearrange("p a b (g w) -> p a b g w", w=16)
            rpb_pad = qkT[0:7, 0:DEPTH * HC * P // SEQ, :].rearrange("p (l a) c -> p l (a c)", l=DEPTH)
            rpb_pad = rpb_pad.rearrange("p l (h c) -> p l h c", c=P)
            shifted = qkT[:, 6:15, :].rearrange("p a (b c) -> p (a b) c", c=GRID_W)
            rpb_rows = sb("rpb_rows", [7, DEPTH, HC, 2 * NA_COLS - 1], scope=s)
            neg_max = sb("neg_max", [P, 4, 2], scope=s)
            sums = sb("sums", [P, NT, 20], scope=s)
            rsum = sb("rsum", [P, NT, 20], scope=s)
            oa = sb("oa", [P, HA, HD], scope=s)
            oa_sq = sb("oa_sq", [P, HA, HD], scope=s)
            ms_a = sb("ms_a", [P, HA], scope=s)
            rms_a = sb("rms_a", [P, HA], scope=s)
            half_a = sb("half_a", [P, HA], scope=s)
        with ExitStack() as s:
            hT_hi = sb("hT_hi", [P, F_DENSE // P, SEQ], F32R, scope=s)
            hT_lo = sb("hT_lo", [P, F_DENSE // P, SEQ], F32R, scope=s)
            silu = sb("silu", [P, NT, CW], scope=s)
            hid = sb("hid", [P, NT, CW], scope=s)
        with ExitStack() as s:
            xk_hi = sb("xk_hi", [P, NT, D], F32R, scope=s)
            xk_lo = sb("xk_lo", [P, NT, D], F32R, scope=s)
            mT_hi = sb("mT_hi", [P, F_EXP // P, P], F32R, scope=s)
            mT_lo = sb("mT_lo", [P, F_EXP // P, P], F32R, scope=s)
            m_silu = sb("m_silu", [P, 1, CW], scope=s)
            m_hid = sb("m_hid", [P, 1, CW], scope=s)
            sel = sb("sel", [P, NT, P], F32R, scope=s)
            selT = sb("selT", [P, NT, P], F32R, scope=s)
            logit = sb("logit", [P, NT, NE], scope=s)
            rank3 = sb("rank3", [P, NT, NE, NE], scope=s)
            tie3 = sb("tie3", [P, NT, NE, NE], scope=s)
            rank = sb("rank", [P, NT, NE], scope=s)
            first = sb("first", [P, NT, NE], scope=s)
            second = sb("second", [P, NT, NE], scope=s)
            chosen = sb("chosen", [P, NT, NE], scope=s)
            pick = sb("pick", [P, NT, NE], scope=s)
            top = sb("top", [P, 2, NT], scope=s)
            e_diff = sb("e_diff", [P, NT], scope=s)
            gate = sb("gate", [P, 3, NT], scope=s)
            comb = sb("comb", [P, NT, 2 * NE], scope=s)
            key = sb("key", [P, NT, 2 * NE], scope=s)
            most = sb("most", [P, 2], scope=s)
            rounds = sb("rounds", [P, 1], I32, scope=s)
        bank = ctx.enter_context(nc.psum_tensor("bank", [P, 8, CW], F32))
        rpb_dram = nc.dram_tensor("rpb_scratch", [DEPTH, 2, HC, 6, P], F32)

        def const(name, *shape):
            o, w = TABLE[name]
            v = tab[:, o:o + w]
            if len(shape) == 2:
                v = v.rearrange("p (a b) -> p a b", b=shape[1])
            return v

        ident = const("ident")

        x_in = sem("x_in")
        consts_in = sem("consts_in")
        small_in = sem("small_in")
        raw_in = [sem(f"raw_in{i}") for i in range(NR)]
        hi_done = sem("hi_done")
        lo_done = sem("lo_done")
        unit_used = sem("unit_used")
        t_psum = sem("t_psum")
        t_hi = sem("t_hi")
        t_lo = sem("t_lo")
        proj_in = sem("proj_in")
        roped = sem("roped")
        qk_psum = sem("qk_psum")
        qk_in = [sem("qk_in_act"), sem("qk_in_dve")]
        s_psum = sem("s_psum")
        max_done = sem("max_done")
        exp_done = sem("exp_done")
        diff_done = sem("diff_done")
        p_psum = sem("p_psum")
        p_in = sem("p_in")
        pv_done = sem("pv_done")
        ms_ready = sem("ms_ready")
        rms_ready = sem("rms_ready")
        merged = sem("merged")
        lam_summed = sem("lam_summed")
        lam_exped = sem("lam_exped")
        beta_in = sem("beta_in")
        gb_in = sem("gb_in")
        pad_zero = sem("pad_zero")
        pad_in = sem("pad_in")
        scratch_in = sem("scratch_in")
        toeplitz_in = sem("toeplitz_in")
        bias_ready = sem("bias_ready")
        var_ready = sem("var_ready")
        rstd_ready = sem("rstd_ready")
        ln_done = sem("ln_done")
        silu_done = sem("silu_done")
        hid_done = sem("hid_done")
        h_psum = sem("h_psum")
        h_hi = sem("h_hi")
        h_lo = sem("h_lo")
        xk_split = sem("xk_split")
        tok_ready = sem("tok_ready")
        wr_split = sem("wr_split")
        logit_psum = sem("logit_psum")
        chosen_ready = sem("chosen_ready")
        diff_ready = sem("diff_ready")
        diff_exped = sem("diff_exped")
        pos_psum = sem("pos_psum")
        routed = sem("routed")
        sel_ready = sem("sel_ready")
        gather_psum = sem("gather_psum")
        g_hi = sem("g_hi")
        g_lo = sem("g_lo")
        selT_psum = sem("selT_psum")
        selT_in = sem("selT_in")
        y_hi = sem("y_hi")
        y_lo = sem("y_lo")
        scatter_psum = sem("scatter_psum")
        added = sem("added")
        dve_step = sem("dve_step")
        out_done = sem("out_done")

        xg_hi, xg_lo = xT_hi[:, :, 0:P], xT_lo[:, :, 0:P]
        yo_hi, yo_lo = xT_hi[:, :, P:SEQ], xT_lo[:, :, P:SEQ]

        def ffn_units(w_col):
            return [(c, kind, part, n) for c, n in enumerate(w_col) for kind in ("gate", "up") for part in range(n)]

        block = ctx.enter_context(nc.Block())

        @block.sync
        def _(sp):
            for tt in range(NT):
                sp.dma_start(xtok[:, tt, :], x[0, tt * P:(tt + 1) * P, :]).then_inc(x_in, 16)

            def load(n, src, off=0, use=0):
                if n >= NR:
                    sp.wait_ge(lo_done, n - NR + 1 + off)
                k = src.shape[1]
                sp.dma_start(raw[:, n % NR, :].rearrange("p (k n) -> p k n", k=k), src).then_inc(raw_in[n % NR], 16)

            def columns(w, c, part, parts, width):
                k = D // parts
                return w[part * k:(part + 1) * k, c * CW:c * CW + width].rearrange("(k p) n -> p k n", p=P)

            def row_pair(w, i):
                return w[i * 256:(i + 1) * 256, :].rearrange("(k p) n -> p k n", p=P)

            for l in range(DEPTH):
                for u in range(U_IN):
                    load(BASE_IN[l] + u, columns(w_in[l], u // 2, u % 2, 2, CW))
                for u in range(U_OUT):
                    load(BASE_OUT[l] + u, row_pair(w_out[l], u))
                if l == 0:
                    cols = ffn_units(U_FFN_COL)
                    for u, (c, kind, part, parts) in enumerate(cols):
                        w = ffn_w_gate if kind == "gate" else ffn_w_up
                        load(BASE_FFN + u, columns(w[0], c, part, parts, FFN_W[c]))
                    for i in range(F_DENSE // 256):
                        load(BASE_FFN + len(cols) + i, row_pair(ffn_w_down[0], i))

            def sweep(first_round):
                with sp.Fori(0, NE) as e:
                    off = (e + first_round * NE) * U_MOE
                    cols = ffn_units(MOE_COL)
                    for u, (c, kind, part, parts) in enumerate(cols):
                        w = moe_w_gate if kind == "gate" else moe_w_up
                        k = D // parts
                        src = w[0, bass.ds(e, 1), part * k:(part + 1) * k, c * CW:(c + 1) * CW]
                        load(BASE_MOE + u, src.rearrange("o (k p) n -> p (o k) n", p=P), off)
                    for i in range(F_EXP // 256):
                        src = moe_w_down[0, bass.ds(e, 1), i * 256:(i + 1) * 256, :]
                        load(BASE_MOE + len(cols) + i, src.rearrange("o (k p) n -> p (o k) n", p=P), off)

            sweep(0)
            sp.wait_ge(routed, 1)
            n_rounds = sp.value_load(rounds[0:1, 0:1], min_val=NE, max_val=2 * NE)
            with sp.If(n_rounds > NE):
                sweep(1)
            for tt in range(NT):
                sp.wait_ge(ln_done, 2 * NT * DEPTH - NT + tt + 1)
                sp.dma_start(out[0, tt * P:(tt + 1) * P, :], xtok[:, tt, :]).then_inc(out_done, 16)
            sp.wait_ge(out_done, 16 * NT)

        @block.gpsimd
        def _(pool):
            pool.dma_start(gain_a[:], diff_norm_g.unsqueeze(0).broadcast_to([P, DEPTH, HD])).then_inc(small_in, 16)
            pool.dma_start(lam_in[:], diff_lambda.unsqueeze(0).broadcast_to([P, DEPTH, 4, DIFF])).then_inc(small_in, 16)
            pool.dma_start(router[:], moe_w_router[0].rearrange("(k p) e -> p k e", p=P)).then_inc(small_in, 16)
            nc.gpsimd.memset(half_a[:], -0.5).then_inc(pad_zero, 1)
            nc.gpsimd.memset(qkT[0:7, 0:DEPTH * HC * P // SEQ, :], 0.0).then_inc(pad_zero, 1)
            pool.wait_ge(pad_zero, 2)
            for l in range(DEPTH):
                pool.dma_start(rpb_rows[:, l], na_rpb[l].rearrange("h r c -> r h c")[
                    NA_ROWS - ROWS:NA_ROWS + ROWS - 1]).then_inc(pad_in, 16)
            pool.wait_ge(pad_in, 16 * DEPTH)
            n = 2 * NA_COLS - 1
            lo_col = GRID_W - NA_COLS
            for l in range(DEPTH):
                nc.gpsimd.tensor_copy(rpb_pad[:, l, :, lo_col:lo_col + n], rpb_rows[:, l, :, ::-1]).then_inc(pad_zero, 1)
            pool.wait_ge(pad_zero, 2 + DEPTH)
            for l in range(DEPTH):
                for rl in range(2):
                    pool.dma_start(rpb_dram[l, rl].rearrange("h j c -> j h c"),
                                   rpb_pad[1 - rl:7 - rl, l]).then_inc(scratch_in, 16)
            pool.wait_ge(scratch_in, 16 * 2 * DEPTH)
            pool.wait_ge(consts_in, 16)
            mask = const("mask_c").unsqueeze(1).broadcast_to([P, HC * 6, GRID_W])

            def toeplitz(l):
                for rl in range(2):
                    src = bass.AP(tensor=rpb_dram, offset=(l * 2 + rl) * HC * 6 * P,
                                  ap=[[1, GRID_W], [P, HC * 6], [1, GRID_W]])
                    pool.dma_start(shifted[rl * GRID_W:(rl + 1) * GRID_W], src).then_inc(toeplitz_in, 16)
                pool.wait_ge(toeplitz_in, 32 * (l + 1))
                nc.gpsimd.tensor_tensor(bias_c[:].rearrange("p h j c -> p (h j) c"), shifted[:, :, ::-1], mask,
                                        ALU.add).then_inc(bias_ready, 1)

            def inverse_roots(ln):
                for tt in range(NT):
                    n = ln * NT + tt + 1
                    pool.wait_ge(var_ready, n)
                    nc.gpsimd.tensor_tensor(rstd[:, tt:tt + 1], var_eps[:, tt:tt + 1],
                                            const("minus_half")[:, 0:1], ALU.pow).then_inc(rstd_ready, 1)

            for l in range(DEPTH):
                pool.dma_start(rows[:, 0, :], beta_mix[l:l + 1, :].broadcast_to([P, D])).then_inc(beta_in, 16)
                for g, b, ln in ((ln1_g, ln1_b, 2 * l), (ln2_g, ln2_b, 2 * l + 1)):
                    if ln:
                        pool.wait_ge(ln_done, NT * ln)
                    pool.dma_start(rows[:, 1, :], g[l:l + 1, :].broadcast_to([P, D])).then_inc(gb_in, 16)
                    pool.dma_start(rows[:, 2, :], b[l:l + 1, :].broadcast_to([P, D])).then_inc(gb_in, 16)
                    if ln == 2 * l:
                        toeplitz(l)
                        for qt in range(NT):
                            pool.wait_ge(ms_ready, NT * l + qt + 1)
                            nc.gpsimd.tensor_tensor(rms_a[:], ms_a[:], half_a[:], ALU.pow).then_inc(rms_ready, 1)
                    inverse_roots(ln)

        GROUPS = ([("a", (h, h)) for h in range(HA)] + [("b", (h, h + 1)) for h in range(0, HB, 2)]
                  + [("c", (h, h + 1)) for h in range(0, HC, 2)])
        NG = len(GROUPS)
        NGL = NT * NG

        @block.scalar
        def _(act):
            act.dma_start(tab[:], table).then_inc(consts_in, 16)

            def split_hi(n, off=0, use=0):
                act.wait_ge(raw_in[n % NR], 16 * (n // NR + 1) + use)
                if n >= NH:
                    act.wait_ge(unit_used, n - NH + 1 + off)
                nc.scalar.activation(w_hi[:, n % NH, :], raw[:, n % NR, :], ACT.Copy).then_inc(hi_done, 1)

            def transposed(rnd):
                for g in range(4):
                    tt, half = g // 2, g % 2
                    act.wait_ge(t_psum, 4 * rnd + g + 1)
                    nc.scalar.activation(xT_hi[:, 4 * half:4 * half + 4, tt * P:(tt + 1) * P],
                                         bank[:, g, :].rearrange("p (k t) -> p k t", t=P), ACT.Copy).then_inc(t_hi, 1)

            def lambda_exp(l):
                act.wait_ge(lam_summed, l + 1)
                nc.scalar.activation(lam_exp[:], lam_sum[:], ACT.Exp).then_inc(lam_exped, 1)

            def exps(l, a):
                qt, (kind, heads) = a // NG, GROUPS[a % NG]
                ga = l * NGL + a
                act.wait_ge(max_done, ga + 1)
                if ga >= 2:
                    act.wait_ge(p_psum, ga - 1)
                for i in range(2):
                    slot = 2 * (a % NG) + i
                    src = bank[:, 2 * (ga % 2) + i, 0:SEQ] if kind == "a" else score[:, ga % 2, i, :]
                    ins = nc.scalar.activation(prob[:, ga % 2, i, :], src, ACT.Exp,
                                               bias=neg_max[:, ga % 4, i:i + 1],
                                               scale=DIFF ** -0.5 if kind == "a" else 1.0,
                                               accum_out=sums[:, qt, slot:slot + 1])
                ins.then_inc(exp_done, 1)

            def prob_copy(l, a):
                kind = GROUPS[a % NG][0]
                ga = l * NGL + a
                n = 2 if kind == "a" else 4
                act.wait_ge(p_psum, ga + 1)
                if ga >= 2:
                    act.wait_ge(pv_done, ga - 1)
                nc.scalar.activation(probT[:, ga % 2, 0:n, :],
                                     bank[:, 4 + ga % 2, 0:n * P].rearrange("p (n q) -> p n q", q=P),
                                     ACT.Copy).then_inc(p_in, 1)

            def hidden_hi(c, w, cb, hT, tts, off=0):
                act.wait_ge(h_psum, cb + c + 1 + off)
                for tt in tts:
                    n = w[c] // P
                    b = 4 + tt if len(tts) > 1 else 4 + c % 2
                    ins = nc.scalar.activation(hT[:, 4 * c:4 * c + n, tt * P:(tt + 1) * P],
                                               bank[:, b, 0:w[c]].rearrange("p (k t) -> p k t", t=P), ACT.Copy)
                ins.then_inc(h_hi, 1)

            def gate_up(ub, w, w_col, cb, hT, sl, tts, split, off=0):
                for u, (c, kind, part, parts) in enumerate(ffn_units(w_col)):
                    n = ub + u
                    split(n + NH)
                    if kind == "gate" and part == parts - 1:
                        act.wait_ge(unit_used, n + 1 + off)
                        if cb + c > 0:
                            act.wait_ge(hid_done, cb + c + off_chunks(off))
                        for tt in tts:
                            ins = nc.scalar.activation(sl[:, tt, 0:w[c]], bank[:, tt, 0:w[c]], ACT.Silu)
                        ins.then_inc(silu_done, 1)
                        if c > 0:
                            hidden_hi(c - 1, w, cb, hT, tts, off_chunks(off))
                return ub + len(ffn_units(w_col))

            def off_chunks(off):
                return loop_chunks[0] if loop_chunks else 0

            loop_chunks = []

            def static_split(n):
                if n < BASE_MOE:
                    split_hi(n)

            for l in range(DEPTH):
                transposed(3 * l)
                if l == 0:
                    for n in range(NH):
                        split_hi(n)
                    act.wait_ge(small_in, 48)
                for j in range(IN_CHUNKS):
                    for half in range(2):
                        n = BASE_IN[l] + 2 * j + half
                        static_split(n + NH)
                        act.wait_ge(unit_used, n + 1)
                    for tt in range(NT):
                        nc.scalar.activation(proj[:, tt, j * CW:(j + 1) * CW], bank[:, 4 + (j % 2) * 2 + tt, :],
                                             ACT.Copy).then_inc(proj_in, 1)
                lambda_exp(l)
                act.wait_ge(bias_ready, l + 1)
                for g in range(4):
                    act.wait_ge(qk_psum, l * 8 + 2 * g + 1)
                    nc.scalar.activation(qkT[:, 4 * g:4 * g + 4, 0:P],
                                         bank[:, (2 * g) % 4, :].rearrange("p (k t) -> p k t", t=P),
                                         ACT.Copy).then_inc(qk_in[0], 1)
                for a in range(NGL + 1):
                    if a < NGL:
                        exps(l, a)
                    if a >= 1:
                        prob_copy(l, a - 1)
                transposed(3 * l + 1)
                for i in range(U_OUT):
                    static_split(BASE_OUT[l] + i + NH)
                transposed_round = 3 * l + 2
                transposed(transposed_round)
                if l == 0:
                    n = gate_up(BASE_FFN, FFN_W, U_FFN_COL, 0, hT_hi, silu, range(NT), static_split)
                    hidden_hi(len(FFN_W) - 1, FFN_W, 0, hT_hi, range(NT))
                    for i in range(F_DENSE // 256):
                        static_split(n + i + NH)

            for tt in range(NT):
                ins = nc.scalar.activation(xk_hi[:, tt, :], xtok[:, tt, :], ACT.Copy)
            ins.then_inc(xk_split, 1)
            act.wait_ge(diff_ready, 1)
            nc.scalar.activation(e_diff[:], top[:, 1, :], ACT.Exp).then_inc(diff_exped, 1)
            act.wait_ge(routed, 1)
            n_rounds = act.value_load(rounds[0:1, 0:1], min_val=NE, max_val=2 * NE)
            with act.Fori(0, n_rounds) as it:
                off = it * U_MOE
                loop_chunks.append(it * len(MOE_W))
                use = it * (16 * U_MOE // NR)
                for q in range(2):
                    act.wait_ge(gather_psum, it * 4 + (2 * q + 1))
                    nc.scalar.activation(xg_hi[:, 4 * q:4 * q + 4, :],
                                         bank[:, 6, :].rearrange("p (k t) -> p k t", t=P), ACT.Copy).then_inc(g_hi, 1)

                def loop_split(n):
                    if n < BASE_MOE + U_MOE:
                        split_hi(n, off, use)

                for n in range(NH):
                    split_hi(BASE_MOE + n, off, use)
                n = gate_up(BASE_MOE, MOE_W, MOE_COL, len(FFN_W), mT_hi, m_silu, [0], loop_split, off)
                hidden_hi(len(MOE_W) - 1, MOE_W, len(FFN_W), mT_hi, [0], loop_chunks[0])
                for i in range(F_EXP // 256):
                    loop_split(n + i + NH)
                act.wait_ge(unit_used, BASE_MOE + U_MOE + off)
                nc.scalar.activation(yo_hi, bank[:, 2:4, :].rearrange("p b (k t) -> p (b k) t", t=P),
                                     ACT.Copy).then_inc(y_hi, 1)

        @block.vector
        def _(dve):
            steps = [0]

            def link(ins):
                steps[0] += 1
                ins.then_inc(dve_step, 1)
                dve.wait_ge(dve_step, steps[0])

            def split_lo(n, off=0):
                dve.wait_ge(hi_done, n + 1 + off)
                nc.vector.tensor_tensor(w_lo[:, n % NH, :], raw[:, n % NR, :], w_hi[:, n % NH, :].bitcast(F32),
                                        ALU.subtract).then_inc(lo_done, 1)

            def transposed(rnd):
                for g in range(4):
                    tt, half = g // 2, g % 2
                    dve.wait_ge(t_hi, 4 * rnd + g + 1)
                    at = (slice(None), slice(4 * half, 4 * half + 4), slice(tt * P, (tt + 1) * P))
                    nc.vector.tensor_tensor(xT_lo[at], bank[:, g, :].rearrange("p (k t) -> p k t", t=P),
                                            xT_hi[at].bitcast(F32), ALU.subtract).then_inc(t_lo, 1)

            def rotary(c0, width, half, groups, name, chunk_count):
                dve.wait_ge(proj_in, chunk_count)
                cos = const("cos_" + name, NT, 2 * half).unsqueeze(2).broadcast_to([P, NT, groups, 2 * half])
                sin = const("sin_" + name, NT, half).unsqueeze(2).broadcast_to([P, NT, groups, half])
                v = proj[:, :, c0:c0 + groups * width].rearrange("p t (g w) -> p t g w", w=width)
                for tt in range(NT):
                    vt = v[:, tt]
                    rc = rope_cos[:, tt, 0, 0:groups, 0:2 * half]
                    rs = rope_sin[:, tt, 0, 0:groups, 0:2 * half]
                    nc.vector.tensor_tensor(rc, vt[:, :, 0:2 * half], cos[:, tt], ALU.mult)
                    nc.vector.tensor_tensor(rs[:, :, 0:half], vt[:, :, half:2 * half], sin[:, tt], ALU.mult)
                    link(nc.vector.tensor_tensor(rs[:, :, half:2 * half], vt[:, :, 0:half], sin[:, tt], ALU.mult))
                    nc.vector.tensor_tensor(vt[:, :, 0:half], rc[:, :, 0:half], rs[:, :, 0:half], ALU.subtract)
                    ins = nc.vector.tensor_tensor(vt[:, :, half:2 * half], rc[:, :, half:2 * half],
                                                  rs[:, :, half:2 * half], ALU.add)
                ins.then_inc(roped, 1)

            def lambda_terms(l):
                lam_init = 0.8 - 0.6 * math.exp(-0.3 * l)
                link(nc.vector.tensor_tensor(lam_prod[:], lam_in[:, l, 0:4:2, :], lam_in[:, l, 1:4:2, :], ALU.mult))
                nc.vector.tensor_reduce(lam_sum[:], lam_prod[:], AX.X, ALU.add).then_inc(lam_summed, 1)
                link(nc.vector.tensor_scalar(gain_a[:, l, :], gain_a[:, l, :], 1.0 - lam_init, None, ALU.mult))

            def lambda_value(l):
                lam_init = 0.8 - 0.6 * math.exp(-0.3 * l)
                dve.wait_ge(lam_exped, l + 1)
                link(nc.vector.tensor_tensor(lam_neg[:], lam_exp[:, 1:2], lam_exp[:, 0:1], ALU.subtract))
                link(nc.vector.tensor_scalar(lam_neg[:], lam_neg[:], -lam_init, None, ALU.add))

            def row_max(l, a):
                qt, (kind, heads) = a // NG, GROUPS[a % NG]
                ga = l * NGL + a
                dve.wait_ge(s_psum, ga + 1)
                s2 = bank[:, 2 * (ga % 2):2 * (ga % 2) + 2, 0:SEQ]
                nm = neg_max[:, ga % 4, :]
                if kind == "a":
                    link(nc.vector.tensor_reduce(nm, s2, AX.X, ALU.max, negate=True))
                    nc.vector.tensor_scalar(nm, nm, DIFF ** -0.5, None, ALU.mult).then_inc(max_done, 1)
                    return
                if kind == "b":
                    bias = const("bias_b", NT, SEQ)[:, qt:qt + 1, :].broadcast_to([P, 2, SEQ])
                else:
                    j0 = 2 if qt == 0 else 0
                    bias = bias_c[:, heads[0]:heads[0] + 2, j0:j0 + 4, :].rearrange("p h j c -> p h (j c)")
                sc = score[:, ga % 2]
                if ga >= 2:
                    dve.wait_ge(exp_done, ga - 1)
                link(nc.vector.scalar_tensor_tensor(sc, s2, HD ** -0.5, bias, ALU.mult, ALU.add))
                nc.vector.tensor_reduce(nm, sc, AX.X, ALU.max, negate=True).then_inc(max_done, 1)

            def differential(l, a):
                qt = a // NG
                ga = l * NGL + a
                s0 = 2 * (a % NG)
                dve.wait_ge(exp_done, ga + 1)
                link(nc.vector.reciprocal(rsum[:, qt, s0:s0 + 2], sums[:, qt, s0:s0 + 2]))
                link(nc.vector.tensor_tensor(rsum[:, qt, s0 + 1:s0 + 2], rsum[:, qt, s0 + 1:s0 + 2], lam_neg[:], ALU.mult))
                p0, p1 = prob[:, ga % 2, 0, :], prob[:, ga % 2, 1, :]
                link(nc.vector.tensor_scalar(p1, p1, rsum[:, qt, s0 + 1:s0 + 2], None, ALU.mult))
                if ga >= 2:
                    dve.wait_ge(p_psum, ga - 1)
                nc.vector.scalar_tensor_tensor(prob_d[:, ga % 2, :], p0, rsum[:, qt, s0:s0 + 1], p1,
                                               ALU.mult, ALU.add).then_inc(diff_done, 1)

            def merge(l, qt):
                dve.wait_ge(pv_done, l * NGL + (qt + 1) * NG)
                o = bank[:, 6:8, :].rearrange("p b (h d) -> p (b h) d", d=HD)
                link(nc.vector.tensor_copy(oa[:], o[:, 0:HA, :]))
                link(nc.vector.tensor_tensor(oa_sq[:], oa[:], oa[:], ALU.mult))
                link(nc.vector.tensor_reduce(ms_a[:], oa_sq[:], AX.X, ALU.add))
                nc.vector.tensor_scalar(ms_a[:], ms_a[:], 1.0 / HD, EPS, ALU.mult, ALU.add).then_inc(ms_ready, 1)
                link(nc.vector.reciprocal(rsum[:, qt, 8:20], sums[:, qt, 8:20]))
                for h0, n, c0, s0 in ((HA, HB, QB, 8), (HA + HB, HC, QC, 14)):
                    m = proj[:, qt, c0:c0 + n * HD].rearrange("p (h d) -> p h d", d=HD)
                    r = rsum[:, qt, s0:s0 + n].unsqueeze(2).broadcast_to([P, n, HD])
                    link(nc.vector.tensor_tensor(m, o[:, h0:h0 + n, :], r, ALU.mult))
                m = proj[:, qt, QA:QA + WA].rearrange("p (h d) -> p h d", d=HD)
                dve.wait_ge(rms_ready, NT * l + qt + 1)
                link(nc.vector.tensor_tensor(oa[:], oa[:], rms_a[:].unsqueeze(2).broadcast_to([P, HA, HD]), ALU.mult))
                link(nc.vector.tensor_tensor(m, oa[:], gain_a[:, l:l + 1, :].broadcast_to([P, HA, HD]), ALU.mult))
                dve.wait_ge(beta_in, 16 * (l + 1))
                b0 = 0
                for c0, w in ((QA, WA), (QB, WB), (QC, WC)):
                    m = proj[:, qt, c0:c0 + w]
                    ins = nc.vector.tensor_tensor(m, m, rows[:, 0, b0:b0 + w], ALU.mult)
                    b0 += w
                ins.then_inc(merged, 1)

            def layer_norm(ln, banks, unit):
                if banks is not None:
                    dve.wait_ge(unit_used, unit)
                for tt in range(NT):
                    v = xtok[:, tt, :]
                    if banks is not None:
                        sub = bank[:, banks[tt]:banks[tt] + 2, :].rearrange("p b n -> p (b n)")
                        link(nc.vector.scalar_tensor_tensor(v, v, ALPHA, sub, ALU.mult, ALU.add))
                    for h in range(2):
                        ins = nc.vector.bn_stats(stats[:, tt, 6 * h:6 * h + 6], xtok[:, tt, h * CW:(h + 1) * CW])
                    link(ins)
                    link(nc.vector.bn_aggr(mean_var[:, tt, :], stats[:, tt, :]))
                    nc.vector.tensor_scalar(var_eps[:, tt:tt + 1], mean_var[:, tt, 1:2], EPS, None,
                                            ALU.add).then_inc(var_ready, 1)
                dve.wait_ge(gb_in, 32 * (ln + 1))
                for tt in range(NT):
                    v = xtok[:, tt, :]
                    dve.wait_ge(rstd_ready, ln * NT + tt + 1)
                    link(nc.vector.tensor_scalar(v, v, mean_var[:, tt, 0:1], rstd[:, tt:tt + 1], ALU.subtract, ALU.mult))
                    link(nc.vector.tensor_tensor(v, v, rows[:, 1, :], ALU.mult))
                    nc.vector.tensor_tensor(v, v, rows[:, 2, :], ALU.add).then_inc(ln_done, 1)

            def hidden_lo(c, w, cb, hT, hTl, tts, off=0):
                dve.wait_ge(h_hi, cb + c + 1 + off)
                for tt in tts:
                    n = w[c] // P
                    b = 4 + tt if len(tts) > 1 else 4 + c % 2
                    at = (slice(None), slice(4 * c, 4 * c + n), slice(tt * P, (tt + 1) * P))
                    ins = nc.vector.tensor_tensor(hTl[at], bank[:, b, 0:w[c]].rearrange("p (k t) -> p k t", t=P),
                                                  hT[at].bitcast(F32), ALU.subtract)
                ins.then_inc(h_lo, 1)

            def gate_up(ub, w, w_col, cb, hT, hTl, sl, hd, tts, split, off=0, off_c=0):
                for u, (c, kind, part, parts) in enumerate(ffn_units(w_col)):
                    n = ub + u
                    split(n + NH)
                    if part < parts - 1:
                        continue
                    if kind == "gate" and c > 0:
                        hidden_lo(c - 1, w, cb, hT, hTl, tts, off_c)
                    if kind == "up":
                        dve.wait_ge(unit_used, n + 1 + off)
                        dve.wait_ge(silu_done, cb + c + 1 + off_c)
                        if cb + c > 0:
                            dve.wait_ge(h_psum, cb + c + off_c)
                        for tt in tts:
                            ins = nc.vector.tensor_tensor(hd[:, tt, 0:w[c]], sl[:, tt, 0:w[c]],
                                                          bank[:, len(tts) + tt, 0:w[c]], ALU.mult)
                        ins.then_inc(hid_done, 1)
                return ub + len(ffn_units(w_col))

            def static_split(n):
                if n < BASE_MOE:
                    split_lo(n)

            dve.wait_ge(consts_in, 16)
            for l in range(DEPTH):
                transposed(3 * l)
                if l == 0:
                    for n in range(NH):
                        split_lo(n)
                    dve.wait_ge(small_in, 48)
                    nc.vector.tensor_copy(router_hi[:], router[:]).then_inc(wr_split, 1)
                    dve.wait_ge(wr_split, 1)
                    nc.vector.tensor_tensor(router_lo[:], router[:], router_hi[:].bitcast(F32),
                                            ALU.subtract).then_inc(wr_split, 1)
                lambda_terms(l)
                for j in range(IN_CHUNKS):
                    for half in range(2):
                        static_split(BASE_IN[l] + 2 * j + half + NH)
                    if j == 1:
                        rotary(QA, DIFF, DIFF // 8, 2 * WA // DIFF, "a", (l * IN_CHUNKS + 1) * NT)
                    if j == 3:
                        rotary(QB, HD, HD // 8, 2 * HB, "b", (l * IN_CHUNKS + 3) * NT)
                dve.wait_ge(bias_ready, l + 1)
                for g in range(4):
                    dve.wait_ge(qk_psum, l * 8 + 2 * g + 2)
                    nc.vector.tensor_copy(qkT[:, 4 * g:4 * g + 4, P:SEQ],
                                          bank[:, (2 * g + 1) % 4, :].rearrange("p (k t) -> p k t", t=P)).then_inc(qk_in[1], 1)
                lambda_value(l)
                dve.wait_ge(bias_ready, l + 1)
                row_max(l, 0)
                for a in range(NGL):
                    if a + 1 < NGL:
                        row_max(l, a + 1)
                    if GROUPS[a % NG][0] == "a":
                        differential(l, a)
                    if a == NG:
                        merge(l, 0)
                merge(l, 1)
                transposed(3 * l + 1)
                for i in range(U_OUT):
                    static_split(BASE_OUT[l] + i + NH)
                layer_norm(2 * l, [4, 6], BASE_OUT[l] + U_OUT)
                transposed(3 * l + 2)
                if l == 0:
                    n = gate_up(BASE_FFN, FFN_W, U_FFN_COL, 0, hT_hi, hT_lo, silu, hid, range(NT), static_split)
                    hidden_lo(len(FFN_W) - 1, FFN_W, 0, hT_hi, hT_lo, range(NT))
                    for i in range(F_DENSE // 256):
                        static_split(n + i + NH)
                    layer_norm(1, [0, 2], BASE_FFN + U_FFN)

            dve.wait_ge(xk_split, 1)
            nc.vector.tensor_tensor(xk_lo[:], xtok[:], xk_hi[:].bitcast(F32), ALU.subtract).then_inc(tok_ready, 1)
            nc.vector.tensor_scalar(xtok[:], xtok[:], ALPHA, None, ALU.mult).then_inc(added, 1)
            dve.wait_ge(logit_psum, 1)
            link(nc.vector.tensor_copy(logit[:], bank[:, 6, 0:NT * NE].rearrange("p (t e) -> p t e", e=NE)))
            other = logit[:].unsqueeze(2).broadcast_to([P, NT, NE, NE])
            own = logit[:].unsqueeze(3).broadcast_to([P, NT, NE, NE])
            nc.vector.tensor_tensor(rank3[:], other, own, ALU.is_gt)
            link(nc.vector.tensor_tensor(tie3[:], other, own, ALU.is_equal))
            flat = "p t e j -> p t (e j)"
            link(nc.vector.tensor_tensor(tie3[:].rearrange(flat), tie3[:].rearrange(flat),
                                         const("lower").unsqueeze(1).broadcast_to([P, NT, NE * NE]), ALU.mult))
            link(nc.vector.tensor_tensor(rank3[:], rank3[:], tie3[:], ALU.add))
            link(nc.vector.tensor_reduce(rank[:], rank3[:], AX.X, ALU.add))
            nc.vector.tensor_scalar(first[:], rank[:], 0.0, None, ALU.is_equal)
            nc.vector.tensor_scalar(second[:], rank[:], 1.0, None, ALU.is_equal)
            nc.vector.tensor_scalar(chosen[:], rank[:], 2.0, None, ALU.is_lt).then_inc(chosen_ready, 1)
            dve.wait_ge(chosen_ready, 1)
            link(nc.vector.tensor_tensor(pick[:], first[:], logit[:], ALU.mult))
            link(nc.vector.tensor_reduce(top[:, 0, :], pick[:], AX.X, ALU.add))
            link(nc.vector.tensor_tensor(pick[:], second[:], logit[:], ALU.mult))
            link(nc.vector.tensor_reduce(top[:, 1, :], pick[:], AX.X, ALU.add))
            nc.vector.tensor_tensor(top[:, 1, :], top[:, 1, :], top[:, 0, :], ALU.subtract).then_inc(diff_ready, 1)
            dve.wait_ge(diff_exped, 1)
            link(nc.vector.tensor_scalar(gate[:, 2, :], e_diff[:], 1.0, None, ALU.add))
            link(nc.vector.reciprocal(gate[:, 0, :], gate[:, 2, :]))
            link(nc.vector.tensor_tensor(gate[:, 1, :], gate[:, 0, :], e_diff[:], ALU.mult))
            link(nc.vector.tensor_tensor(first[:], first[:], gate[:, 0, :].unsqueeze(2).broadcast_to([P, NT, NE]), ALU.mult))
            link(nc.vector.tensor_tensor(second[:], second[:], gate[:, 1, :].unsqueeze(2).broadcast_to([P, NT, NE]), ALU.mult))
            nc.vector.tensor_tensor(comb[:, :, 0:NE], first[:], second[:], ALU.add)
            nc.vector.tensor_tensor(comb[:, :, NE:2 * NE], first[:], second[:], ALU.add)
            dve.wait_ge(pos_psum, 1)
            places = bank[:, 7, 0:NT * NE].rearrange("p (t e) -> p t e", e=NE)
            link(nc.vector.scalar_tensor_tensor(key[:, :, 0:NE], places, 1.0, chosen[:], ALU.add, ALU.mult))
            link(nc.vector.tensor_scalar(key[:, :, 0:NE], key[:, :, 0:NE], -1.0, None, ALU.add))
            nc.vector.tensor_scalar(key[:, :, NE:2 * NE], key[:, :, 0:NE], -float(P), None, ALU.add)
            link(nc.vector.tensor_reduce(most[:, 0:1], bank[:, 7, NT * NE:(NT + 1) * NE], AX.X, ALU.max))
            link(nc.vector.tensor_scalar(most[:, 1:2], most[:, 0:1], float(P), float(NE), ALU.is_gt, ALU.mult))
            nc.vector.tensor_scalar(rounds[:], most[:, 1:2], float(NE), None, ALU.add).then_inc(routed, 1)
            dve.wait_ge(routed, 1)
            n_rounds = dve.value_load(rounds[0:1, 0:1], min_val=NE, max_val=2 * NE)

            with dve.Fori(0, n_rounds) as it:
                off = it * U_MOE
                off_c = it * len(MOE_W)
                for tt in range(NT):
                    ins = nc.vector.tensor_scalar(sel[:, tt, :], const("iota"), key[:, tt, bass.ds(it, 1)], None, ALU.is_equal)
                ins.then_inc(sel_ready, 1)
                for q in range(2):
                    dve.wait_ge(gather_psum, it * 4 + (2 * q + 2))
                    nc.vector.tensor_copy(xg_lo[:, 4 * q:4 * q + 4, :],
                                          bank[:, 7, :].rearrange("p (k t) -> p k t", t=P)).then_inc(g_lo, 1)
                dve.wait_ge(selT_psum, it + 1)
                nc.vector.tensor_copy(selT[:], bank[:, 6, 0:NT * P].rearrange("p (t j) -> p t j", j=P)).then_inc(selT_in, 1)

                def loop_split(n):
                    if n < BASE_MOE + U_MOE:
                        split_lo(n, off)

                for n in range(NH):
                    split_lo(BASE_MOE + n, off)
                n = gate_up(BASE_MOE, MOE_W, MOE_COL, len(FFN_W), mT_hi, mT_lo, m_silu, m_hid, [0],
                            loop_split, off, off_c)
                hidden_lo(len(MOE_W) - 1, MOE_W, len(FFN_W), mT_hi, mT_lo, [0], off_c)
                for i in range(F_EXP // 256):
                    loop_split(n + i + NH)
                dve.wait_ge(y_hi, it + 1)
                nc.vector.tensor_tensor(yo_lo, bank[:, 2:4, :].rearrange("p b (k t) -> p (b k) t", t=P),
                                        yo_hi.bitcast(F32), ALU.subtract).then_inc(y_lo, 1)
                for q in range(4):
                    tt, ch = q // 2, q % 2
                    dve.wait_ge(scatter_psum, it * 4 + (q + 1))
                    v = xtok[:, tt, ch * CW:(ch + 1) * CW]
                    nc.vector.scalar_tensor_tensor(v, bank[:, 6 + q % 2, :], comb[:, tt, bass.ds(it, 1)], v,
                                                   ALU.mult, ALU.add).then_inc(added, 1)
            dve.wait_ge(added, 4 * NE + 1)
            layer_norm(3, None, None)

        @block.tensor
        def _(pe):
            def three(o, hi, lo, n, rhs, start, stop):
                wh, wl = rhs(w_hi[:, n % NH, :]), rhs(w_lo[:, n % NH, :])
                nc.tensor.matmul(o, hi, wh, start=start, stop=False)
                nc.tensor.matmul(o, hi, wl, start=False, stop=False)
                return nc.tensor.matmul(o, lo, wh, start=False, stop=stop)

            def transpose_round(rnd, src):
                for g in range(4):
                    tt, half = g // 2, g % 2
                    for k in range(4):
                        ins = nc.tensor.transpose(bank[:, g, k * P:(k + 1) * P], src(tt, 4 * half + k), ident)
                    ins.then_inc(t_psum, 1)

            def operand_ready(rnd):
                pe.wait_ge(t_hi, 4 * (rnd + 1))
                pe.wait_ge(t_lo, 4 * (rnd + 1))

            def unit_ready(n, off=0):
                pe.wait_ge(lo_done, n + 1 + off)

            def column_unit(n, part, parts, width, xh, xl, tts, b0, off=0):
                unit_ready(n, off)
                nk = KT // parts
                for tt in tts:
                    for k in range(nk):
                        kt = part * nk + k
                        t = slice(tt * P, (tt + 1) * P)
                        ins = three(bank[:, b0 + tt, 0:width], xh[:, kt, t], xl[:, kt, t], n,
                                    lambda w: w.rearrange("p (k n) -> p k n", k=nk)[:, k, :],
                                    kt == 0, kt == KT - 1)
                ins.then_inc(unit_used, 1)

            def row_unit(n, i, last, xh, xl, tts, b0, off=0):
                unit_ready(n, off)
                for tt in tts:
                    for k in range(2):
                        for ch in range(2):
                            t = slice(tt * P, (tt + 1) * P)
                            ins = three(bank[:, b0 + 2 * tt + ch, :], xh[:, 2 * i + k, t], xl[:, 2 * i + k, t], n,
                                        lambda w: w[:, k * D + ch * CW:k * D + (ch + 1) * CW],
                                        i == 0 and k == 0, last and k == 1)
                ins.then_inc(unit_used, 1)

            def feed_forward(ub, w, w_col, cb, xh, xl, hTh, hTl, hd, tts, off=0, off_c=0):
                def transposes(c):
                    pe.wait_ge(hid_done, cb + c + 1 + off_c)
                    back = 1 if len(tts) > 1 else 2
                    if c >= back or cb > 0:
                        pe.wait_ge(h_lo, cb + c + 1 - back + off_c)
                    for tt in tts:
                        b = 4 + tt if len(tts) > 1 else 4 + c % 2
                        for k in range(w[c] // P):
                            ins = nc.tensor.transpose(bank[:, b, k * P:(k + 1) * P], hd[:, tt, k * P:(k + 1) * P], ident)
                    ins.then_inc(h_psum, 1)

                cols = ffn_units(w_col)
                for u, (c, kind, part, parts) in enumerate(cols):
                    if part == 0 and cb + c > 0:
                        pe.wait_ge(silu_done if kind == "gate" else hid_done, cb + c + off_c)
                    column_unit(ub + u, part, parts, w[c], xh, xl, tts, 0 if kind == "gate" else len(tts), off)
                    if kind == "gate" and part == parts - 1 and c > 0:
                        transposes(c - 1)
                transposes(len(w) - 1)
                pe.wait_ge(h_lo, cb + len(w) + off_c)
                n_rows = sum(w) // 256
                for i in range(n_rows):
                    row_unit(ub + len(cols) + i, i, i == n_rows - 1, hTh, hTl, tts, 0 if len(tts) > 1 else 2, off)

            def scores(l, a):
                qt, (kind, heads) = a // NG, GROUPS[a % NG]
                ga = l * NGL + a
                if ga >= 2:
                    last_kind = GROUPS[(a - 2) % NG][0]
                    pe.wait_ge(exp_done if last_kind == "a" else max_done, ga - 1)
                for i, h in enumerate(heads):
                    q0, k0, base, size = {"a": (0, 2, (h % 2) * HD + i * DIFF, DIFF),
                                          "b": (4, 7, (h % 2) * HD, HD),
                                          "c": (10, 13, (h % 2) * HD, HD)}[kind]
                    part = slice(base, base + size)
                    ins = nc.tensor.matmul(bank[:, 2 * (ga % 2) + i, 0:SEQ], qkT[part, q0 + h // 2, qt * P:(qt + 1) * P],
                                           qkT[part, k0 + h // 2, :], start=True, stop=True)
                ins.then_inc(s_psum, 1)

            def prob_transposes(l, a):
                kind = GROUPS[a % NG][0]
                ga = l * NGL + a
                if kind == "a":
                    pe.wait_ge(diff_done, (l * NT + a // NG) * HA + a % NG + 1)
                else:
                    pe.wait_ge(exp_done, ga + 1)
                if ga >= 2:
                    pe.wait_ge(p_in, ga - 1)
                for i in range(1 if kind == "a" else 2):
                    src = prob_d[:, ga % 2] if kind == "a" else prob[:, ga % 2, i]
                    for kt in range(NT):
                        j = i * NT + kt
                        ins = nc.tensor.transpose(bank[:, 4 + ga % 2, j * P:(j + 1) * P], src[:, kt * P:(kt + 1) * P], ident)
                ins.then_inc(p_psum, 1)

            def weigh_values(l, a):
                qt, (kind, heads) = a // NG, GROUPS[a % NG]
                ga = l * NGL + a
                pe.wait_ge(p_in, ga + 1)
                if a == NG:
                    pe.wait_ge(merged, l * NT + 1)
                v0, o0 = {"a": (VA, 0), "b": (VB, HA), "c": (VC, HA + HB)}[kind]
                for i, h in enumerate(heads[:1] if kind == "a" else heads):
                    col = (o0 + h) * HD
                    for kt in range(NT):
                        ins = nc.tensor.matmul(bank[:, 6 + col // CW, col % CW:col % CW + HD],
                                               probT[:, ga % 2, i * NT + kt, :],
                                               proj[:, kt, v0 + h * HD:v0 + (h + 1) * HD],
                                               start=(kt == 0), stop=(kt == NT - 1))
                ins.then_inc(pv_done, 1)

            pe.wait_ge(x_in, 16 * NT)
            pe.wait_ge(consts_in, 16)
            for l in range(DEPTH):
                if l > 0:
                    pe.wait_ge(ln_done, 2 * NT * l)
                transpose_round(3 * l, lambda tt, kt: xtok[:, tt, kt * P:(kt + 1) * P])
                operand_ready(3 * l)
                for j in range(IN_CHUNKS):
                    if j >= 2:
                        pe.wait_ge(proj_in, (l * IN_CHUNKS + j - 1) * NT)
                    for half in range(2):
                        column_unit(BASE_IN[l] + 2 * j + half, half, 2, CW, xT_hi, xT_lo, range(NT), 4 + (j % 2) * 2)
                pe.wait_ge(proj_in, (l + 1) * IN_CHUNKS * NT)
                pe.wait_ge(roped, 2 * (l + 1))
                for g in range(4):
                    for tt in range(NT):
                        b = (2 * g + tt) % 4
                        if g >= 2:
                            pe.wait_ge(qk_in[tt], 4 * l + g - 1)
                        for k in range(4):
                            c0 = QK_TILES[4 * g + k]
                            ins = nc.tensor.transpose(bank[:, b, k * P:(k + 1) * P], proj[:, tt, c0:c0 + P], ident)
                        ins.then_inc(qk_psum, 1)
                for tt in range(NT):
                    pe.wait_ge(qk_in[tt], 4 * (l + 1))
                scores(l, 0)
                scores(l, 1)
                for a in range(NGL):
                    prob_transposes(l, a)
                    if a + 2 < NGL:
                        scores(l, a + 2)
                    if a >= 1:
                        weigh_values(l, a - 1)
                weigh_values(l, NGL - 1)
                pe.wait_ge(merged, NT * (l + 1))
                transpose_round(3 * l + 1, lambda tt, kt: proj[:, tt, MERGED_TILES[kt]:MERGED_TILES[kt] + P])
                operand_ready(3 * l + 1)
                for i in range(U_OUT):
                    row_unit(BASE_OUT[l] + i, i, i == U_OUT - 1, xT_hi, xT_lo, range(NT), 4)
                pe.wait_ge(ln_done, (2 * l + 1) * NT)
                transpose_round(3 * l + 2, lambda tt, kt: xtok[:, tt, kt * P:(kt + 1) * P])
                operand_ready(3 * l + 2)
                if l == 0:
                    feed_forward(BASE_FFN, FFN_W, U_FFN_COL, 0, xT_hi, xT_lo, hT_hi, hT_lo, hid, range(NT))

            pe.wait_ge(wr_split, 2)
            for tt in range(NT):
                for kt in range(KT):
                    t = slice(tt * P, (tt + 1) * P)
                    o = bank[:, 6, tt * NE:(tt + 1) * NE]
                    nc.tensor.matmul(o, xT_hi[:, kt, t], router_hi[:, kt, :], start=(kt == 0), stop=False)
                    nc.tensor.matmul(o, xT_hi[:, kt, t], router_lo[:, kt, :], start=False, stop=False)
                    ins = nc.tensor.matmul(o, xT_lo[:, kt, t], router_hi[:, kt, :], start=False, stop=(kt == KT - 1))
            ins.then_inc(logit_psum, 1)
            pe.wait_ge(chosen_ready, 1)
            before, ones = const("before"), const("ones")
            o = bank[:, 7, :]
            nc.tensor.matmul(o[:, 0:NE], before, chosen[:, 0, :], start=True, stop=True)
            nc.tensor.matmul(o[:, NE:2 * NE], ones, chosen[:, 0, :], start=True, stop=False)
            nc.tensor.matmul(o[:, NE:2 * NE], before, chosen[:, 1, :], start=False, stop=True)
            nc.tensor.matmul(o[:, 2 * NE:3 * NE], ones, chosen[:, 0, :], start=True, stop=False)
            nc.tensor.matmul(o[:, 2 * NE:3 * NE], ones, chosen[:, 1, :], start=False, stop=True).then_inc(pos_psum, 1)
            pe.wait_ge(tok_ready, 1)
            pe.wait_ge(routed, 1)
            n_rounds = pe.value_load(rounds[0:1, 0:1], min_val=NE, max_val=2 * NE)
            with pe.Fori(0, n_rounds) as it:
                off = it * U_MOE
                off_c = it * len(MOE_W)
                pe.wait_ge(sel_ready, it + 1)
                pe.wait_ge(added, it * 4 + 1)
                for q in range(4):
                    src = (xk_hi, xk_lo)[q % 2]
                    if q >= 2:
                        pe.wait_ge((g_hi, g_lo)[q % 2], it * 2 + 1)
                    for k in range(4):
                        kt = 4 * (q // 2) + k
                        for tt in range(NT):
                            ins = nc.tensor.matmul(bank[:, 6 + q % 2, k * P:(k + 1) * P], src[:, tt, kt * P:(kt + 1) * P],
                                                   sel[:, tt, :], start=(tt == 0), stop=(tt == NT - 1))
                    ins.then_inc(gather_psum, 1)
                pe.wait_ge(g_hi, it * 2 + 2)
                for tt in range(NT):
                    ins = nc.tensor.transpose(bank[:, 6, tt * P:(tt + 1) * P], sel[:, tt, :].bitcast(F32), ident)
                ins.then_inc(selT_psum, 1)
                pe.wait_ge(g_lo, it * 2 + 2)
                feed_forward(BASE_MOE, MOE_W, MOE_COL, len(FFN_W), xg_hi, xg_lo, mT_hi, mT_lo, m_hid, [0], off, off_c)
                pe.wait_ge(selT_in, it + 1)
                pe.wait_ge(y_lo, it + 1)
                for q in range(4):
                    tt, ch = q // 2, q % 2
                    if q >= 2:
                        pe.wait_ge(added, it * 4 + q)
                    for y, stop in ((yo_hi, False), (yo_lo, True)):
                        ins = nc.tensor.matmul(bank[:, 6 + q % 2, :], selT[:, tt, :], y[:, 4 * ch:4 * ch + 4, :],
                                               start=not stop, stop=stop)
                    ins.then_inc(scatter_psum, 1)


_INS = ["x", "w_in", "w_out", "beta_mix", "diff_lambda", "diff_norm_g", "na_rpb", "ln1_g", "ln1_b", "ln2_g", "ln2_b",
        "ffn_w_gate", "ffn_w_up", "ffn_w_down", "moe_w_router", "moe_w_gate", "moe_w_up", "moe_w_down"]


def kernel(**inputs):
    import concourse.bacc as bacc
    from concourse.bass_utils import run_bass_kernel_spmd

    nc = bacc.Bacc("TRN2", target_bir_lowering=False, num_devices=1)
    arrays, args = {}, []
    for name in _INS + ["table"]:
        a = np.ascontiguousarray(inputs[name]) if name != "table" else shape_table()
        arrays[f"in_{name}"] = a
        args.append(nc.dram_tensor(f"in_{name}", a.shape, F32, kind="ExternalInput").ap())
    args.append(nc.dram_tensor("out_x", (1, SEQ, D), F32, kind="ExternalOutput").ap())
    encoder(nc, *args)
    r = run_bass_kernel_spmd(nc, [arrays], core_ids=[0])
    return r.results[0]["out_x"]
```

```python
from contextlib import ExitStack
import math

import numpy as np
import concourse.bass as bass
from concourse import mybir

P = 128
D = 1024
SEQ = 256
NT = SEQ // P
KT = D // P
DEPTH = 2
HD = 64
HA, HB, HC = 4, 6, 6
WA, WB, WC = HA * HD, HB * HD, HC * HD
QKV = 3 * D
DIFF = HD // 2
GRID_W, NA_ROWS, NA_COLS = 64, 8, 16
ROWS = SEQ // GRID_W
F_DENSE, F_EXP, NE = 2816, 3584, 8
ALPHA = (2 * DEPTH) ** 0.25
EPS = 1e-5
NEG = -1e30
TOP = 2
MAX_LARGE = TOP * SEQ // (P + 1)
CW = 512

F32 = mybir.dt.float32
F32R = mybir.dt.float32r
I32 = mybir.dt.int32
ALU = mybir.AluOpType
ACT = mybir.ActivationFunctionType
AX = mybir.AxisListType

QA, KA, VA = 0, WA, 2 * WA
QB, KB, VB = 3 * WA, 3 * WA + WB, 3 * WA + 2 * WB
QC, KC, VC = 3 * (WA + WB), 3 * (WA + WB) + WC, 3 * (WA + WB) + 2 * WC
QK_TILES = ([c for c in range(QA, VA, P)] + [c for c in range(QB, VB, P)] + [c for c in range(QC, VC, P)])
MERGED_TILES = ([QA + c for c in range(0, WA, P)] + [QB + c for c in range(0, WB, P)]
                + [QC + c for c in range(0, WC, P)])

NR = 6
NH = 3
UNIT = 2048
IN_CHUNKS = QKV // CW
U_IN = 2 * IN_CHUNKS
U_OUT = D // 256
FFN_W = [CW] * (F_DENSE // CW) + [F_DENSE % CW]
U_FFN_COL = [2] * (F_DENSE // CW) + [1]
U_FFN = 2 * sum(U_FFN_COL) + F_DENSE // 256
BASE_IN = [0, U_IN + U_OUT + U_FFN]
BASE_OUT = [b + U_IN for b in BASE_IN]
BASE_FFN = BASE_OUT[0] + U_OUT
BASE_MOE = BASE_OUT[1] + U_OUT
MOE_W = [CW] * (F_EXP // CW)
MOE_COL = [2] * len(MOE_W)
U_MOE = 2 * sum(MOE_COL) + F_EXP // 256
GATHER_AT = 4
AT_LARGE, AT_SMALL = 14, 15
assert MAX_LARGE + NE <= AT_LARGE
SCATTER_BANKS = (0, 1, 4, 5)
OUT_BANKS = (2 * NT - 1) * (2 * DEPTH - 1)
assert U_MOE % NR == 0 and U_MOE % NH == 0 and F_DENSE % CW == 256

TABLE = {}
_at = 0
for _name, _w in (("ident", P), ("iota", P), ("before", P), ("ones", P), ("lower", NE * NE),
                  ("bias_b", NT * SEQ), ("mask_c", GRID_W), ("cos_a", NT * 8), ("sin_a", NT * 4),
                  ("cos_b", NT * 16), ("sin_b", NT * 8), ("minus_half", NT)):
    TABLE[_name] = (_at, _w)
    _at += _w
TABLE_W = _at


def shape_table():
    t = np.zeros((P, TABLE_W), np.float32)

    def put(name, a):
        o, w = TABLE[name]
        t[:, o:o + w] = np.asarray(a, np.float32).reshape(P, w)

    p = np.arange(P)
    put("ident", np.eye(P))
    put("iota", np.tile(p, (P, 1)))
    put("before", p[:, None] < p[None, :])
    put("ones", np.ones((P, P)))
    e = np.arange(NE)
    put("lower", np.tile((e[None, :] < e[:, None]).reshape(1, -1), (P, 1)))
    q = np.arange(SEQ)
    d = np.abs(q[:, None] - q[None, :])
    count = np.zeros((SEQ, SEQ))
    for window, dil in ((128, 1), (512, 4), (2048, 16)):
        count += (d % dil == 0) & (d // dil <= window // (2 * dil))
    bias = np.where(count > 0, np.log(np.maximum(count, 1)), NEG)
    put("bias_b", bias.reshape(NT, P, SEQ).transpose(1, 0, 2))
    c = np.arange(GRID_W)
    start = np.clip(c - NA_COLS // 2, 0, GRID_W - NA_COLS)
    ok = (c[None, :] >= start[:, None]) & (c[None, :] < start[:, None] + NA_COLS)
    put("mask_c", np.tile(np.where(ok, 0.0, NEG), (P // GRID_W, 1)))
    for name, rot in (("a", DIFF // 4), ("b", HD // 4)):
        inv = (np.float32(500000.0) ** (-np.arange(0, rot, 2, dtype=np.float32) / np.float32(rot))).astype(np.float32)
        ang = (np.arange(SEQ, dtype=np.float32)[:, None] * inv[None, :]).astype(np.float32)
        cos = np.cos(ang.astype(np.float64)).reshape(NT, P, rot // 2).transpose(1, 0, 2)
        sin = np.sin(ang.astype(np.float64)).reshape(NT, P, rot // 2).transpose(1, 0, 2)
        put("cos_" + name, np.concatenate([cos, cos], axis=-1))
        put("sin_" + name, sin)
    put("minus_half", np.full((P, NT), -0.5))
    return t


def encoder(nc, x, w_in, w_out, beta_mix, diff_lambda, diff_norm_g, na_rpb, ln1_g, ln1_b, ln2_g, ln2_b,
            ffn_w_gate, ffn_w_up, ffn_w_down, moe_w_router, moe_w_gate, moe_w_up, moe_w_down, table, out):
    ctx = ExitStack()
    with ctx:
        def sb(name, shape, dt=F32, scope=None):
            return (scope or ctx).enter_context(nc.sbuf_tensor(name, shape, dt))

        def sem(name):
            return ctx.enter_context(nc.semaphore(name))

        raw = sb("raw", [P, NR, UNIT])
        w_hi = sb("w_hi", [P, NH, UNIT], F32R)
        w_lo = sb("w_lo", [P, NH, UNIT], F32R)
        xtok = sb("xtok", [P, NT, D])
        xT_hi = sb("xT_hi", [P, KT, SEQ], F32R)
        xT_lo = sb("xT_lo", [P, KT, SEQ], F32R)
        rows = sb("rows", [P, 3, D])
        hid = rows[:, 0, :].rearrange("p (t n) -> p t n", t=NT)
        tab = sb("tab", [P, TABLE_W])
        gain_a = sb("gain_a", [P, DEPTH, HD])
        lam_in = sb("lam_in", [P, DEPTH, 4, DIFF])
        router_hi = sb("router_hi", [P, KT, NE], F32R)
        router_lo = sb("router_lo", [P, KT, NE], F32R)
        stats = sb("stats", [P, NT, 12])
        mean_var = sb("mean_var", [P, NT, 2])
        var_eps = sb("var_eps", [P, NT])
        rstd = sb("rstd", [P, NT])
        lam_prod = sb("lam_prod", [P, 2, DIFF])
        lam_sum = sb("lam_sum", [P, 2])
        lam_exp = sb("lam_exp", [P, 2])
        lam_neg = sb("lam_neg", [P, 1])
        with ExitStack() as s:
            proj = sb("proj", [P, NT, QKV], scope=s)
            qk_hi = sb("qk_hi", [P, KT, SEQ], F32R, scope=s)
            qk_lo = sb("qk_lo", [P, KT, SEQ], F32R, scope=s)
            bias_c = sb("bias_c", [P, HC, 6, GRID_W], scope=s)
            soft = sb("soft", [P, 12 * SEQ], scope=s)
            score = soft[:, 0:4 * SEQ].rearrange("p (a b c) -> p a b c", b=2, c=SEQ)
            prob = soft[:, 4 * SEQ:8 * SEQ].rearrange("p (a b c) -> p a b c", b=2, c=SEQ)
            probT = soft[:, 8 * SEQ:12 * SEQ].rearrange("p (a b c) -> p a b c", b=4, c=P)
            rope_b = soft[:, 0:2 * NT * 2 * HB * 16].rearrange("p (t x g w) -> p t x g w", t=NT, x=2, w=16)
            shifted = soft[:, 0:HC * 6 * GRID_W].rearrange("p (b c) -> p b c", c=GRID_W)
            rpb_rows = sb("rpb_rows", [7, HC, 2 * NA_COLS - 1], scope=s)
            rpb_pad = bias_c[0:7].rearrange("p h j c -> p (h j c)")[:, 0:HC * P].rearrange("p (h c) -> p h c", c=P)
            neg_max = sb("neg_max", [P, 4, 2], scope=s)
            sums = sb("sums", [P, NT, 20], scope=s)
            rsum = sb("rsum", [P, NT, 20], scope=s)
            oa = sb("oa", [P, HA, HD], scope=s)
            oa_sq = sb("oa_sq", [P, HA, HD], scope=s)
            rope_a = [t[:].rearrange("p h (g w) -> p (h g w)", w=8).rearrange("p (t g w) -> p t g w", t=NT, w=8)
                      for t in (oa, oa_sq)]
            ms_a = sb("ms_a", [P, HA], scope=s)
            rms_a = sb("rms_a", [P, HA], scope=s)
            half_a = sb("half_a", [P, HA], scope=s)
        with ExitStack() as s:
            hT_hi = sb("hT_hi", [P, F_EXP // P, SEQ], F32R, scope=s)
            hT_lo = sb("hT_lo", [P, F_EXP // P, SEQ], F32R, scope=s)
            acc = sb("acc", [P, NT, D], scope=s)
            chosen = sb("chosen", [P, NT, NE], scope=s)
            comb = sb("comb", [P, NT, NE], scope=s)
            key = sb("key", [P, NT, NE], scope=s)
            sel = sb("sel", [P, NT, P], scope=s)
            work = sb("work", [P, 16], I32, scope=s)
            selT = sb("selT", [P, NT, P], F32R, scope=s)
            logit = sb("logit", [P, NT, NE], scope=s)
            rank = sb("rank", [P, NT, NE], scope=s)
            first = sb("first", [P, NT, NE], scope=s)
            second = sb("second", [P, NT, NE], scope=s)
            top = sb("top", [P, 2, NT], scope=s)
            e_diff = sb("e_diff", [P, NT], scope=s)
            gate = sb("gate", [P, 3, NT], scope=s)
            rank3 = sel[:].rearrange("p t j -> p (t j)")[:, 0:NT * NE * NE].rearrange("p (t e j) -> p t e j", t=NT, e=NE)
            tie3 = sel[:].rearrange("p t j -> p (t j)")[:, NT * NE * NE:2 * NT * NE * NE].rearrange(
                "p (t e j) -> p t e j", t=NT, e=NE)
            pick = rank
            large = sb("large", [P, NE], scope=s)
            active = sb("active", [P, NE], scope=s)
            order = sb("order", [P, NE], scope=s)
            place = sb("place", [P, NE], scope=s)
            work_f = sb("work_f", [P, 16], scope=s)
        router = sb("router", [P, KT, NE])
        bank = ctx.enter_context(nc.psum_tensor("bank", [P, 8, CW], F32))
        rpb_dram = nc.dram_tensor("rpb_scratch", [DEPTH, 2, HC, 6, P], F32)

        def const(name, *shape):
            o, w = TABLE[name]
            v = tab[:, o:o + w]
            if len(shape) == 2:
                v = v.rearrange("p (a b) -> p a b", b=shape[1])
            return v

        ident = const("ident")

        x_in = [sem(f"x_in{tt}") for tt in range(NT)]
        consts_in = sem("consts_in")
        small_in = sem("small_in")
        raw_in = [sem(f"raw_in{i}") for i in range(NR)]
        hi_done = sem("hi_done")
        lo_done = sem("lo_done")
        unit_used = sem("unit_used")
        bank_done = sem("bank_done")
        t_psum = sem("t_psum")
        t_hi = sem("t_hi")
        t_lo = sem("t_lo")
        proj_in = sem("proj_in")
        roped = sem("roped")
        qk_psum = sem("qk_psum")
        qk_hi_in = sem("qk_hi_in")
        qk_lo_in = sem("qk_lo_in")
        s_psum = sem("s_psum")
        max_done = sem("max_done")
        exp_done = sem("exp_done")
        p_psum = sem("p_psum")
        p_in = sem("p_in")
        pv_done = sem("pv_done")
        o_read = sem("o_read")
        ms_ready = sem("ms_ready")
        rms_ready = sem("rms_ready")
        merged = sem("merged")
        lam_summed = sem("lam_summed")
        lam_exped = sem("lam_exped")
        beta_in = sem("beta_in")
        gb_in = sem("gb_in")
        half_set = sem("half_set")
        pad_zero = sem("pad_zero")
        pad_in = sem("pad_in")
        scratch_in = sem("scratch_in")
        toeplitz_in = sem("toeplitz_in")
        bias_ready = sem("bias_ready")
        var_ready = sem("var_ready")
        rstd_ready = sem("rstd_ready")
        ln_done = sem("ln_done")
        silu_done = sem("silu_done")
        hid_done = sem("hid_done")
        h_psum = sem("h_psum")
        h_hi = sem("h_hi")
        h_lo = sem("h_lo")
        wr_split = sem("wr_split")
        logit_psum = sem("logit_psum")
        chosen_ready = sem("chosen_ready")
        diff_ready = sem("diff_ready")
        diff_exped = sem("diff_exped")
        pos_psum = sem("pos_psum")
        routed = sem("routed")
        sel_ready = sem("sel_ready")
        gather_psum = sem("gather_psum")
        g_hi = sem("g_hi")
        g_lo = sem("g_lo")
        selT_psum = sem("selT_psum")
        selT_in = sem("selT_in")
        y_hi = sem("y_hi")
        y_lo = sem("y_lo")
        scatter_psum = sem("scatter_psum")
        added = sem("added")
        dve_step = sem("dve_step")
        out_done = sem("out_done")

        xg_hi, xg_lo = xT_hi[:, :, 0:P], xT_lo[:, :, 0:P]
        yo_hi, yo_lo = xT_hi[:, :, P:SEQ], xT_lo[:, :, P:SEQ]

        def ffn_units(w_col):
            return [(c, kind, part, n) for c, n in enumerate(w_col) for kind in ("gate", "up") for part in range(n)]

        SEGMENTS = [("a", 0), ("a", 1), ("b", 0), ("b", 1), ("c", 0), ("c", 1)]
        O_BANK = [5, 5, 6, 7, 5, 6]
        O_FREE = [0, 1, 0, 0, 2, 3]
        GROUPS = []
        for seg, (kind, qt) in enumerate(SEGMENTS):
            pairs = [(h, h) for h in range(HA)] if kind == "a" else [(h, h + 1) for h in range(0, HB, 2)]
            GROUPS += [(seg, kind, qt, pair) for pair in pairs]
        NG = len(GROUPS)
        SEG_END = [max(i for i, g in enumerate(GROUPS) if g[0] == seg) + 1 for seg in range(len(SEGMENTS))]
        NSEG = len(SEGMENTS)
        SUM_AT = {"a": 0, "b": 8, "c": 14}

        def sum_column(kind, heads, i):
            return SUM_AT[kind] + (2 * heads[0] + i if kind == "a" else heads[i])

        FIRST_SLOT = 5
        SLOTS = {FIRST_SLOT + a: a for a in range(U_IN - FIRST_SLOT)}

        def proj_banks(j):
            return 4 if j == 1 else 6

        block = ctx.enter_context(nc.Block())

        @block.sync
        def _(sp):
            for tt in range(NT):
                sp.dma_start(xtok[:, tt, :], x[0, tt * P:(tt + 1) * P, :]).then_inc(x_in[tt], 16)

            def load(n, src, off=0):
                if n >= NR:
                    sp.wait_ge(lo_done, n - NR + 1 + off)
                k = src.shape[1]
                sp.dma_start(raw[:, n % NR, :].rearrange("p (k n) -> p k n", k=k), src).then_inc(raw_in[n % NR], 16)

            def columns(w, c, part, parts, width):
                k = D // parts
                return w[part * k:(part + 1) * k, c * CW:c * CW + width].rearrange("(k p) n -> p k n", p=P)

            def row_pair(w, i):
                return w[i * 256:(i + 1) * 256, :].rearrange("(k p) n -> p k n", p=P)

            for l in range(DEPTH):
                for u in range(U_IN):
                    load(BASE_IN[l] + u, columns(w_in[l], u // 2, u % 2, 2, CW))
                for u in range(U_OUT):
                    load(BASE_OUT[l] + u, row_pair(w_out[l], u))
                if l == 0:
                    cols = ffn_units(U_FFN_COL)
                    for u, (c, kind, part, parts) in enumerate(cols):
                        w = ffn_w_gate if kind == "gate" else ffn_w_up
                        load(BASE_FFN + u, columns(w[0], c, part, parts, FFN_W[c]))
                    for i in range(F_DENSE // 256):
                        load(BASE_FFN + len(cols) + i, row_pair(ffn_w_down[0], i))

            sp.wait_ge(routed, 1)
            n_large = sp.value_load(work[0:1, AT_LARGE:AT_LARGE + 1], min_val=0, max_val=MAX_LARGE)
            n_small = sp.value_load(work[0:1, AT_SMALL:AT_SMALL + 1], min_val=0, max_val=NE)
            with sp.Fori(0, n_large + n_small) as r:
                e = sp.value_load(work[0:1, bass.ds(r, 1)], min_val=0, max_val=NE - 1)
                off = r * U_MOE
                cols = ffn_units(MOE_COL)
                for u, (c, kind, part, parts) in enumerate(cols):
                    w = moe_w_gate if kind == "gate" else moe_w_up
                    k = D // parts
                    src = w[0, bass.ds(e, 1), part * k:(part + 1) * k, c * CW:(c + 1) * CW]
                    load(BASE_MOE + u, src.rearrange("o (k p) n -> p (o k) n", p=P), off)
                for i in range(F_EXP // 256):
                    src = moe_w_down[0, bass.ds(e, 1), i * 256:(i + 1) * 256, :]
                    load(BASE_MOE + len(cols) + i, src.rearrange("o (k p) n -> p (o k) n", p=P), off)
            for tt in range(NT):
                sp.wait_ge(ln_done, 2 * NT * DEPTH - NT + tt + 1)
                sp.dma_start(out[0, tt * P:(tt + 1) * P, :], acc[:, tt, :]).then_inc(out_done, 16)
            sp.wait_ge(out_done, 16 * NT)

        @block.gpsimd
        def _(pool):
            nc.gpsimd.memset(half_a[:], -0.5).then_inc(half_set, 1)
            pool.dma_start(gain_a[:], diff_norm_g.unsqueeze(0).broadcast_to([P, DEPTH, HD])).then_inc(small_in, 16)
            pool.dma_start(lam_in[:], diff_lambda.unsqueeze(0).broadcast_to([P, DEPTH, 4, DIFF])).then_inc(small_in, 16)
            pool.dma_start(router[:], moe_w_router[0].rearrange("(k p) e -> p k e", p=P)).then_inc(small_in, 16)

            def padded_rows(l):
                nc.gpsimd.memset(bias_c[0:7], 0.0).then_inc(pad_zero, 1)
                pool.dma_start(rpb_rows[:], na_rpb[l].rearrange("h r c -> r h c")[
                    NA_ROWS - ROWS:NA_ROWS + ROWS - 1]).then_inc(pad_in, 16)
                pool.wait_ge(pad_in, 16 * (l + 1))
                pool.wait_ge(pad_zero, 2 * l + 1)
                n = 2 * NA_COLS - 1
                lo_col = GRID_W - NA_COLS
                nc.gpsimd.tensor_copy(rpb_pad[:, :, lo_col:lo_col + n], rpb_rows[:, :, ::-1]).then_inc(pad_zero, 1)
                pool.wait_ge(pad_zero, 2 * l + 2)
                for rl in range(2):
                    pool.dma_start(rpb_dram[l, rl].rearrange("h j c -> j h c"),
                                   rpb_pad[1 - rl:7 - rl]).then_inc(scratch_in, 16)
                pool.wait_ge(scratch_in, 32 * (l + 1))

            def toeplitz(l):
                for rl in range(2):
                    src = bass.AP(tensor=rpb_dram, offset=(l * 2 + rl) * HC * 6 * P,
                                  ap=[[1, GRID_W], [P, HC * 6], [1, GRID_W]])
                    pool.dma_start(shifted[rl * GRID_W:(rl + 1) * GRID_W], src).then_inc(toeplitz_in, 16)
                pool.wait_ge(toeplitz_in, 32 * (l + 1))
                pool.wait_ge(consts_in, 16)
                mask = const("mask_c").unsqueeze(1).broadcast_to([P, HC * 6, GRID_W])
                nc.gpsimd.tensor_tensor(bias_c[:].rearrange("p h j c -> p (h j) c"), shifted[:, :, ::-1], mask,
                                        ALU.add).then_inc(bias_ready, 1)

            def inverse_roots(ln):
                for tt in range(NT):
                    n = ln * NT + tt + 1
                    pool.wait_ge(var_ready, n)
                    nc.gpsimd.tensor_tensor(rstd[:, tt:tt + 1], var_eps[:, tt:tt + 1],
                                            const("minus_half")[:, 0:1], ALU.pow).then_inc(rstd_ready, 1)

            def norm_rows(ln, g, b, l):
                if ln:
                    pool.wait_ge(ln_done, NT * ln)
                pool.dma_start(rows[:, 1, :], g[l:l + 1, :].broadcast_to([P, D])).then_inc(gb_in, 16)
                pool.dma_start(rows[:, 2, :], b[l:l + 1, :].broadcast_to([P, D])).then_inc(gb_in, 16)

            for l in range(DEPTH):
                if l:
                    pool.wait_ge(ln_done, NT * 2 * l)
                padded_rows(l)
                toeplitz(l)
                pool.dma_start(rows[:, 0, :], beta_mix[l:l + 1, :].broadcast_to([P, D])).then_inc(beta_in, 16)
                norm_rows(2 * l, ln1_g, ln1_b, l)
                if l == 0:
                    pool.wait_ge(half_set, 1)
                for qt in range(NT):
                    pool.wait_ge(ms_ready, NT * l + qt + 1)
                    nc.gpsimd.tensor_tensor(rms_a[:], ms_a[:], half_a[:], ALU.pow).then_inc(rms_ready, 1)
                inverse_roots(2 * l)
                norm_rows(2 * l + 1, ln2_g, ln2_b, l)
                inverse_roots(2 * l + 1)

        @block.scalar
        def _(act):
            act.dma_start(tab[:], table).then_inc(consts_in, 16)

            def split_hi(n, off=0, use=0):
                act.wait_ge(raw_in[n % NR], 16 * (n // NR + 1) + use)
                if n >= NH:
                    act.wait_ge(unit_used, n - NH + 1 + off)
                nc.scalar.activation(w_hi[:, n % NH, :], raw[:, n % NR, :], ACT.Copy).then_inc(hi_done, 1)

            def static_split(n):
                if n < BASE_MOE:
                    split_hi(n)

            def transposed(rnd):
                for g in range(4):
                    tt, half = g // 2, g % 2
                    act.wait_ge(t_psum, 4 * rnd + g + 1)
                    nc.scalar.activation(xT_hi[:, 4 * half:4 * half + 4, tt * P:(tt + 1) * P],
                                         bank[:, g, :].rearrange("p (k t) -> p k t", t=P), ACT.Copy).then_inc(t_hi, 1)

            def qk_group(l, k):
                g, tt = k // 2, k % 2
                act.wait_ge(qk_psum, 8 * l + k + 1)
                dst = (qk_hi, xT_hi)[g // 2][:, 4 * (g % 2):4 * (g % 2) + 4, tt * P:(tt + 1) * P]
                nc.scalar.activation(dst, bank[:, k % 4, :].rearrange("p (k t) -> p k t", t=P),
                                     ACT.Copy).then_inc(qk_hi_in, 1)

            def exps(l, a):
                seg, kind, qt, heads = GROUPS[a]
                ga = l * NG + a
                act.wait_ge(max_done, ga + 1)
                if ga >= 2:
                    act.wait_ge(p_psum, ga - 1)
                for i in range(2):
                    at = sum_column(kind, heads, i)
                    src = bank[:, 2 * (ga % 2) + i, 0:SEQ] if kind == "a" else score[:, ga % 2, i, :]
                    ins = nc.scalar.activation(prob[:, ga % 2, i, :], src, ACT.Exp,
                                               bias=neg_max[:, ga % 4, i:i + 1],
                                               scale=DIFF ** -0.5 if kind == "a" else 1.0,
                                               accum_out=sums[:, qt, at:at + 1])
                ins.then_inc(exp_done, 1)

            def prob_copy(l, a):
                ga = l * NG + a
                act.wait_ge(p_psum, ga + 1)
                if ga >= 2:
                    act.wait_ge(pv_done, ga - 1)
                nc.scalar.activation(probT[:, ga % 2], bank[:, 4, :].rearrange("p (n q) -> p n q", q=P),
                                     ACT.Copy).then_inc(p_in, 1)

            def hidden_hi(c, w, cb, tts, off_c=0):
                act.wait_ge(h_psum, cb + c + 1 + off_c)
                for tt in tts:
                    n = w[c] // P
                    b = 4 + tt if len(tts) > 1 else 4 + c % 2
                    ins = nc.scalar.activation(hT_hi[:, 4 * c:4 * c + n, tt * P:(tt + 1) * P],
                                               bank[:, b, 0:w[c]].rearrange("p (k t) -> p k t", t=P), ACT.Copy)
                ins.then_inc(h_hi, 1)

            def gate_up(ub, w, w_col, cb, tts, split, off=0, off_c=0):
                cols = ffn_units(w_col)
                for u, (c, kind, part, parts) in enumerate(cols):
                    n = ub + u
                    if kind == "gate" and part == parts - 1:
                        act.wait_ge(unit_used, n + 1 + off)
                        if cb + c > 0:
                            act.wait_ge(h_psum, cb + c + off_c)
                        for tt in tts:
                            ins = nc.scalar.activation(hid[:, tt, 0:w[c]], bank[:, tt, 0:w[c]], ACT.Silu)
                        ins.then_inc(silu_done, 1)
                        if c > 0:
                            hidden_hi(c - 1, w, cb, tts, off_c)
                    split(n + NH)
                n = ub + len(cols)
                split(n + NH)
                hidden_hi(len(w) - 1, w, cb, tts, off_c)
                return n

            for l in range(DEPTH):
                if l == 0:
                    split_hi(0)
                transposed(3 * l)
                if l == 0:
                    for n in range(1, NH):
                        split_hi(n)
                for u in range(U_IN):
                    n = BASE_IN[l] + u
                    if SLOTS.get(u, 0) >= 1:
                        prob_copy(l, SLOTS[u] - 1)
                    if u in SLOTS:
                        exps(l, SLOTS[u])
                    if u % 2:
                        j = u // 2
                        act.wait_ge(unit_used, n + 1)
                        for tt in range(NT):
                            nc.scalar.activation(proj[:, tt, j * CW:(j + 1) * CW], bank[:, proj_banks(j) + tt, :],
                                                 ACT.Copy).then_inc(proj_in, 1)
                    if u == 3:
                        for k in range(2):
                            qk_group(l, k)
                    static_split(n + NH)
                    if u == 0:
                        act.wait_ge(lam_summed, l + 1)
                        nc.scalar.activation(lam_exp[:], lam_sum[:], ACT.Exp).then_inc(lam_exped, 1)
                last = SLOTS[U_IN - 1]
                exps(l, last + 1)
                prob_copy(l, last)
                for k in range(2, 8):
                    qk_group(l, k)
                prob_copy(l, last + 1)
                for a in range(last + 2, NG + 1):
                    if a < NG:
                        exps(l, a)
                    if a > last + 2:
                        prob_copy(l, a - 1)
                transposed(3 * l + 1)
                for i in range(U_OUT):
                    static_split(BASE_OUT[l] + i + NH)
                transposed(3 * l + 2)
                if l == 0:
                    n = gate_up(BASE_FFN, FFN_W, U_FFN_COL, 0, range(NT), static_split)
                    for i in range(1, F_DENSE // 256):
                        static_split(n + i + NH)

            act.wait_ge(diff_ready, 1)
            nc.scalar.activation(e_diff[:], top[:, 1, :], ACT.Exp).then_inc(diff_exped, 1)
            act.wait_ge(routed, 1)
            n_large = act.value_load(work[0:1, AT_LARGE:AT_LARGE + 1], min_val=0, max_val=MAX_LARGE)
            n_small = act.value_load(work[0:1, AT_SMALL:AT_SMALL + 1], min_val=0, max_val=NE)
            n_items = act.snap(n_large + n_small)
            for n in range(NH):
                split_hi(BASE_MOE + n)

            def expert(r, tts):
                off, off_c = r * U_MOE, r * len(MOE_W)
                use = r * (16 * U_MOE // NR)

                def loop_split(n):
                    if n < BASE_MOE + U_MOE:
                        split_hi(n, off, use)

                n = gate_up(BASE_MOE, MOE_W, MOE_COL, len(FFN_W), tts, loop_split, off, off_c)
                return n, loop_split, off, use

            def next_units(r, off, use, which):
                with act.If(r + 1 < n_items):
                    for n in which:
                        split_hi(BASE_MOE + U_MOE + n, off, use)

            with act.If(n_large > 0):
                with act.Fori(0, n_large) as r:
                    n, loop_split, off, use = expert(r, range(NT))
                    for i in range(1, F_EXP // 256 - NH):
                        loop_split(n + i + NH)
                    next_units(r, off, use, range(NH))

            def gathered(i):
                for q in range(2):
                    act.wait_ge(gather_psum, i * 2 + (q + 1))
                    nc.scalar.activation(xg_hi[:, 4 * q:4 * q + 4, :],
                                         bank[:, 6 + q, :].rearrange("p (k t) -> p k t", t=P), ACT.Copy).then_inc(g_hi, 1)

            first_out = act.snap(n_large * 3 + (OUT_BANKS + 1))
            with act.If(n_small > 0):
                gathered(0)
                with act.Fori(0, n_small) as i:
                    r = act.snap(n_large + i)
                    n, loop_split, off, use = expert(r, [0])
                    for u in range(1, F_EXP // 256 - NH):
                        loop_split(n + u + NH)
                        if u == GATHER_AT:
                            with act.If(i + 1 < n_small):
                                gathered(i + 1)
                    next_units(r, off, use, range(1))
                    for ch in range(2):
                        if ch == 0:
                            act.wait_ge(bank_done, first_out + i)
                        else:
                            act.wait_ge(unit_used, BASE_MOE + U_MOE + off)
                        nc.scalar.activation(yo_hi[:, 4 * ch:4 * ch + 4, :],
                                             bank[:, 2 + ch, :].rearrange("p (k t) -> p k t", t=P), ACT.Copy).then_inc(y_hi, 1)
                    next_units(r, off, use, range(1, NH))

        @block.vector
        def _(dve):
            steps = [0]

            def link(ins):
                steps[0] += 1
                ins.then_inc(dve_step, 1)
                dve.wait_ge(dve_step, steps[0])

            def split_lo(n, off=0):
                dve.wait_ge(hi_done, n + 1 + off)
                nc.vector.tensor_tensor(w_lo[:, n % NH, :], raw[:, n % NR, :], w_hi[:, n % NH, :].bitcast(F32),
                                        ALU.subtract).then_inc(lo_done, 1)

            def static_split(n):
                if n < BASE_MOE:
                    split_lo(n)

            def transposed(rnd):
                for g in range(4):
                    tt, half = g // 2, g % 2
                    dve.wait_ge(t_hi, 4 * rnd + g + 1)
                    at = (slice(None), slice(4 * half, 4 * half + 4), slice(tt * P, (tt + 1) * P))
                    nc.vector.tensor_tensor(xT_lo[at], bank[:, g, :].rearrange("p (k t) -> p k t", t=P),
                                            xT_hi[at].bitcast(F32), ALU.subtract).then_inc(t_lo, 1)

            def qk_group(l, k):
                g, tt = k // 2, k % 2
                dve.wait_ge(qk_hi_in, 8 * l + k + 1)
                at = (slice(None), slice(4 * (g % 2), 4 * (g % 2) + 4), slice(tt * P, (tt + 1) * P))
                nc.vector.tensor_tensor((qk_lo, xT_lo)[g // 2][at], bank[:, k % 4, :].rearrange("p (k t) -> p k t", t=P),
                                        (qk_hi, xT_hi)[g // 2][at].bitcast(F32), ALU.subtract).then_inc(qk_lo_in, 1)

            def rotary(c0, width, half, groups, name, rc, rs, chunk_count):
                dve.wait_ge(proj_in, chunk_count)
                cos = const("cos_" + name, NT, 2 * half).unsqueeze(2).broadcast_to([P, NT, groups, 2 * half])
                sin = const("sin_" + name, NT, half).unsqueeze(2).broadcast_to([P, NT, groups, half])
                v = proj[:, :, c0:c0 + groups * width].rearrange("p t (g w) -> p t g w", w=width)
                nc.vector.tensor_tensor(rc, v[:, :, :, 0:2 * half], cos, ALU.mult)
                nc.vector.tensor_tensor(rs[:, :, :, 0:half], v[:, :, :, half:2 * half], sin, ALU.mult)
                link(nc.vector.tensor_tensor(rs[:, :, :, half:2 * half], v[:, :, :, 0:half], sin, ALU.mult))
                nc.vector.tensor_tensor(v[:, :, :, 0:half], rc[:, :, :, 0:half], rs[:, :, :, 0:half], ALU.subtract)
                nc.vector.tensor_tensor(v[:, :, :, half:2 * half], rc[:, :, :, half:2 * half],
                                        rs[:, :, :, half:2 * half], ALU.add).then_inc(roped, 1)

            def lambda_terms(l):
                lam_init = 0.8 - 0.6 * math.exp(-0.3 * l)
                link(nc.vector.tensor_tensor(lam_prod[:], lam_in[:, l, 0:4:2, :], lam_in[:, l, 1:4:2, :], ALU.mult))
                nc.vector.tensor_reduce(lam_sum[:], lam_prod[:], AX.X, ALU.add).then_inc(lam_summed, 1)
                link(nc.vector.tensor_scalar(gain_a[:, l, :], gain_a[:, l, :], 1.0 - lam_init, None, ALU.mult))

            def lambda_value(l):
                lam_init = 0.8 - 0.6 * math.exp(-0.3 * l)
                dve.wait_ge(lam_exped, l + 1)
                link(nc.vector.tensor_tensor(lam_neg[:], lam_exp[:, 1:2], lam_exp[:, 0:1], ALU.subtract))
                link(nc.vector.tensor_scalar(lam_neg[:], lam_neg[:], -lam_init, None, ALU.add))

            def row_max(l, a):
                seg, kind, qt, heads = GROUPS[a]
                ga = l * NG + a
                dve.wait_ge(s_psum, ga + 1)
                s2 = bank[:, 2 * (ga % 2):2 * (ga % 2) + 2, 0:SEQ]
                nm = neg_max[:, ga % 4, :]
                if kind == "a":
                    link(nc.vector.tensor_reduce(nm, s2, AX.X, ALU.max, negate=True))
                    nc.vector.tensor_scalar(nm, nm, DIFF ** -0.5, None, ALU.mult).then_inc(max_done, 1)
                    return
                if kind == "b":
                    bias = const("bias_b", NT, SEQ)[:, qt:qt + 1, :].broadcast_to([P, 2, SEQ])
                else:
                    j0 = 2 if qt == 0 else 0
                    bias = bias_c[:, heads[0]:heads[0] + 2, j0:j0 + 4, :].rearrange("p h j c -> p h (j c)")
                sc = score[:, ga % 2]
                if ga >= 2:
                    dve.wait_ge(exp_done, ga - 1)
                link(nc.vector.scalar_tensor_tensor(sc, s2, HD ** -0.5, bias, ALU.mult, ALU.add))
                nc.vector.tensor_reduce(nm, sc, AX.X, ALU.max, negate=True).then_inc(max_done, 1)

            def merge(l, seg):
                kind, qt = SEGMENTS[seg]
                dve.wait_ge(pv_done, l * NG + SEG_END[seg])
                s0, n = SUM_AT[kind], 8 if kind == "a" else 6
                c0, w, b0 = {"a": (QA, WA, 0), "b": (QB, WB, WA), "c": (QC, WC, WA + WB)}[kind]
                r = rsum[:, qt, s0:s0 + n]
                m = proj[:, qt, c0:c0 + w].rearrange("p (h d) -> p h d", d=HD)
                link(nc.vector.reciprocal(r, sums[:, qt, s0:s0 + n]))
                if seg == 0:
                    dve.wait_ge(beta_in, 16 * (l + 1))
                o = bank[:, O_BANK[seg], 0:n * HD].rearrange("p (h d) -> p h d", d=HD)
                if kind == "a":
                    link(nc.vector.tensor_tensor(r[:, 1:n:2], r[:, 1:n:2], lam_neg[:].broadcast_to([P, HA]), ALU.mult))
                    nc.vector.tensor_tensor(oa[:], o[:, 0:n:2], r[:, 0:n:2].unsqueeze(2).broadcast_to([P, HA, HD]), ALU.mult)
                    ins = nc.vector.tensor_tensor(oa_sq[:], o[:, 1:n:2], r[:, 1:n:2].unsqueeze(2).broadcast_to([P, HA, HD]),
                                                  ALU.mult)
                    ins.then_inc(o_read, 1)
                    dve.wait_ge(o_read, l * NSEG + seg + 1)
                    link(nc.vector.tensor_tensor(oa[:], oa[:], oa_sq[:], ALU.add))
                    link(nc.vector.tensor_tensor(oa_sq[:], oa[:], oa[:], ALU.mult))
                    link(nc.vector.tensor_reduce(ms_a[:], oa_sq[:], AX.X, ALU.add))
                    nc.vector.tensor_scalar(ms_a[:], ms_a[:], 1.0 / HD, EPS, ALU.mult, ALU.add).then_inc(ms_ready, 1)
                    link(nc.vector.tensor_tensor(oa[:], oa[:], gain_a[:, l:l + 1, :].broadcast_to([P, HA, HD]), ALU.mult))
                    link(nc.vector.tensor_tensor(oa[:].rearrange("p h d -> p (h d)"), oa[:].rearrange("p h d -> p (h d)"),
                                                 rows[:, 0, b0:b0 + w], ALU.mult))
                    dve.wait_ge(rms_ready, NT * l + qt + 1)
                    nc.vector.tensor_tensor(m, oa[:], rms_a[:].unsqueeze(2).broadcast_to([P, HA, HD]),
                                            ALU.mult).then_inc(merged, 1)
                    return
                ins = nc.vector.tensor_tensor(m, o, r.unsqueeze(2).broadcast_to([P, n, HD]), ALU.mult)
                ins.then_inc(o_read, 1)
                dve.wait_ge(o_read, l * NSEG + seg + 1)
                mf = proj[:, qt, c0:c0 + w]
                nc.vector.tensor_tensor(mf, mf, rows[:, 0, b0:b0 + w], ALU.mult).then_inc(merged, 1)

            def layer_norm(ln, v2, first_bank=None, unit=0):
                for tt in range(NT):
                    v = v2[:, tt, :]
                    for h in range(2):
                        vh = v2[:, tt, h * CW:(h + 1) * CW]
                        if first_bank is not None:
                            q = 2 * tt + h
                            if q < 2 * NT - 1:
                                dve.wait_ge(bank_done, (2 * NT - 1) * ln + q + 1)
                            else:
                                dve.wait_ge(unit_used, unit)
                            link(nc.vector.scalar_tensor_tensor(vh, vh, ALPHA, bank[:, first_bank + q, :],
                                                                ALU.mult, ALU.add))
                        ins = nc.vector.bn_stats(stats[:, tt, 6 * h:6 * h + 6], vh)
                    link(ins)
                    link(nc.vector.bn_aggr(mean_var[:, tt, :], stats[:, tt, :]))
                    nc.vector.tensor_scalar(var_eps[:, tt:tt + 1], mean_var[:, tt, 1:2], EPS, None,
                                            ALU.add).then_inc(var_ready, 1)
                    if tt == 0:
                        dve.wait_ge(gb_in, 32 * (ln + 1))
                    link(nc.vector.scalar_tensor_tensor(v, v, mean_var[:, tt, 0:1], rows[:, 1, :],
                                                        ALU.subtract, ALU.mult))
                    dve.wait_ge(rstd_ready, ln * NT + tt + 1)
                    nc.vector.scalar_tensor_tensor(v, v, rstd[:, tt:tt + 1], rows[:, 2, :],
                                                   ALU.mult, ALU.add).then_inc(ln_done, 1)

            def hidden_lo(c, w, cb, tts, off_c=0):
                dve.wait_ge(h_hi, cb + c + 1 + off_c)
                for tt in tts:
                    n = w[c] // P
                    b = 4 + tt if len(tts) > 1 else 4 + c % 2
                    at = (slice(None), slice(4 * c, 4 * c + n), slice(tt * P, (tt + 1) * P))
                    ins = nc.vector.tensor_tensor(hT_lo[at], bank[:, b, 0:w[c]].rearrange("p (k t) -> p k t", t=P),
                                                  hT_hi[at].bitcast(F32), ALU.subtract)
                ins.then_inc(h_lo, 1)

            def gate_up(ub, w, w_col, cb, tts, split, off=0, off_c=0):
                cols = ffn_units(w_col)
                for u, (c, kind, part, parts) in enumerate(cols):
                    n = ub + u
                    if part == parts - 1 and kind == "up":
                        dve.wait_ge(unit_used, n + 1 + off)
                        dve.wait_ge(silu_done, cb + c + 1 + off_c)
                        for tt in tts:
                            ins = nc.vector.tensor_tensor(hid[:, tt, 0:w[c]], hid[:, tt, 0:w[c]],
                                                          bank[:, len(tts) + tt, 0:w[c]], ALU.mult)
                        ins.then_inc(hid_done, 1)
                    split(n + NH)
                    if part == parts - 1 and kind == "gate" and c > 0:
                        hidden_lo(c - 1, w, cb, tts, off_c)
                n = ub + len(cols)
                split(n + NH)
                hidden_lo(len(w) - 1, w, cb, tts, off_c)
                return n

            dve.wait_ge(consts_in, 16)
            for l in range(DEPTH):
                if l == 0:
                    split_lo(0)
                transposed(3 * l)
                if l == 0:
                    for n in range(1, NH):
                        split_lo(n)
                    dve.wait_ge(small_in, 48)
                    nc.vector.tensor_copy(router_hi[:], router[:]).then_inc(wr_split, 1)
                    dve.wait_ge(wr_split, 1)
                    nc.vector.tensor_tensor(router_lo[:], router[:], router_hi[:].bitcast(F32),
                                            ALU.subtract).then_inc(wr_split, 1)
                lambda_terms(l)
                for u in range(U_IN):
                    if u == FIRST_SLOT:
                        dve.wait_ge(bias_ready, l + 1)
                        row_max(l, 0)
                    if u in SLOTS:
                        row_max(l, SLOTS[u] + 1)
                    if SLOTS.get(u) == SEG_END[0] + 1:
                        merge(l, 0)
                    if u == 3:
                        for k in range(2):
                            qk_group(l, k)
                    static_split(BASE_IN[l] + u + NH)
                    if u == 2:
                        lambda_value(l)
                        rotary(QA, DIFF, DIFF // 8, 2 * WA // DIFF, "a", rope_a[0], rope_a[1], (l * IN_CHUNKS + 1) * NT)
                    if u == 6:
                        dve.wait_ge(bias_ready, l + 1)
                        rotary(QB, HD, HD // 8, 2 * HB, "b", rope_b[:, :, 0], rope_b[:, :, 1], (l * IN_CHUNKS + 3) * NT)
                last = SLOTS[U_IN - 1]
                for k in range(2, 8):
                    qk_group(l, k)
                for a in range(last + 2, NG):
                    row_max(l, a)
                    for seg in range(NSEG):
                        if seg > 0 and a == SEG_END[seg] + 1:
                            merge(l, seg)
                merge(l, NSEG - 1)
                transposed(3 * l + 1)
                for i in range(U_OUT):
                    static_split(BASE_OUT[l] + i + NH)
                layer_norm(2 * l, xtok, 4, BASE_OUT[l] + U_OUT)
                transposed(3 * l + 2)
                if l == 0:
                    n = gate_up(BASE_FFN, FFN_W, U_FFN_COL, 0, range(NT), static_split)
                    for i in range(1, F_DENSE // 256):
                        static_split(n + i + NH)
                    layer_norm(1, xtok, 0, BASE_FFN + U_FFN)

            nc.vector.tensor_scalar(acc[:], xtok[:], ALPHA, None, ALU.mult).then_inc(added, 1)
            dve.wait_ge(logit_psum, 1)
            link(nc.vector.tensor_copy(logit[:], bank[:, 6, 0:NT * NE].rearrange("p (t e) -> p t e", e=NE)))
            other = logit[:].unsqueeze(2).broadcast_to([P, NT, NE, NE])
            own = logit[:].unsqueeze(3).broadcast_to([P, NT, NE, NE])
            nc.vector.tensor_tensor(rank3, other, own, ALU.is_gt)
            link(nc.vector.tensor_tensor(tie3, other, own, ALU.is_equal))
            flat = "p t e j -> p t (e j)"
            link(nc.vector.tensor_tensor(tie3.rearrange(flat), tie3.rearrange(flat),
                                         const("lower").unsqueeze(1).broadcast_to([P, NT, NE * NE]), ALU.mult))
            link(nc.vector.tensor_tensor(rank3, rank3, tie3, ALU.add))
            link(nc.vector.tensor_reduce(rank[:], rank3, AX.X, ALU.add))
            nc.vector.tensor_scalar(first[:], rank[:], 0.0, None, ALU.is_equal)
            nc.vector.tensor_scalar(second[:], rank[:], 1.0, None, ALU.is_equal)
            nc.vector.tensor_scalar(chosen[:], rank[:], float(TOP), None, ALU.is_lt).then_inc(chosen_ready, 1)
            dve.wait_ge(chosen_ready, 1)
            e8 = const("iota")[:, 0:NE]
            cmp = rank3[:, 0]
            dve.wait_ge(pos_psum, 1)
            count = bank[:, 7, NT * NE:(NT + 1) * NE]
            nc.vector.tensor_scalar(large[:], count, float(P), None, ALU.is_gt)
            link(nc.vector.tensor_scalar(active[:], count, 0.0, None, ALU.is_gt))
            link(nc.vector.tensor_tensor(order[:], large[:], active[:], ALU.add))
            link(nc.vector.scalar_tensor_tensor(order[:], order[:], -float(NE), e8, ALU.mult, ALU.add))
            link(nc.vector.tensor_tensor(cmp, order[:].unsqueeze(1).broadcast_to([P, NE, NE]),
                                         order[:].unsqueeze(2).broadcast_to([P, NE, NE]), ALU.is_lt))
            link(nc.vector.tensor_reduce(place[:], cmp, AX.X, ALU.add))
            link(nc.vector.tensor_tensor(cmp, place[:].unsqueeze(1).broadcast_to([P, NE, NE]),
                                         e8.unsqueeze(2).broadcast_to([P, NE, NE]), ALU.is_equal))
            link(nc.vector.tensor_tensor(cmp, cmp, e8.unsqueeze(1).broadcast_to([P, NE, NE]), ALU.mult))
            nc.vector.tensor_reduce(work_f[:, 0:NE], cmp, AX.X, ALU.add)
            nc.vector.tensor_reduce(work_f[:, AT_LARGE:AT_LARGE + 1], large[:], AX.X, ALU.add)
            link(nc.vector.tensor_tensor(active[:], active[:], large[:], ALU.subtract))
            link(nc.vector.tensor_reduce(work_f[:, AT_SMALL:AT_SMALL + 1], active[:], AX.X, ALU.add))
            nc.vector.tensor_copy(work[:, 0:NE], work_f[:, 0:NE])
            nc.vector.tensor_copy(work[:, AT_LARGE:16], work_f[:, AT_LARGE:16]).then_inc(routed, 1)
            link(nc.vector.tensor_tensor(pick[:], first[:], logit[:], ALU.mult))
            link(nc.vector.tensor_reduce(top[:, 0, :], pick[:], AX.X, ALU.add))
            link(nc.vector.tensor_tensor(pick[:], second[:], logit[:], ALU.mult))
            link(nc.vector.tensor_reduce(top[:, 1, :], pick[:], AX.X, ALU.add))
            nc.vector.tensor_tensor(top[:, 1, :], top[:, 1, :], top[:, 0, :], ALU.subtract).then_inc(diff_ready, 1)
            dve.wait_ge(diff_exped, 1)
            link(nc.vector.tensor_scalar(gate[:, 2, :], e_diff[:], 1.0, None, ALU.add))
            link(nc.vector.reciprocal(gate[:, 0, :], gate[:, 2, :]))
            link(nc.vector.tensor_tensor(gate[:, 1, :], gate[:, 0, :], e_diff[:], ALU.mult))
            nc.vector.tensor_tensor(first[:], first[:], gate[:, 0, :].unsqueeze(2).broadcast_to([P, NT, NE]), ALU.mult)
            link(nc.vector.tensor_tensor(second[:], second[:], gate[:, 1, :].unsqueeze(2).broadcast_to([P, NT, NE]), ALU.mult))
            link(nc.vector.tensor_tensor(comb[:], first[:], second[:], ALU.add))
            places = bank[:, 7, 0:NT * NE].rearrange("p (t e) -> p t e", e=NE)
            link(nc.vector.scalar_tensor_tensor(key[:], places, 1.0, chosen[:], ALU.add, ALU.mult))
            link(nc.vector.tensor_scalar(key[:], key[:], -1.0, None, ALU.add))
            dve.wait_ge(routed, 1)
            n_large = dve.value_load(work[0:1, AT_LARGE:AT_LARGE + 1], min_val=0, max_val=MAX_LARGE)
            n_small = dve.value_load(work[0:1, AT_SMALL:AT_SMALL + 1], min_val=0, max_val=NE)
            n_items = dve.snap(n_large + n_small)
            for n in range(NH):
                split_lo(BASE_MOE + n)

            def expert(r, tts):
                off, off_c = r * U_MOE, r * len(MOE_W)

                def loop_split(n):
                    if n < BASE_MOE + U_MOE:
                        split_lo(n, off)

                n = gate_up(BASE_MOE, MOE_W, MOE_COL, len(FFN_W), tts, loop_split, off, off_c)
                return n, loop_split, off

            def next_units(r, off, which):
                with dve.If(r + 1 < n_items):
                    for n in which:
                        split_lo(BASE_MOE + U_MOE + n, off)

            def add_output(e, tt, ch, src):
                v = acc[:, tt, ch * CW:(ch + 1) * CW]
                nc.vector.scalar_tensor_tensor(v, src, comb[:, tt, bass.ds(e, 1)], v, ALU.mult, ALU.add).then_inc(added, 1)

            with dve.If(n_large > 0):
                with dve.Fori(0, n_large) as r:
                    n, loop_split, off = expert(r, range(NT))
                    for i in range(1, F_EXP // 256 - NH):
                        loop_split(n + i + NH)
                    next_units(r, off, range(NH - 1))
                    e = dve.value_load(work[0:1, bass.ds(r, 1)], min_val=0, max_val=NE - 1)
                    dve.wait_ge(added, r * 4 + 1)
                    for q in range(4):
                        if q < 3:
                            dve.wait_ge(bank_done, r * 3 + (OUT_BANKS + q + 1))
                        else:
                            dve.wait_ge(unit_used, BASE_MOE + U_MOE + off)
                        add_output(e, q // 2, q % 2, bank[:, q, :])
                    next_units(r, off, range(NH - 1, NH))

            def select(i):
                e = dve.value_load(work[0:1, bass.ds(dve.snap(n_large + i), 1)], min_val=0, max_val=NE - 1)
                for tt in range(NT):
                    ins = nc.vector.tensor_scalar(sel[:, tt, :], const("iota"), key[:, tt, bass.ds(e, 1)], None, ALU.is_equal)
                ins.then_inc(sel_ready, 1)

            def gathered(i):
                for q in range(2):
                    dve.wait_ge(g_hi, i * 2 + (q + 1))
                    nc.vector.tensor_tensor(xg_lo[:, 4 * q:4 * q + 4, :], bank[:, 6 + q, :].rearrange("p (k t) -> p k t", t=P),
                                            xg_hi[:, 4 * q:4 * q + 4, :].bitcast(F32), ALU.subtract).then_inc(g_lo, 1)

            with dve.If(n_small > 0):
                select(0)
                gathered(0)
                with dve.Fori(0, n_small) as i:
                    r = dve.snap(n_large + i)
                    dve.wait_ge(selT_psum, i + 1)
                    nc.vector.tensor_copy(selT[:], bank[:, 6, 0:NT * P].rearrange("p (t j) -> p t j", j=P)).then_inc(selT_in, 1)
                    n, loop_split, off = expert(r, [0])
                    for u in range(1, F_EXP // 256 - NH):
                        loop_split(n + u + NH)
                        if u == 1:
                            with dve.If(i + 1 < n_small):
                                select(i + 1)
                        if u == GATHER_AT:
                            with dve.If(i + 1 < n_small):
                                gathered(i + 1)
                    next_units(r, off, range(1))
                    e = dve.value_load(work[0:1, bass.ds(r, 1)], min_val=0, max_val=NE - 1)
                    for ch in range(2):
                        dve.wait_ge(y_hi, i * 2 + (ch + 1))
                        nc.vector.tensor_tensor(yo_lo[:, 4 * ch:4 * ch + 4, :],
                                                bank[:, 2 + ch, :].rearrange("p (k t) -> p k t", t=P),
                                                yo_hi[:, 4 * ch:4 * ch + 4, :].bitcast(F32), ALU.subtract).then_inc(y_lo, 1)
                    dve.wait_ge(added, r * 4 + 1)
                    for q in range(4):
                        ch, tt = q // 2, q % 2
                        dve.wait_ge(scatter_psum, i * 4 + (q + 1))
                        add_output(e, tt, ch, bank[:, SCATTER_BANKS[q], :])
                    next_units(r, off, range(1, NH))
            dve.wait_ge(added, n_items * 4 + 1)
            layer_norm(3, acc)

        @block.tensor
        def _(pe):
            def three(o, hi, lo, wh, wl, start, stop):
                nc.tensor.matmul(o, hi, wh, start=start, stop=False)
                nc.tensor.matmul(o, hi, wl, start=False, stop=False)
                return nc.tensor.matmul(o, lo, wh, start=False, stop=stop)

            def transpose_tile(rnd, tt, src, ready):
                ready()
                for half in range(2):
                    for k in range(4):
                        ins = nc.tensor.transpose(bank[:, 2 * tt + half, k * P:(k + 1) * P], src(4 * half + k), ident)
                    ins.then_inc(t_psum, 1)

            def operand_ready(rnd, tt):
                pe.wait_ge(t_hi, 4 * rnd + 2 * (tt + 1))
                pe.wait_ge(t_lo, 4 * rnd + 2 * (tt + 1))

            def operand(rnd, src, ready):
                def tile(tt):
                    transpose_tile(rnd, tt, lambda kt: src(tt, kt), lambda: ready(tt))
                    operand_ready(rnd, tt)
                return tile

            def column_unit(n, part, parts, width, xh, xl, tts, b0, off=0, between=None):
                pe.wait_ge(lo_done, n + 1 + off)
                nk = KT // parts
                wh = w_hi[:, n % NH, :].rearrange("p (k n) -> p k n", k=nk)
                wl = w_lo[:, n % NH, :].rearrange("p (k n) -> p k n", k=nk)
                for tt in tts:
                    if between:
                        between(tt)
                    for k in range(nk):
                        kt = part * nk + k
                        t = slice(tt * P, (tt + 1) * P)
                        ins = three(bank[:, b0 + tt, 0:width], xh[:, kt, t], xl[:, kt, t], wh[:, k, :], wl[:, k, :],
                                    kt == 0, kt == KT - 1)
                ins.then_inc(unit_used, 1)

            def row_unit(n, i, last, xh, xl, tts, b0, off=0, between=None):
                pe.wait_ge(lo_done, n + 1 + off)
                wh = w_hi[:, n % NH, :].rearrange("p (k n) -> p k n", k=4)
                wl = w_lo[:, n % NH, :].rearrange("p (k n) -> p k n", k=4)
                for tt in tts:
                    if between:
                        between(tt)
                    for ch in range(2):
                        for k in range(2):
                            t = slice(tt * P, (tt + 1) * P)
                            ins = three(bank[:, b0 + 2 * tt + ch, :], xh[:, 2 * i + k, t], xl[:, 2 * i + k, t],
                                        wh[:, 2 * k + ch, :], wl[:, 2 * k + ch, :],
                                        i == 0 and k == 0, last and k == 1)
                        if last and (tt, ch) != (tts[-1], 1):
                            ins.then_inc(bank_done, 1)
                ins.then_inc(unit_used, 1)

            def feed_forward(ub, w, w_col, cb, xh, xl, tts, off=0, off_c=0, first=None, gathering=None):
                def transposes(c):
                    pe.wait_ge(hid_done, cb + c + 1 + off_c)
                    if cb + c > 0:
                        pe.wait_ge(h_lo, cb + c + off_c)
                    for tt in tts:
                        b = 4 + tt if len(tts) > 1 else 4 + c % 2
                        for k in range(w[c] // P):
                            ins = nc.tensor.transpose(bank[:, b, k * P:(k + 1) * P], hid[:, tt, k * P:(k + 1) * P], ident)
                    ins.then_inc(h_psum, 1)

                cols = ffn_units(w_col)
                for u, (c, kind, part, parts) in enumerate(cols):
                    if part == 0 and cb + c > 0:
                        pe.wait_ge(silu_done if kind == "gate" else hid_done, cb + c + off_c)
                    column_unit(ub + u, part, parts, w[c], xh, xl, tts, 0 if kind == "gate" else len(tts), off,
                                first if u == 0 else None)
                    if kind == "gate" and part == parts - 1 and c > 0:
                        transposes(c - 1)
                n_rows = sum(w) // 256
                y0 = 0 if len(tts) > 1 else 2

                def bank_free(tt):
                    if tt == 1:
                        pe.wait_ge(hid_done, cb + len(w) + off_c)

                for i in range(n_rows):
                    if i == 0 and y0 == 0:
                        pe.wait_ge(silu_done, cb + len(w) + off_c)
                    if i in (0, n_rows - 1 - (n_rows - 1) % 2):
                        pe.wait_ge(h_lo, cb + (len(w) - 1 if i == 0 else len(w)) + off_c)
                    row_unit(ub + len(cols) + i, i, i == n_rows - 1, hT_hi, hT_lo, tts, y0, off,
                             bank_free if i == 0 else None)
                    if i == 0:
                        transposes(len(w) - 1)
                    if gathering and i == GATHER_AT:
                        gathering()

            def qk_group(l, k):
                g, tt = k // 2, k % 2
                if k >= 4:
                    pe.wait_ge(qk_lo_in, 8 * l + k - 3)
                for j in range(4):
                    c0 = QK_TILES[4 * g + j]
                    ins = nc.tensor.transpose(bank[:, k % 4, j * P:(j + 1) * P], proj[:, tt, c0:c0 + P], ident)
                ins.then_inc(qk_psum, 1)

            def qk_ready(l, k):
                pe.wait_ge(qk_hi_in, 8 * l + k)
                pe.wait_ge(qk_lo_in, 8 * l + k)

            def scores(l, a):
                seg, kind, qt, heads = GROUPS[a]
                ga = l * NG + a
                if a >= 2:
                    pe.wait_ge(exp_done if GROUPS[a - 2][1] == "a" else max_done, ga - 1)
                for i, h in enumerate(heads):
                    q0, k0, base, size = {"a": (0, 2, (h % 2) * HD + i * DIFF, DIFF),
                                          "b": (4, 7, (h % 2) * HD, HD),
                                          "c": (10, 13, (h % 2) * HD, HD)}[kind]
                    part = slice(base, base + size)
                    qtile, ktile = q0 + h // 2, k0 + h // 2
                    qh, ql = ((qk_hi, qk_lo), (xT_hi, xT_lo))[qtile // KT]
                    kh, kl = ((qk_hi, qk_lo), (xT_hi, xT_lo))[ktile // KT]
                    q, k = (qtile % KT, slice(qt * P, (qt + 1) * P)), ktile % KT
                    ins = three(bank[:, 2 * (ga % 2) + i, 0:SEQ], qh[part, q[0], q[1]], ql[part, q[0], q[1]],
                                kh[part, k, :], kl[part, k, :], True, True)
                ins.then_inc(s_psum, 1)

            def prob_transposes(l, a):
                ga = l * NG + a
                pe.wait_ge(exp_done, ga + 1)
                if ga >= 1:
                    pe.wait_ge(p_in, ga)
                for j in range(4):
                    i, kt = j // NT, j % NT
                    ins = nc.tensor.transpose(bank[:, 4, j * P:(j + 1) * P], prob[:, ga % 2, i, kt * P:(kt + 1) * P], ident)
                ins.then_inc(p_psum, 1)

            def weigh_values(l, a):
                seg, kind, qt, heads = GROUPS[a]
                ga = l * NG + a
                pe.wait_ge(p_in, ga + 1)
                if O_FREE[seg] and GROUPS[a - 1][0] != seg:
                    pe.wait_ge(o_read, l * NSEG + O_FREE[seg])
                v0 = {"a": VA, "b": VB, "c": VC}[kind]
                for i, h in enumerate(heads):
                    col = (2 * h + i if kind == "a" else h) * HD
                    for kt in range(NT):
                        ins = nc.tensor.matmul(bank[:, O_BANK[seg], col:col + HD], probT[:, ga % 2, i * NT + kt, :],
                                               proj[:, kt, v0 + h * HD:v0 + (h + 1) * HD],
                                               start=(kt == 0), stop=(kt == NT - 1))
                ins.then_inc(pv_done, 1)

            def token_tile(tt, kt):
                return xtok[:, tt, kt * P:(kt + 1) * P]

            pe.wait_ge(consts_in, 16)
            for l in range(DEPTH):
                first_unit = operand(3 * l, token_tile,
                                     lambda tt: pe.wait_ge(ln_done, 2 * NT * l + tt + 1 - NT) if l else pe.wait_ge(x_in[tt], 16))
                for u in range(U_IN):
                    j = u // 2
                    if u % 2 == 0 and j >= 2:
                        pe.wait_ge(proj_in, (l * IN_CHUNKS + (1 if j == 2 else j)) * NT)
                    column_unit(BASE_IN[l] + u, u % 2, 2, CW, xT_hi, xT_lo, range(NT), proj_banks(j),
                                between=first_unit if u == 0 else None)
                    if u == 3:
                        pe.wait_ge(roped, 2 * l + 1)
                        for k in range(2):
                            qk_group(l, k)
                    if u == FIRST_SLOT - 1:
                        qk_ready(l, 2)
                        pe.wait_ge(proj_in, (l * IN_CHUNKS + 2) * NT)
                        scores(l, 0)
                        scores(l, 1)
                    if u in SLOTS:
                        a = SLOTS[u]
                        if a + 2 < SEG_END[1]:
                            scores(l, a + 2)
                        prob_transposes(l, a)
                        if a >= 1:
                            weigh_values(l, a - 1)
                a = SEG_END[1] - 1
                prob_transposes(l, a)
                weigh_values(l, a - 1)
                pe.wait_ge(proj_in, (l + 1) * IN_CHUNKS * NT)
                pe.wait_ge(roped, 2 * (l + 1))
                for k in range(2, 8):
                    qk_group(l, k)
                weigh_values(l, a)
                qk_ready(l, 8)
                scores(l, a + 1)
                scores(l, a + 2)
                for a in range(SEG_END[1], NG):
                    if a + 2 < NG:
                        scores(l, a + 2)
                    prob_transposes(l, a)
                    if a > SEG_END[1]:
                        weigh_values(l, a - 1)
                weigh_values(l, NG - 1)
                first_unit = operand(3 * l + 1, lambda tt, kt: proj[:, tt, MERGED_TILES[kt]:MERGED_TILES[kt] + P],
                                     lambda tt: pe.wait_ge(merged, NSEG * l + NSEG - 1 + tt))
                for i in range(U_OUT):
                    row_unit(BASE_OUT[l] + i, i, i == U_OUT - 1, xT_hi, xT_lo, range(NT), 4,
                             between=first_unit if i == 0 else None)
                first_unit = operand(3 * l + 2, token_tile, lambda tt: pe.wait_ge(ln_done, 2 * NT * l + tt + 1))
                if l == 0:
                    feed_forward(BASE_FFN, FFN_W, U_FFN_COL, 0, xT_hi, xT_lo, range(NT), first=first_unit)

            pe.wait_ge(wr_split, 2)
            for tt in range(NT):
                first_unit(tt)
                for kt in range(KT):
                    t = slice(tt * P, (tt + 1) * P)
                    ins = three(bank[:, 6, tt * NE:(tt + 1) * NE], xT_hi[:, kt, t], xT_lo[:, kt, t],
                                router_hi[:, kt, :], router_lo[:, kt, :], kt == 0, kt == KT - 1)
            ins.then_inc(logit_psum, 1)
            pe.wait_ge(chosen_ready, 1)
            before, ones = const("before"), const("ones")
            o = bank[:, 7, :]
            nc.tensor.matmul(o[:, 0:NE], before, chosen[:, 0, :], start=True, stop=True)
            nc.tensor.matmul(o[:, NE:2 * NE], ones, chosen[:, 0, :], start=True, stop=False)
            nc.tensor.matmul(o[:, NE:2 * NE], before, chosen[:, 1, :], start=False, stop=True)
            nc.tensor.matmul(o[:, 2 * NE:3 * NE], ones, chosen[:, 0, :], start=True, stop=False)
            nc.tensor.matmul(o[:, 2 * NE:3 * NE], ones, chosen[:, 1, :], start=False, stop=True).then_inc(pos_psum, 1)

            pe.wait_ge(routed, 1)
            n_large = pe.value_load(work[0:1, AT_LARGE:AT_LARGE + 1], min_val=0, max_val=MAX_LARGE)
            n_small = pe.value_load(work[0:1, AT_SMALL:AT_SMALL + 1], min_val=0, max_val=NE)
            with pe.If(n_large > 0):
                with pe.Fori(0, n_large) as r:
                    pe.wait_ge(added, r * 4 + 1)
                    feed_forward(BASE_MOE, MOE_W, MOE_COL, len(FFN_W), xT_hi, xT_lo, range(NT),
                                 r * U_MOE, r * len(MOE_W))

            def gather(i):
                pe.wait_ge(sel_ready, i + 1)
                for q in range(2):
                    for k in range(4):
                        kt = 4 * q + k
                        for tt in range(NT):
                            ins = nc.tensor.matmul(bank[:, 6 + q, k * P:(k + 1) * P], xtok[:, tt, kt * P:(kt + 1) * P],
                                                   sel[:, tt, :], start=(tt == 0), stop=(tt == NT - 1))
                    ins.then_inc(gather_psum, 1)

            with pe.If(n_small > 0):
                gather(0)
                with pe.Fori(0, n_small) as i:
                    r = pe.snap(n_large + i)
                    pe.wait_ge(added, r * 4 + 1)
                    pe.wait_ge(g_hi, i * 2 + 2)
                    pe.wait_ge(g_lo, i * 2 + 2)
                    for tt in range(NT):
                        ins = nc.tensor.transpose(bank[:, 6, tt * P:(tt + 1) * P], sel[:, tt, :], ident)
                    ins.then_inc(selT_psum, 1)

                    def gather_next():
                        with pe.If(i + 1 < n_small):
                            pe.wait_ge(selT_in, i + 1)
                            gather(i + 1)

                    feed_forward(BASE_MOE, MOE_W, MOE_COL, len(FFN_W), xg_hi, xg_lo, [0],
                                 r * U_MOE, r * len(MOE_W), gathering=gather_next)
                    pe.wait_ge(selT_in, i + 1)
                    for q in range(4):
                        ch, tt = q // 2, q % 2
                        if tt == 0:
                            pe.wait_ge(y_lo, i * 2 + (ch + 1))
                        for y, stop in ((yo_hi, False), (yo_lo, True)):
                            ins = nc.tensor.matmul(bank[:, SCATTER_BANKS[q], :], selT[:, tt, :], y[:, 4 * ch:4 * ch + 4, :],
                                                   start=not stop, stop=stop)
                        ins.then_inc(scatter_psum, 1)


_INS = ["x", "w_in", "w_out", "beta_mix", "diff_lambda", "diff_norm_g", "na_rpb", "ln1_g", "ln1_b", "ln2_g", "ln2_b",
        "ffn_w_gate", "ffn_w_up", "ffn_w_down", "moe_w_router", "moe_w_gate", "moe_w_up", "moe_w_down"]


def kernel(**inputs):
    import concourse.bacc as bacc
    from concourse.bass_utils import run_bass_kernel_spmd

    nc = bacc.Bacc("TRN2", target_bir_lowering=False, num_devices=1)
    arrays, args = {}, []
    for name in _INS + ["table"]:
        a = np.ascontiguousarray(inputs[name]) if name != "table" else shape_table()
        arrays[f"in_{name}"] = a
        args.append(nc.dram_tensor(f"in_{name}", a.shape, F32, kind="ExternalInput").ap())
    args.append(nc.dram_tensor("out_x", (1, SEQ, D), F32, kind="ExternalOutput").ap())
    encoder(nc, *args)
    r = run_bass_kernel_spmd(nc, [arrays], core_ids=[0])
    return r.results[0]["out_x"]
```

```python
from contextlib import ExitStack
import math

import numpy as np
import concourse.bass as bass
from concourse import mybir

P = 128
D = 1024
SEQ = 256
NT = SEQ // P
KT = D // P
DEPTH = 2
HD = 64
HA, HB, HC = 4, 6, 6
WA, WB, WC = HA * HD, HB * HD, HC * HD
QKV = 3 * D
DIFF = HD // 2
GRID_W, NA_ROWS, NA_COLS = 64, 8, 16
ROWS = SEQ // GRID_W
F_DENSE, F_EXP, NE = 2816, 3584, 8
ALPHA = (2 * DEPTH) ** 0.25
EPS = 1e-5
NEG = -1e30
TOP = 2
MAX_LARGE = TOP * SEQ // (P + 1)
CW = 512

F32 = mybir.dt.float32
F32R = mybir.dt.float32r
I32 = mybir.dt.int32
ALU = mybir.AluOpType
ACT = mybir.ActivationFunctionType
AX = mybir.AxisListType

QA, KA, VA = 0, WA, 2 * WA
QB, KB, VB = 3 * WA, 3 * WA + WB, 3 * WA + 2 * WB
QC, KC, VC = 3 * (WA + WB), 3 * (WA + WB) + WC, 3 * (WA + WB) + 2 * WC
QK_TILES = ([c for c in range(QA, VA, P)] + [c for c in range(QB, VB, P)] + [c for c in range(QC, VC, P)])
MERGED_TILES = ([QA + c for c in range(0, WA, P)] + [QB + c for c in range(0, WB, P)]
                + [QC + c for c in range(0, WC, P)])

NR = 6
NH = 3
UNIT = 2048
IN_CHUNKS = QKV // CW
U_IN = 2 * IN_CHUNKS
U_OUT = D // 256
FFN_W = [CW] * (F_DENSE // CW) + [F_DENSE % CW]
U_FFN_COL = [2] * (F_DENSE // CW) + [1]
U_FFN = 2 * sum(U_FFN_COL) + F_DENSE // 256
BASE_IN = [0, U_IN + U_OUT + U_FFN]
BASE_OUT = [b + U_IN for b in BASE_IN]
BASE_FFN = BASE_OUT[0] + U_OUT
BASE_MOE = BASE_OUT[1] + U_OUT
MOE_W = [CW] * (F_EXP // CW)
MOE_COL = [2] * len(MOE_W)
U_MOE = 2 * sum(MOE_COL) + F_EXP // 256
GATHER_AT = 4
AT_LARGE, AT_SMALL = 14, 15
assert MAX_LARGE + NE <= AT_LARGE
SCATTER_BANKS = (0, 1, 4, 5)
OUT_BANKS = (2 * NT - 1) * (2 * DEPTH - 1)
assert U_MOE % NR == 0 and U_MOE % NH == 0 and F_DENSE % CW == 256

TABLE = {}
_at = 0
for _name, _w in (("ident", P), ("iota", P), ("before", P), ("ones", P), ("lower", NE * NE),
                  ("bias_b", NT * SEQ), ("mask_c", GRID_W), ("cos_a", NT * 8), ("sin_a", NT * 4),
                  ("cos_b", NT * 16), ("sin_b", NT * 8), ("minus_half", NT)):
    TABLE[_name] = (_at, _w)
    _at += _w
TABLE_W = _at


def shape_table():
    t = np.zeros((P, TABLE_W), np.float32)

    def put(name, a):
        o, w = TABLE[name]
        t[:, o:o + w] = np.asarray(a, np.float32).reshape(P, w)

    p = np.arange(P)
    put("ident", np.eye(P))
    put("iota", np.tile(p, (P, 1)))
    put("before", p[:, None] < p[None, :])
    put("ones", np.ones((P, P)))
    e = np.arange(NE)
    put("lower", np.tile((e[None, :] < e[:, None]).reshape(1, -1), (P, 1)))
    q = np.arange(SEQ)
    d = np.abs(q[:, None] - q[None, :])
    count = np.zeros((SEQ, SEQ))
    for window, dil in ((128, 1), (512, 4), (2048, 16)):
        count += (d % dil == 0) & (d // dil <= window // (2 * dil))
    bias = np.where(count > 0, np.log(np.maximum(count, 1)), NEG)
    put("bias_b", bias.reshape(NT, P, SEQ).transpose(1, 0, 2))
    c = np.arange(GRID_W)
    start = np.clip(c - NA_COLS // 2, 0, GRID_W - NA_COLS)
    ok = (c[None, :] >= start[:, None]) & (c[None, :] < start[:, None] + NA_COLS)
    put("mask_c", np.tile(np.where(ok, 0.0, NEG), (P // GRID_W, 1)))
    for name, rot in (("a", DIFF // 4), ("b", HD // 4)):
        inv = (np.float32(500000.0) ** (-np.arange(0, rot, 2, dtype=np.float32) / np.float32(rot))).astype(np.float32)
        ang = (np.arange(SEQ, dtype=np.float32)[:, None] * inv[None, :]).astype(np.float32)
        cos = np.cos(ang.astype(np.float64)).reshape(NT, P, rot // 2).transpose(1, 0, 2)
        sin = np.sin(ang.astype(np.float64)).reshape(NT, P, rot // 2).transpose(1, 0, 2)
        put("cos_" + name, np.concatenate([cos, cos], axis=-1))
        put("sin_" + name, sin)
    put("minus_half", np.full((P, NT), -0.5))
    return t


def encoder(nc, x, w_in, w_out, beta_mix, diff_lambda, diff_norm_g, na_rpb, ln1_g, ln1_b, ln2_g, ln2_b,
            ffn_w_gate, ffn_w_up, ffn_w_down, moe_w_router, moe_w_gate, moe_w_up, moe_w_down, table, out):
    ctx = ExitStack()
    with ctx:
        def sb(name, shape, dt=F32, scope=None):
            return (scope or ctx).enter_context(nc.sbuf_tensor(name, shape, dt))

        def sem(name):
            return ctx.enter_context(nc.semaphore(name))

        raw = sb("raw", [P, NR, UNIT])
        w_hi = sb("w_hi", [P, NH, UNIT], F32R)
        w_lo = sb("w_lo", [P, NH, UNIT], F32R)
        xtok = sb("xtok", [P, NT, D])
        xT_hi = sb("xT_hi", [P, KT, SEQ], F32R)
        xT_lo = sb("xT_lo", [P, KT, SEQ], F32R)
        rows = sb("rows", [P, 3, D])
        hid = rows[:, 0, :].rearrange("p (t n) -> p t n", t=NT)
        tab = sb("tab", [P, TABLE_W])
        gain_a = sb("gain_a", [P, DEPTH, HD])
        lam_in = sb("lam_in", [P, DEPTH, 4, DIFF])
        router = sb("router", [P, KT, NE])
        router_parts = sb("router_parts", [P, KT, 2 * NE], F32R)
        stats = sb("stats", [P, NT, 12])
        mean_var = sb("mean_var", [P, NT, 2])
        var_eps = sb("var_eps", [P, NT])
        rstd = sb("rstd", [P, NT])
        lam_prod = sb("lam_prod", [P, 2, DIFF])
        lam_sum = sb("lam_sum", [P, 2])
        lam_exp = sb("lam_exp", [P, 2])
        lam_neg = sb("lam_neg", [P, 1])
        with ExitStack() as s:
            proj = sb("proj", [P, NT, QKV], scope=s)
            qk_hi = sb("qk_hi", [P, KT, SEQ], F32R, scope=s)
            qk_lo = sb("qk_lo", [P, KT, SEQ], F32R, scope=s)
            bias_c = sb("bias_c", [P, HC, 6, GRID_W], scope=s)
            soft = sb("soft", [P, 12 * SEQ], scope=s)
            score = soft[:, 0:4 * SEQ].rearrange("p (a b c) -> p a b c", b=2, c=SEQ)
            prob = soft[:, 4 * SEQ:8 * SEQ].rearrange("p (a b c) -> p a b c", b=2, c=SEQ)
            probT = soft[:, 8 * SEQ:12 * SEQ].rearrange("p (a b c) -> p a b c", b=4, c=P)
            rope_b = soft[:, 0:2 * NT * 2 * HB * 16].rearrange("p (t x g w) -> p t x g w", t=NT, x=2, w=16)
            shifted = soft[:, 0:HC * 6 * GRID_W].rearrange("p (b c) -> p b c", c=GRID_W)
            rpb_rows = sb("rpb_rows", [7, HC, 2 * NA_COLS - 1], scope=s)
            rpb_pad = bias_c[0:7].rearrange("p h j c -> p (h j c)")[:, 0:HC * P].rearrange("p (h c) -> p h c", c=P)
            neg_max = sb("neg_max", [P, 4, 2], scope=s)
            sums = sb("sums", [P, NT, 20], scope=s)
            rsum = sb("rsum", [P, NT, 20], scope=s)
            oa = sb("oa", [P, HA, HD], scope=s)
            oa_sq = sb("oa_sq", [P, HA, HD], scope=s)
            rope_a = [t[:].rearrange("p h (g w) -> p (h g w)", w=8).rearrange("p (t g w) -> p t g w", t=NT, w=8)
                      for t in (oa, oa_sq)]
            ms_a = sb("ms_a", [P, HA], scope=s)
            rms_a = sb("rms_a", [P, HA], scope=s)
            half_a = sb("half_a", [P, HA], scope=s)
        with ExitStack() as s:
            hT_hi = sb("hT_hi", [P, F_EXP // P, SEQ], F32R, scope=s)
            hT_lo = sb("hT_lo", [P, F_EXP // P, SEQ], F32R, scope=s)
            acc = sb("acc", [P, NT, D], scope=s)
            chosen = sb("chosen", [P, NT, NE], scope=s)
            comb = sb("comb", [P, NT, NE], scope=s)
            key = sb("key", [P, NT, NE], scope=s)
            sel = sb("sel", [P, NT, P], scope=s)
            work = sb("work", [P, 16], I32, scope=s)
            selT = sb("selT", [P, NT, P], F32R, scope=s)
            logit = sb("logit", [P, NT, NE], scope=s)
            rank = sb("rank", [P, NT, NE], scope=s)
            first = sb("first", [P, NT, NE], scope=s)
            second = sb("second", [P, NT, NE], scope=s)
            top = sb("top", [P, 2, NT], scope=s)
            e_diff = sb("e_diff", [P, NT], scope=s)
            gate = sb("gate", [P, 3, NT], scope=s)
            rank3 = sel[:].rearrange("p t j -> p (t j)")[:, 0:NT * NE * NE].rearrange("p (t e j) -> p t e j", t=NT, e=NE)
            tie3 = sel[:].rearrange("p t j -> p (t j)")[:, NT * NE * NE:2 * NT * NE * NE].rearrange(
                "p (t e j) -> p t e j", t=NT, e=NE)
            pick = rank
            large = sb("large", [P, NE], scope=s)
            active = sb("active", [P, NE], scope=s)
            order = sb("order", [P, NE], scope=s)
            place = sb("place", [P, NE], scope=s)
            work_f = sb("work_f", [P, 16], scope=s)
        bank = ctx.enter_context(nc.psum_tensor("bank", [P, 8, CW], F32))
        rpb_dram = nc.dram_tensor("rpb_scratch", [DEPTH, 2, HC, 6, P], F32)

        def const(name, *shape):
            o, w = TABLE[name]
            v = tab[:, o:o + w]
            if len(shape) == 2:
                v = v.rearrange("p (a b) -> p a b", b=shape[1])
            return v

        ident = const("ident")

        x_in = [sem(f"x_in{tt}") for tt in range(NT)]
        ident_in = sem("ident_in")
        consts_in = sem("consts_in")
        small_in = sem("small_in")
        raw_in = [sem(f"raw_in{i}") for i in range(NR)]
        hi_done = sem("hi_done")
        lo_done = sem("lo_done")
        unit_used = sem("unit_used")
        bank_done = sem("bank_done")
        t_psum = sem("t_psum")
        t_hi = sem("t_hi")
        t_lo = sem("t_lo")
        proj_in = sem("proj_in")
        roped = sem("roped")
        qk_psum = sem("qk_psum")
        qk_hi_in = sem("qk_hi_in")
        qk_lo_in = sem("qk_lo_in")
        s_psum = sem("s_psum")
        mixed = sem("mixed")
        max_done = sem("max_done")
        exp_done = sem("exp_done")
        p_psum = sem("p_psum")
        p_in = sem("p_in")
        pv_done = sem("pv_done")
        o_read = sem("o_read")
        ms_ready = sem("ms_ready")
        rms_ready = sem("rms_ready")
        merged = sem("merged")
        lam_summed = sem("lam_summed")
        lam_exped = sem("lam_exped")
        beta_in = sem("beta_in")
        gb_in = sem("gb_in")
        half_set = sem("half_set")
        pad_zero = sem("pad_zero")
        pad_in = sem("pad_in")
        scratch_in = sem("scratch_in")
        toeplitz_in = sem("toeplitz_in")
        bias_ready = sem("bias_ready")
        var_ready = sem("var_ready")
        rstd_ready = sem("rstd_ready")
        ln_done = sem("ln_done")
        silu_done = sem("silu_done")
        hid_done = sem("hid_done")
        h_psum = sem("h_psum")
        h_hi = sem("h_hi")
        h_lo = sem("h_lo")
        wr_split = sem("wr_split")
        logit_psum = sem("logit_psum")
        chosen_ready = sem("chosen_ready")
        diff_ready = sem("diff_ready")
        diff_exped = sem("diff_exped")
        pos_psum = sem("pos_psum")
        routed = sem("routed")
        sel_ready = sem("sel_ready")
        gather_psum = sem("gather_psum")
        g_hi = sem("g_hi")
        g_lo = sem("g_lo")
        selT_psum = sem("selT_psum")
        selT_in = sem("selT_in")
        y_hi = sem("y_hi")
        y_lo = sem("y_lo")
        scatter_psum = sem("scatter_psum")
        added = sem("added")
        dve_step = sem("dve_step")
        out_done = sem("out_done")

        xg_hi, xg_lo = xT_hi[:, :, 0:P], xT_lo[:, :, 0:P]
        yo_hi, yo_lo = xT_hi[:, :, P:SEQ], xT_lo[:, :, P:SEQ]

        def ffn_units(w_col):
            return [(c, kind, part, n) for c, n in enumerate(w_col) for kind in ("gate", "up") for part in range(n)]

        SEGMENTS = [("a", 0), ("a", 1), ("b", 0), ("b", 1), ("c", 0), ("c", 1)]
        O_BANK = [5, 5, 6, 7, 5, 6]
        O_FREE = [0, 1, 0, 0, 2, 3]
        GROUPS = []
        for seg, (kind, qt) in enumerate(SEGMENTS):
            pairs = [(h, h) for h in range(HA)] if kind == "a" else [(h, h + 1) for h in range(0, HB, 2)]
            GROUPS += [(seg, kind, qt, pair) for pair in pairs]
        NG = len(GROUPS)
        SEG_END = [max(i for i, g in enumerate(GROUPS) if g[0] == seg) + 1 for seg in range(len(SEGMENTS))]
        NSEG = len(SEGMENTS)
        SUM_AT = {"a": 0, "b": 8, "c": 14}

        def prob_matrices(kind):
            return 1 if kind == "a" else 2

        def sum_column(kind, heads, i):
            return SUM_AT[kind] + (2 * heads[0] + i if kind == "a" else heads[i])

        FIRST_SLOT = 5
        SLOTS = {FIRST_SLOT + a: a for a in range(U_IN - FIRST_SLOT)}

        SPLIT_AFTER = [SEG_END[1] + 3, SEG_END[1] + 6, SEG_END[1] + 9]
        assert len(SPLIT_AFTER) == NH

        def qk_bank(k):
            return k if k < 2 else (k - 2) % 4

        def proj_banks(j):
            return 4 if j == 1 else 6

        block = ctx.enter_context(nc.Block())

        @block.sync
        def _(sp):
            def load_tokens(tt):
                sp.dma_start(xtok[:, tt, :], x[0, tt * P:(tt + 1) * P, :]).then_inc(x_in[tt], 16)

            def load(n, src, off=0):
                if n >= NR:
                    sp.wait_ge(lo_done, n - NR + 1 + off)
                k = src.shape[1]
                sp.dma_start(raw[:, n % NR, :].rearrange("p (k n) -> p k n", k=k), src).then_inc(raw_in[n % NR], 16)

            def columns(w, c, part, parts, width):
                k = D // parts
                return w[part * k:(part + 1) * k, c * CW:c * CW + width].rearrange("(k p) n -> p k n", p=P)

            def row_pair(w, i):
                return w[i * 256:(i + 1) * 256, :].rearrange("(k p) n -> p k n", p=P)

            load_tokens(0)
            for l in range(DEPTH):
                for u in range(U_IN):
                    if l == 0 and u == 1:
                        load_tokens(1)
                    if l == 0 and u == NH:
                        sp.wait_ge(scratch_in, 32)
                    load(BASE_IN[l] + u, columns(w_in[l], u // 2, u % 2, 2, CW))
                for u in range(U_OUT):
                    load(BASE_OUT[l] + u, row_pair(w_out[l], u))
                if l == 0:
                    cols = ffn_units(U_FFN_COL)
                    for u, (c, kind, part, parts) in enumerate(cols):
                        w = ffn_w_gate if kind == "gate" else ffn_w_up
                        load(BASE_FFN + u, columns(w[0], c, part, parts, FFN_W[c]))
                    for i in range(F_DENSE // 256):
                        load(BASE_FFN + len(cols) + i, row_pair(ffn_w_down[0], i))

            sp.wait_ge(routed, 1)
            n_large = sp.value_load(work[0:1, AT_LARGE:AT_LARGE + 1], min_val=0, max_val=MAX_LARGE)
            n_small = sp.value_load(work[0:1, AT_SMALL:AT_SMALL + 1], min_val=0, max_val=NE)
            with sp.Fori(0, n_large + n_small) as r:
                e = sp.value_load(work[0:1, bass.ds(r, 1)], min_val=0, max_val=NE - 1)
                off = r * U_MOE
                cols = ffn_units(MOE_COL)
                for u, (c, kind, part, parts) in enumerate(cols):
                    w = moe_w_gate if kind == "gate" else moe_w_up
                    k = D // parts
                    src = w[0, bass.ds(e, 1), part * k:(part + 1) * k, c * CW:(c + 1) * CW]
                    load(BASE_MOE + u, src.rearrange("o (k p) n -> p (o k) n", p=P), off)
                for i in range(F_EXP // 256):
                    src = moe_w_down[0, bass.ds(e, 1), i * 256:(i + 1) * 256, :]
                    load(BASE_MOE + len(cols) + i, src.rearrange("o (k p) n -> p (o k) n", p=P), off)
            for tt in range(NT):
                sp.wait_ge(ln_done, 2 * NT * DEPTH - NT + tt + 1)
                sp.dma_start(out[0, tt * P:(tt + 1) * P, :], acc[:, tt, :]).then_inc(out_done, 16)
            sp.wait_ge(out_done, 16 * NT)

        @block.gpsimd
        def _(pool):
            nc.gpsimd.memset(half_a[:], -0.5).then_inc(half_set, 1)

            def small_tables():
                pool.dma_start(lam_in[:], diff_lambda.unsqueeze(0).broadcast_to([P, DEPTH, 4, DIFF])).then_inc(small_in, 16)
                pool.dma_start(gain_a[:], diff_norm_g.unsqueeze(0).broadcast_to([P, DEPTH, HD])).then_inc(small_in, 16)
                pool.dma_start(router[:], moe_w_router[0].rearrange("(k p) e -> p k e", p=P)).then_inc(small_in, 16)

            def padded_rows(l):
                pool.dma_start(rpb_rows[:], na_rpb[l].rearrange("h r c -> r h c")[
                    NA_ROWS - ROWS:NA_ROWS + ROWS - 1]).then_inc(pad_in, 16)
                nc.gpsimd.memset(bias_c[0:7], 0.0).then_inc(pad_zero, 1)
                pool.wait_ge(pad_in, 16 * (l + 1))
                pool.wait_ge(pad_zero, 2 * l + 1)
                n = 2 * NA_COLS - 1
                lo_col = GRID_W - NA_COLS
                nc.gpsimd.tensor_copy(rpb_pad[:, :, lo_col:lo_col + n], rpb_rows[:, :, ::-1]).then_inc(pad_zero, 1)
                pool.wait_ge(pad_zero, 2 * l + 2)
                for rl in range(2):
                    pool.dma_start(rpb_dram[l, rl].rearrange("h j c -> j h c"),
                                   rpb_pad[1 - rl:7 - rl]).then_inc(scratch_in, 16)

            def toeplitz(l):
                pool.wait_ge(scratch_in, 32 * (l + 1))
                for rl in range(2):
                    src = bass.AP(tensor=rpb_dram, offset=(l * 2 + rl) * HC * 6 * P,
                                  ap=[[1, GRID_W], [P, HC * 6], [1, GRID_W]])
                    pool.dma_start(shifted[rl * GRID_W:(rl + 1) * GRID_W], src).then_inc(toeplitz_in, 16)
                pool.wait_ge(toeplitz_in, 32 * (l + 1))
                pool.wait_ge(consts_in, 16)
                mask = const("mask_c").unsqueeze(1).broadcast_to([P, HC * 6, GRID_W])
                nc.gpsimd.tensor_tensor(bias_c[:].rearrange("p h j c -> p (h j) c"), shifted[:, :, ::-1], mask,
                                        ALU.add).then_inc(bias_ready, 1)

            def inverse_roots(ln, split=None):
                for tt in range(NT):
                    if tt == 1 and split is not None:
                        pool.wait_ge(lo_done, split)
                        pool.wait_ge(hi_done, split + 1)
                        nc.gpsimd.tensor_tensor(w_lo[:, split % NH, :], raw[:, split % NR, :],
                                                w_hi[:, split % NH, :].bitcast(F32), ALU.subtract).then_inc(lo_done, 1)
                    n = ln * NT + tt + 1
                    pool.wait_ge(var_ready, n)
                    nc.gpsimd.tensor_tensor(rstd[:, tt:tt + 1], var_eps[:, tt:tt + 1],
                                            const("minus_half")[:, 0:1], ALU.pow).then_inc(rstd_ready, 1)

            def norm_rows(ln, g, b, l):
                if ln:
                    pool.wait_ge(ln_done, NT * ln)
                pool.dma_start(rows[:, 1, :], g[l:l + 1, :].broadcast_to([P, D])).then_inc(gb_in, 16)
                pool.dma_start(rows[:, 2, :], b[l:l + 1, :].broadcast_to([P, D])).then_inc(gb_in, 16)

            for l in range(DEPTH):
                if l:
                    pool.wait_ge(ln_done, NT * 2 * l)
                padded_rows(l)
                if l == 0:
                    small_tables()
                toeplitz(l)
                pool.dma_start(rows[:, 0, :], beta_mix[l:l + 1, :].broadcast_to([P, D])).then_inc(beta_in, 16)
                norm_rows(2 * l, ln1_g, ln1_b, l)
                if l == 0:
                    pool.wait_ge(half_set, 1)
                for qt in range(NT):
                    pool.wait_ge(ms_ready, NT * l + qt + 1)
                    nc.gpsimd.tensor_tensor(rms_a[:], ms_a[:], half_a[:], ALU.pow).then_inc(rms_ready, 1)
                inverse_roots(2 * l, BASE_OUT[l] + U_OUT - 2 + NH if l == 0 else None)
                norm_rows(2 * l + 1, ln2_g, ln2_b, l)
                inverse_roots(2 * l + 1, BASE_FFN + U_FFN - 2 + NH if l == 0 else None)

        @block.scalar
        def _(act):
            act.dma_start(tab[:, 0:P], table[:, 0:P]).then_inc(ident_in, 16)

            def split_hi(n, off=0, use=0):
                act.wait_ge(raw_in[n % NR], 16 * (n // NR + 1) + use)
                if n >= NH:
                    act.wait_ge(unit_used, n - NH + 1 + off)
                nc.scalar.activation(w_hi[:, n % NH, :], raw[:, n % NR, :], ACT.Copy).then_inc(hi_done, 1)

            def static_split(n):
                if n < BASE_MOE:
                    split_hi(n)

            def transposed(rnd, tt):
                for half in range(2):
                    g = 2 * tt + half
                    act.wait_ge(t_psum, 4 * rnd + g + 1)
                    nc.scalar.activation(xT_hi[:, 4 * half:4 * half + 4, tt * P:(tt + 1) * P],
                                         bank[:, g, :].rearrange("p (k t) -> p k t", t=P), ACT.Copy).then_inc(t_hi, 1)

            def qk_group(l, k):
                g, tt = k // 2, k % 2
                act.wait_ge(qk_psum, 8 * l + k + 1)
                dst = (qk_hi, xT_hi)[g // 2][:, 4 * (g % 2):4 * (g % 2) + 4, tt * P:(tt + 1) * P]
                nc.scalar.activation(dst, bank[:, qk_bank(k), :].rearrange("p (k t) -> p k t", t=P),
                                     ACT.Copy).then_inc(qk_hi_in, 1)

            def exps(l, a):
                seg, kind, qt, heads = GROUPS[a]
                ga = l * NG + a
                act.wait_ge(max_done, ga + 1)
                if ga >= 2:
                    act.wait_ge(p_psum, ga - 1)
                for i in range(2):
                    at = sum_column(kind, heads, i)
                    src = bank[:, 2 * (ga % 2) + i, 0:SEQ] if kind == "a" else score[:, ga % 2, i, :]
                    ins = nc.scalar.activation(prob[:, ga % 2, i, :], src, ACT.Exp,
                                               bias=neg_max[:, ga % 4, i:i + 1],
                                               scale=DIFF ** -0.5 if kind == "a" else 1.0,
                                               accum_out=sums[:, qt, at:at + 1])
                ins.then_inc(exp_done, 1)

            def prob_copy(l, a):
                ga = l * NG + a
                act.wait_ge(p_psum, ga + 1)
                if ga >= 2:
                    act.wait_ge(pv_done, ga - 1)
                n = NT * prob_matrices(GROUPS[a][1])
                nc.scalar.activation(probT[:, ga % 2, 0:n, :], bank[:, 4, 0:n * P].rearrange("p (n q) -> p n q", q=P),
                                     ACT.Copy).then_inc(p_in, 1)

            def next_operand(rnd, n):
                transposed(rnd, 0)
                static_split(n + NH)
                transposed(rnd, 1)

            def hidden_hi(c, w, cb, tts, off_c=0):
                act.wait_ge(h_psum, cb + c + 1 + off_c)
                for tt in tts:
                    n = w[c] // P
                    b = 4 + tt if len(tts) > 1 else 4 + c % 2
                    ins = nc.scalar.activation(hT_hi[:, 4 * c:4 * c + n, tt * P:(tt + 1) * P],
                                               bank[:, b, 0:w[c]].rearrange("p (k t) -> p k t", t=P), ACT.Copy)
                ins.then_inc(h_hi, 1)

            def gate_up(ub, w, w_col, cb, tts, split, off=0, off_c=0):
                cols = ffn_units(w_col)
                for u, (c, kind, part, parts) in enumerate(cols):
                    n = ub + u
                    if kind == "gate" and part == parts - 1:
                        act.wait_ge(unit_used, n + 1 + off)
                        if cb + c > 0:
                            act.wait_ge(h_psum, cb + c + off_c)
                        for tt in tts:
                            ins = nc.scalar.activation(hid[:, tt, 0:w[c]], bank[:, tt, 0:w[c]], ACT.Silu)
                        ins.then_inc(silu_done, 1)
                        if c > 0:
                            hidden_hi(c - 1, w, cb, tts, off_c)
                    split(n + NH)
                n = ub + len(cols)
                split(n + NH)
                hidden_hi(len(w) - 1, w, cb, tts, off_c)
                return n

            for l in range(DEPTH):
                if l == 0:
                    transposed(0, 0)
                    act.dma_start(tab[:, P:], table[:, P:]).then_inc(consts_in, 16)
                    split_hi(0)
                    split_hi(1)
                    transposed(0, 1)
                    split_hi(2)
                for u in range(U_IN):
                    n = BASE_IN[l] + u
                    if SLOTS.get(u, 0) >= 1:
                        prob_copy(l, SLOTS[u] - 1)
                    if u in SLOTS:
                        exps(l, SLOTS[u])
                        if u == U_IN - 1:
                            exps(l, SLOTS[u] + 1)
                    if u % 2:
                        j = u // 2
                        act.wait_ge(unit_used, n + 1)
                        for tt in range(NT):
                            nc.scalar.activation(proj[:, tt, j * CW:(j + 1) * CW], bank[:, proj_banks(j) + tt, :],
                                                 ACT.Copy).then_inc(proj_in, 1)
                    if u == 3:
                        for k in range(2):
                            qk_group(l, k)
                    if u < U_IN - NH:
                        static_split(n + NH)
                    if u == 3:
                        act.wait_ge(lam_summed, l + 1)
                        nc.scalar.activation(lam_exp[:], lam_sum[:], ACT.Exp).then_inc(lam_exped, 1)
                last = SLOTS[U_IN - 1]
                prob_copy(l, last)
                for k in range(2, 8):
                    if k == 4:
                        prob_copy(l, last + 1)
                    qk_group(l, k)
                for a in range(last + 2, NG + 1):
                    if a < NG:
                        exps(l, a)
                        if a in SPLIT_AFTER:
                            static_split(BASE_OUT[l] + SPLIT_AFTER.index(a))
                    if a > last + 2:
                        prob_copy(l, a - 1)
                for tt in range(NT):
                    transposed(3 * l + 1, tt)
                for i in range(U_OUT - 1):
                    static_split(BASE_OUT[l] + i + NH)
                next_operand(3 * l + 2, BASE_OUT[l] + U_OUT - 1)
                if l == 0:
                    n = gate_up(BASE_FFN, FFN_W, U_FFN_COL, 0, range(NT), static_split)
                    for i in range(1, F_DENSE // 256 - 1):
                        static_split(n + i + NH)
                    next_operand(3 * (l + 1), BASE_FFN + U_FFN - 1)

            act.wait_ge(diff_ready, 1)
            nc.scalar.activation(e_diff[:], top[:, 1, :], ACT.Exp).then_inc(diff_exped, 1)
            act.wait_ge(routed, 1)
            n_large = act.value_load(work[0:1, AT_LARGE:AT_LARGE + 1], min_val=0, max_val=MAX_LARGE)
            n_small = act.value_load(work[0:1, AT_SMALL:AT_SMALL + 1], min_val=0, max_val=NE)
            n_items = act.snap(n_large + n_small)
            for n in range(NH):
                split_hi(BASE_MOE + n)

            def expert(r, tts):
                off, off_c = r * U_MOE, r * len(MOE_W)
                use = r * (16 * U_MOE // NR)

                def loop_split(n):
                    if n < BASE_MOE + U_MOE:
                        split_hi(n, off, use)

                n = gate_up(BASE_MOE, MOE_W, MOE_COL, len(FFN_W), tts, loop_split, off, off_c)
                return n, loop_split, off, use

            def next_units(r, off, use, which, count=n_items):
                with act.If(r + 1 < count):
                    for n in which:
                        split_hi(BASE_MOE + U_MOE + n, off, use)

            with act.If(n_large > 0):
                with act.Fori(0, n_large) as r:
                    n, loop_split, off, use = expert(r, range(NT))
                    for i in range(1, F_EXP // 256 - NH):
                        loop_split(n + i + NH)
                    next_units(r, off, use, range(NH - 2))
                    next_units(r, off, use, range(NH - 2, NH), n_large)

            def gathered(i):
                for q in range(2):
                    act.wait_ge(gather_psum, i * 2 + (q + 1))
                    nc.scalar.activation(xg_hi[:, 4 * q:4 * q + 4, :],
                                         bank[:, 6 + q, :].rearrange("p (k t) -> p k t", t=P), ACT.Copy).then_inc(g_hi, 1)

            first_out = act.snap(n_large * 3 + (OUT_BANKS + 1))
            with act.If(n_small > 0):
                gathered(0)
                with act.If(n_large > 0):
                    for n in range(NH - 2, NH):
                        split_hi(BASE_MOE + n, n_large * U_MOE, n_large * (16 * U_MOE // NR))
                with act.Fori(0, n_small) as i:
                    r = act.snap(n_large + i)
                    n, loop_split, off, use = expert(r, [0])
                    for u in range(1, F_EXP // 256 - NH):
                        loop_split(n + u + NH)
                        if u == GATHER_AT:
                            with act.If(i + 1 < n_small):
                                gathered(i + 1)
                    next_units(r, off, use, range(1))
                    for ch in range(2):
                        if ch == 0:
                            act.wait_ge(bank_done, first_out + i)
                        else:
                            act.wait_ge(unit_used, BASE_MOE + U_MOE + off)
                        nc.scalar.activation(yo_hi[:, 4 * ch:4 * ch + 4, :],
                                             bank[:, 2 + ch, :].rearrange("p (k t) -> p k t", t=P), ACT.Copy).then_inc(y_hi, 1)
                    next_units(r, off, use, range(1, NH))

        @block.vector
        def _(dve):
            steps = [0]

            def link(ins):
                steps[0] += 1
                ins.then_inc(dve_step, 1)
                dve.wait_ge(dve_step, steps[0])

            def split_lo(n, off=0):
                dve.wait_ge(hi_done, n + 1 + off)
                nc.vector.tensor_tensor(w_lo[:, n % NH, :], raw[:, n % NR, :], w_hi[:, n % NH, :].bitcast(F32),
                                        ALU.subtract).then_inc(lo_done, 1)

            def static_split(n):
                if n < BASE_MOE:
                    split_lo(n)

            def transposed(rnd, tt):
                for half in range(2):
                    g = 2 * tt + half
                    dve.wait_ge(t_hi, 4 * rnd + g + 1)
                    at = (slice(None), slice(4 * half, 4 * half + 4), slice(tt * P, (tt + 1) * P))
                    nc.vector.tensor_tensor(xT_lo[at], bank[:, g, :].rearrange("p (k t) -> p k t", t=P),
                                            xT_hi[at].bitcast(F32), ALU.subtract).then_inc(t_lo, 1)

            def qk_group(l, k):
                g, tt = k // 2, k % 2
                dve.wait_ge(qk_hi_in, 8 * l + k + 1)
                at = (slice(None), slice(4 * (g % 2), 4 * (g % 2) + 4), slice(tt * P, (tt + 1) * P))
                nc.vector.tensor_tensor((qk_lo, xT_lo)[g // 2][at], bank[:, qk_bank(k), :].rearrange("p (k t) -> p k t", t=P),
                                        (qk_hi, xT_hi)[g // 2][at].bitcast(F32), ALU.subtract).then_inc(qk_lo_in, 1)

            def rotary(c0, width, half, groups, name, rc, rs, chunk_count):
                dve.wait_ge(proj_in, chunk_count)
                cos = const("cos_" + name, NT, 2 * half).unsqueeze(2).broadcast_to([P, NT, groups, 2 * half])
                sin = const("sin_" + name, NT, half).unsqueeze(2).broadcast_to([P, NT, groups, half])
                v = proj[:, :, c0:c0 + groups * width].rearrange("p t (g w) -> p t g w", w=width)
                nc.vector.tensor_tensor(rc, v[:, :, :, 0:2 * half], cos, ALU.mult)
                nc.vector.tensor_tensor(rs[:, :, :, 0:half], v[:, :, :, half:2 * half], sin, ALU.mult)
                link(nc.vector.tensor_tensor(rs[:, :, :, half:2 * half], v[:, :, :, 0:half], sin, ALU.mult))
                nc.vector.tensor_tensor(v[:, :, :, 0:half], rc[:, :, :, 0:half], rs[:, :, :, 0:half], ALU.subtract)
                nc.vector.tensor_tensor(v[:, :, :, half:2 * half], rc[:, :, :, half:2 * half],
                                        rs[:, :, :, half:2 * half], ALU.add).then_inc(roped, 1)

            def split_router():
                nc.vector.tensor_copy(router_parts[:, :, 0:NE], router[:]).then_inc(wr_split, 1)
                dve.wait_ge(wr_split, 1)
                nc.vector.tensor_tensor(router_parts[:, :, NE:2 * NE], router[:], router_parts[:, :, 0:NE].bitcast(F32),
                                        ALU.subtract).then_inc(wr_split, 1)

            def lambda_terms(l):
                lam_init = 0.8 - 0.6 * math.exp(-0.3 * l)
                link(nc.vector.tensor_tensor(lam_prod[:], lam_in[:, l, 0:4:2, :], lam_in[:, l, 1:4:2, :], ALU.mult))
                nc.vector.tensor_reduce(lam_sum[:], lam_prod[:], AX.X, ALU.add).then_inc(lam_summed, 1)
                link(nc.vector.tensor_scalar(gain_a[:, l, :], gain_a[:, l, :], 1.0 - lam_init, None, ALU.mult))

            def lambda_value(l):
                lam_init = 0.8 - 0.6 * math.exp(-0.3 * l)
                dve.wait_ge(lam_exped, l + 1)
                link(nc.vector.tensor_tensor(lam_neg[:], lam_exp[:, 1:2], lam_exp[:, 0:1], ALU.subtract))
                link(nc.vector.tensor_scalar(lam_neg[:], lam_neg[:], -lam_init, None, ALU.add))

            def row_max(l, a):
                seg, kind, qt, heads = GROUPS[a]
                ga = l * NG + a
                dve.wait_ge(s_psum, ga + 1)
                s2 = bank[:, 2 * (ga % 2):2 * (ga % 2) + 2, 0:SEQ]
                nm = neg_max[:, ga % 4, :]
                if kind == "a":
                    link(nc.vector.tensor_reduce(nm, s2, AX.X, ALU.max, negate=True))
                    nc.vector.tensor_scalar(nm, nm, DIFF ** -0.5, None, ALU.mult).then_inc(max_done, 1)
                    return
                if kind == "b":
                    bias = const("bias_b", NT, SEQ)[:, qt:qt + 1, :].broadcast_to([P, 2, SEQ])
                else:
                    j0 = 2 if qt == 0 else 0
                    bias = bias_c[:, heads[0]:heads[0] + 2, j0:j0 + 4, :].rearrange("p h j c -> p h (j c)")
                sc = score[:, ga % 2]
                if ga >= 2:
                    dve.wait_ge(exp_done, ga - 1)
                link(nc.vector.scalar_tensor_tensor(sc, s2, HD ** -0.5, bias, ALU.mult, ALU.add))
                nc.vector.tensor_reduce(nm, sc, AX.X, ALU.max, negate=True).then_inc(max_done, 1)

            def mix_maps(l, a):
                seg, kind, qt, heads = GROUPS[a]
                ga = l * NG + a
                dve.wait_ge(exp_done, ga + 1)
                s0 = sum_column(kind, heads, 0)
                p0, p1 = prob[:, ga % 2, 0, :], prob[:, ga % 2, 1, :]
                r = rsum[:, qt, s0:s0 + 2]
                link(nc.vector.reciprocal(r, sums[:, qt, s0:s0 + 2]))
                link(nc.vector.tensor_scalar(p1, p1, r[:, 1:2], lam_neg[:], ALU.mult, ALU.mult))
                nc.vector.scalar_tensor_tensor(p0, p0, r[:, 0:1], p1, ALU.mult, ALU.add).then_inc(mixed, 1)

            def merge(l, seg):
                kind, qt = SEGMENTS[seg]
                dve.wait_ge(pv_done, l * NG + SEG_END[seg])
                s0, n = SUM_AT[kind], 8 if kind == "a" else 6
                c0, w, b0 = {"a": (QA, WA, 0), "b": (QB, WB, WA), "c": (QC, WC, WA + WB)}[kind]
                r = rsum[:, qt, s0:s0 + n]
                m = proj[:, qt, c0:c0 + w].rearrange("p (h d) -> p h d", d=HD)
                if kind != "a":
                    link(nc.vector.reciprocal(r, sums[:, qt, s0:s0 + n]))
                if seg == 0:
                    dve.wait_ge(beta_in, 16 * (l + 1))
                o = bank[:, O_BANK[seg], 0:w].rearrange("p (h d) -> p h d", d=HD)
                if kind == "a":
                    nc.vector.tensor_copy(oa[:], o).then_inc(o_read, 1)
                    dve.wait_ge(o_read, l * NSEG + seg + 1)
                    link(nc.vector.tensor_tensor(oa_sq[:], oa[:], oa[:], ALU.mult))
                    link(nc.vector.tensor_reduce(ms_a[:], oa_sq[:], AX.X, ALU.add))
                    nc.vector.tensor_scalar(ms_a[:], ms_a[:], 1.0 / HD, EPS, ALU.mult, ALU.add).then_inc(ms_ready, 1)
                    link(nc.vector.tensor_tensor(oa[:], oa[:], gain_a[:, l:l + 1, :].broadcast_to([P, HA, HD]), ALU.mult))
                    link(nc.vector.tensor_tensor(oa[:].rearrange("p h d -> p (h d)"), oa[:].rearrange("p h d -> p (h d)"),
                                                 rows[:, 0, b0:b0 + w], ALU.mult))
                    dve.wait_ge(rms_ready, NT * l + qt + 1)
                    nc.vector.tensor_tensor(m, oa[:], rms_a[:].unsqueeze(2).broadcast_to([P, HA, HD]),
                                            ALU.mult).then_inc(merged, 1)
                    return
                ins = nc.vector.tensor_tensor(m, o, r.unsqueeze(2).broadcast_to([P, n, HD]), ALU.mult)
                ins.then_inc(o_read, 1)
                dve.wait_ge(o_read, l * NSEG + seg + 1)
                mf = proj[:, qt, c0:c0 + w]
                nc.vector.tensor_tensor(mf, mf, rows[:, 0, b0:b0 + w], ALU.mult).then_inc(merged, 1)

            def norm_sums(ln, tt, v, first_bank=None, unit=0, between=None):
                for h in range(2):
                    vh = v[:, h * CW:(h + 1) * CW]
                    if first_bank is not None:
                        q = 2 * tt + h
                        if q < 2 * NT - 1:
                            dve.wait_ge(bank_done, (2 * NT - 1) * ln + q + 1)
                        else:
                            dve.wait_ge(unit_used, unit + 1)
                        link(nc.vector.scalar_tensor_tensor(vh, vh, ALPHA, bank[:, first_bank + q, :],
                                                            ALU.mult, ALU.add))
                    ins = nc.vector.bn_stats(stats[:, tt, 6 * h:6 * h + 6], vh)
                    if h == 0 and between:
                        between()
                link(ins)
                link(nc.vector.bn_aggr(mean_var[:, tt, :], stats[:, tt, :]))
                nc.vector.tensor_scalar(var_eps[:, tt:tt + 1], mean_var[:, tt, 1:2], EPS, None,
                                        ALU.add).then_inc(var_ready, 1)

            def normalise(ln, tt, v):
                if tt == 0:
                    dve.wait_ge(gb_in, 32 * (ln + 1))
                link(nc.vector.scalar_tensor_tensor(v, v, mean_var[:, tt, 0:1], rows[:, 1, :],
                                                    ALU.subtract, ALU.mult))
                dve.wait_ge(rstd_ready, ln * NT + tt + 1)
                nc.vector.scalar_tensor_tensor(v, v, rstd[:, tt:tt + 1], rows[:, 2, :],
                                               ALU.mult, ALU.add).then_inc(ln_done, 1)

            def norm_and_operand(ln, first_bank, n, rnd):
                norm_sums(ln, 0, xtok[:, 0, :], first_bank, n)
                normalise(ln, 0, xtok[:, 0, :])
                norm_sums(ln, 1, xtok[:, 1, :], first_bank, n, lambda: transposed(rnd, 0))
                normalise(ln, 1, xtok[:, 1, :])
                if n + NH < BASE_MOE:
                    dve.wait_ge(lo_done, n + NH)
                    split_lo(n + NH)
                transposed(rnd, 1)

            def hidden_lo(c, w, cb, tts, off_c=0):
                dve.wait_ge(h_hi, cb + c + 1 + off_c)
                for tt in tts:
                    n = w[c] // P
                    b = 4 + tt if len(tts) > 1 else 4 + c % 2
                    at = (slice(None), slice(4 * c, 4 * c + n), slice(tt * P, (tt + 1) * P))
                    ins = nc.vector.tensor_tensor(hT_lo[at], bank[:, b, 0:w[c]].rearrange("p (k t) -> p k t", t=P),
                                                  hT_hi[at].bitcast(F32), ALU.subtract)
                ins.then_inc(h_lo, 1)

            def gate_up(ub, w, w_col, cb, tts, split, off=0, off_c=0):
                cols = ffn_units(w_col)
                for u, (c, kind, part, parts) in enumerate(cols):
                    n = ub + u
                    if part == parts - 1 and kind == "up":
                        dve.wait_ge(unit_used, n + 1 + off)
                        dve.wait_ge(silu_done, cb + c + 1 + off_c)
                        for tt in tts:
                            ins = nc.vector.tensor_tensor(hid[:, tt, 0:w[c]], hid[:, tt, 0:w[c]],
                                                          bank[:, len(tts) + tt, 0:w[c]], ALU.mult)
                        ins.then_inc(hid_done, 1)
                    split(n + NH)
                    if part == parts - 1 and kind == "gate" and c > 0:
                        hidden_lo(c - 1, w, cb, tts, off_c)
                n = ub + len(cols)
                split(n + NH)
                hidden_lo(len(w) - 1, w, cb, tts, off_c)
                return n

            for l in range(DEPTH):
                if l == 0:
                    transposed(0, 0)
                    split_lo(0)
                    split_lo(1)
                    transposed(0, 1)
                    split_lo(2)
                for u in range(U_IN):
                    if u == FIRST_SLOT:
                        dve.wait_ge(bias_ready, l + 1)
                        row_max(l, 0)
                    if u in SLOTS:
                        row_max(l, SLOTS[u] + 1)
                        mix_maps(l, SLOTS[u])
                    if u == U_IN - 1:
                        mix_maps(l, SLOTS[u] + 1)
                    if SLOTS.get(u) == SEG_END[0] + 1:
                        merge(l, 0)
                    if u == 3:
                        for k in range(2):
                            qk_group(l, k)
                    if u < U_IN - NH:
                        static_split(BASE_IN[l] + u + NH)
                    if u == 3:
                        if l == 0:
                            dve.wait_ge(small_in, 48)
                            split_router()
                        lambda_terms(l)
                    if u == 4:
                        lambda_value(l)
                    if u == 2:
                        if l == 0:
                            dve.wait_ge(consts_in, 16)
                        rotary(QA, DIFF, DIFF // 8, 2 * WA // DIFF, "a", rope_a[0], rope_a[1], (l * IN_CHUNKS + 1) * NT)
                    if u == 6:
                        dve.wait_ge(bias_ready, l + 1)
                        rotary(QB, HD, HD // 8, 2 * HB, "b", rope_b[:, :, 0], rope_b[:, :, 1], (l * IN_CHUNKS + 3) * NT)
                last = SLOTS[U_IN - 1]
                for k in range(2, 8):
                    qk_group(l, k)
                for a in range(last + 2, NG):
                    row_max(l, a)
                    if a in SPLIT_AFTER:
                        static_split(BASE_OUT[l] + SPLIT_AFTER.index(a))
                    for seg in range(NSEG):
                        if seg > 0 and a == SEG_END[seg] + 2:
                            merge(l, seg)
                transposed(3 * l + 1, 0)
                merge(l, NSEG - 1)
                transposed(3 * l + 1, 1)
                for i in range(U_OUT - 2):
                    static_split(BASE_OUT[l] + i + NH)
                norm_and_operand(2 * l, 4, BASE_OUT[l] + U_OUT - 1, 3 * l + 2)
                if l == 0:
                    n = gate_up(BASE_FFN, FFN_W, U_FFN_COL, 0, range(NT), static_split)
                    for i in range(1, F_DENSE // 256 - 2):
                        static_split(n + i + NH)
                    norm_and_operand(1, 0, BASE_FFN + U_FFN - 1, 3)

            for tt in range(NT):
                for ch in range(2):
                    c = slice(ch * CW, (ch + 1) * CW)
                    nc.vector.tensor_scalar(acc[:, tt, c], xtok[:, tt, c], ALPHA, None, ALU.mult).then_inc(added, 1)
            dve.wait_ge(logit_psum, 1)
            link(nc.vector.tensor_reduce(logit[:], bank[:, 6, 0:NT * 2 * NE].rearrange("p (t b e) -> p t e b", b=2, e=NE),
                                         AX.X, ALU.add))
            other = logit[:].unsqueeze(2).broadcast_to([P, NT, NE, NE])
            own = logit[:].unsqueeze(3).broadcast_to([P, NT, NE, NE])
            nc.vector.tensor_tensor(rank3, other, own, ALU.is_gt)
            link(nc.vector.tensor_tensor(tie3, other, own, ALU.is_equal))
            flat = "p t e j -> p t (e j)"
            link(nc.vector.tensor_tensor(tie3.rearrange(flat), tie3.rearrange(flat),
                                         const("lower").unsqueeze(1).broadcast_to([P, NT, NE * NE]), ALU.mult))
            link(nc.vector.tensor_tensor(rank3, rank3, tie3, ALU.add))
            link(nc.vector.tensor_reduce(rank[:], rank3, AX.X, ALU.add))
            nc.vector.tensor_scalar(first[:], rank[:], 0.0, None, ALU.is_equal)
            nc.vector.tensor_scalar(second[:], rank[:], 1.0, None, ALU.is_equal)
            nc.vector.tensor_scalar(chosen[:], rank[:], float(TOP), None, ALU.is_lt).then_inc(chosen_ready, 1)
            dve.wait_ge(chosen_ready, 1)
            e8 = const("iota")[:, 0:NE]
            cmp = rank3[:, 0]
            dve.wait_ge(pos_psum, 1)
            count = bank[:, 7, NT * NE:(NT + 1) * NE]
            nc.vector.tensor_scalar(large[:], count, float(P), None, ALU.is_gt)
            link(nc.vector.tensor_scalar(active[:], count, 0.0, None, ALU.is_gt))
            link(nc.vector.tensor_tensor(order[:], large[:], active[:], ALU.add))
            link(nc.vector.scalar_tensor_tensor(order[:], order[:], -float(NE), e8, ALU.mult, ALU.add))
            link(nc.vector.tensor_tensor(cmp, order[:].unsqueeze(1).broadcast_to([P, NE, NE]),
                                         order[:].unsqueeze(2).broadcast_to([P, NE, NE]), ALU.is_lt))
            link(nc.vector.tensor_reduce(place[:], cmp, AX.X, ALU.add))
            link(nc.vector.tensor_tensor(cmp, place[:].unsqueeze(1).broadcast_to([P, NE, NE]),
                                         e8.unsqueeze(2).broadcast_to([P, NE, NE]), ALU.is_equal))
            link(nc.vector.tensor_tensor(cmp, cmp, e8.unsqueeze(1).broadcast_to([P, NE, NE]), ALU.mult))
            nc.vector.tensor_reduce(work_f[:, 0:NE], cmp, AX.X, ALU.add)
            nc.vector.tensor_reduce(work_f[:, AT_LARGE:AT_LARGE + 1], large[:], AX.X, ALU.add)
            link(nc.vector.tensor_tensor(active[:], active[:], large[:], ALU.subtract))
            link(nc.vector.tensor_reduce(work_f[:, AT_SMALL:AT_SMALL + 1], active[:], AX.X, ALU.add))
            nc.vector.tensor_copy(work[:, 0:NE], work_f[:, 0:NE])
            nc.vector.tensor_copy(work[:, AT_LARGE:16], work_f[:, AT_LARGE:16]).then_inc(routed, 1)
            link(nc.vector.tensor_tensor(pick[:], first[:], logit[:], ALU.mult))
            link(nc.vector.tensor_reduce(top[:, 0, :], pick[:], AX.X, ALU.add))
            link(nc.vector.tensor_tensor(pick[:], second[:], logit[:], ALU.mult))
            link(nc.vector.tensor_reduce(top[:, 1, :], pick[:], AX.X, ALU.add))
            nc.vector.tensor_tensor(top[:, 1, :], top[:, 1, :], top[:, 0, :], ALU.subtract).then_inc(diff_ready, 1)
            dve.wait_ge(diff_exped, 1)
            link(nc.vector.tensor_scalar(gate[:, 2, :], e_diff[:], 1.0, None, ALU.add))
            link(nc.vector.reciprocal(gate[:, 0, :], gate[:, 2, :]))
            link(nc.vector.tensor_tensor(gate[:, 1, :], gate[:, 0, :], e_diff[:], ALU.mult))
            nc.vector.tensor_tensor(first[:], first[:], gate[:, 0, :].unsqueeze(2).broadcast_to([P, NT, NE]), ALU.mult)
            link(nc.vector.tensor_tensor(second[:], second[:], gate[:, 1, :].unsqueeze(2).broadcast_to([P, NT, NE]), ALU.mult))
            link(nc.vector.tensor_tensor(comb[:], first[:], second[:], ALU.add))
            places = bank[:, 7, 0:NT * NE].rearrange("p (t e) -> p t e", e=NE)
            link(nc.vector.scalar_tensor_tensor(key[:], places, 1.0, chosen[:], ALU.add, ALU.mult))
            link(nc.vector.tensor_scalar(key[:], key[:], -1.0, None, ALU.add))
            dve.wait_ge(routed, 1)
            n_large = dve.value_load(work[0:1, AT_LARGE:AT_LARGE + 1], min_val=0, max_val=MAX_LARGE)
            n_small = dve.value_load(work[0:1, AT_SMALL:AT_SMALL + 1], min_val=0, max_val=NE)
            n_items = dve.snap(n_large + n_small)

            def expert(r, tts):
                off, off_c = r * U_MOE, r * len(MOE_W)

                def loop_split(n):
                    if n < BASE_MOE + U_MOE:
                        split_lo(n, off)

                n = gate_up(BASE_MOE, MOE_W, MOE_COL, len(FFN_W), tts, loop_split, off, off_c)
                return n, loop_split, off

            def next_units(r, off, which, count=n_items):
                with dve.If(r + 1 < count):
                    for n in which:
                        split_lo(BASE_MOE + U_MOE + n, off)

            def add_output(e, tt, ch, src):
                v = acc[:, tt, ch * CW:(ch + 1) * CW]
                nc.vector.scalar_tensor_tensor(v, src, comb[:, tt, bass.ds(e, 1)], v, ALU.mult, ALU.add).then_inc(added, 1)

            def select(i):
                e = dve.value_load(work[0:1, bass.ds(dve.snap(n_large + i), 1)], min_val=0, max_val=NE - 1)
                for tt in range(NT):
                    ins = nc.vector.tensor_scalar(sel[:, tt, :], const("iota"), key[:, tt, bass.ds(e, 1)], None, ALU.is_equal)
                ins.then_inc(sel_ready, 1)

            with dve.If(n_small > 0):
                select(0)
            for n in range(NH):
                split_lo(BASE_MOE + n)

            with dve.If(n_large > 0):
                with dve.Fori(0, n_large) as r:
                    n, loop_split, off = expert(r, range(NT))
                    for i in range(1, F_EXP // 256 - NH):
                        loop_split(n + i + NH)
                    next_units(r, off, range(NH - 2))
                    e = dve.value_load(work[0:1, bass.ds(r, 1)], min_val=0, max_val=NE - 1)
                    dve.wait_ge(added, r * 4 + 4)
                    for q in range(4):
                        if q == 2:
                            next_units(r, off, [NH - 2], n_large)
                        if q < 3:
                            dve.wait_ge(bank_done, r * 3 + (OUT_BANKS + q + 1))
                        else:
                            dve.wait_ge(unit_used, BASE_MOE + U_MOE + off)
                        add_output(e, q // 2, q % 2, bank[:, q, :])
                    next_units(r, off, [NH - 1], n_large)

            def gathered(i):
                for q in range(2):
                    dve.wait_ge(g_hi, i * 2 + (q + 1))
                    nc.vector.tensor_tensor(xg_lo[:, 4 * q:4 * q + 4, :], bank[:, 6 + q, :].rearrange("p (k t) -> p k t", t=P),
                                            xg_hi[:, 4 * q:4 * q + 4, :].bitcast(F32), ALU.subtract).then_inc(g_lo, 1)

            with dve.If(n_small > 0):
                gathered(0)
                with dve.If(n_large > 0):
                    for n in range(NH - 2, NH):
                        split_lo(BASE_MOE + n, n_large * U_MOE)
                with dve.Fori(0, n_small) as i:
                    r = dve.snap(n_large + i)
                    dve.wait_ge(selT_psum, i + 1)
                    nc.vector.tensor_copy(selT[:], bank[:, 6, 0:NT * P].rearrange("p (t j) -> p t j", j=P)).then_inc(selT_in, 1)
                    n, loop_split, off = expert(r, [0])
                    for u in range(1, F_EXP // 256 - NH):
                        loop_split(n + u + NH)
                        if u == 1:
                            with dve.If(i + 1 < n_small):
                                select(i + 1)
                        if u == GATHER_AT:
                            with dve.If(i + 1 < n_small):
                                gathered(i + 1)
                    next_units(r, off, range(1))
                    e = dve.value_load(work[0:1, bass.ds(r, 1)], min_val=0, max_val=NE - 1)
                    for ch in range(2):
                        dve.wait_ge(y_hi, i * 2 + (ch + 1))
                        nc.vector.tensor_tensor(yo_lo[:, 4 * ch:4 * ch + 4, :],
                                                bank[:, 2 + ch, :].rearrange("p (k t) -> p k t", t=P),
                                                yo_hi[:, 4 * ch:4 * ch + 4, :].bitcast(F32), ALU.subtract).then_inc(y_lo, 1)
                    dve.wait_ge(added, r * 4 + 4)
                    for q in range(4):
                        ch, tt = q // 2, q % 2
                        dve.wait_ge(scatter_psum, i * 4 + (q + 1))
                        add_output(e, tt, ch, bank[:, SCATTER_BANKS[q], :])
                    next_units(r, off, range(1, NH))
            dve.wait_ge(added, n_items * 4 + 4)
            for tt in range(NT):
                norm_sums(3, tt, acc[:, tt, :])
                normalise(3, tt, acc[:, tt, :])

        @block.tensor
        def _(pe):
            def with_hi(o, hi, lo, wh, start):
                nc.tensor.matmul(o, hi, wh, start=start, stop=False)
                nc.tensor.matmul(o, lo, wh, start=False, stop=False)

            def three(o, hi, lo, wh, wl, start, stop):
                nc.tensor.matmul(o, hi, wh, start=start, stop=False)
                nc.tensor.matmul(o, hi, wl, start=False, stop=False)
                return nc.tensor.matmul(o, lo, wh, start=False, stop=stop)

            def transpose_tile(rnd, tt, src, ready):
                ready()
                for half in range(2):
                    for k in range(4):
                        ins = nc.tensor.transpose(bank[:, 2 * tt + half, k * P:(k + 1) * P], src(4 * half + k), ident)
                    ins.then_inc(t_psum, 1)

            def operand(rnd, src, ready, after=0):
                def transposed(tt):
                    transpose_tile(rnd, tt, lambda kt: src(tt, kt), lambda: ready(tt))

                def tile_ready(tt, half):
                    pe.wait_ge(t_hi, 4 * rnd + 2 * tt + half + 1)
                    pe.wait_ge(t_lo, 4 * rnd + 2 * tt + half + 1)

                transposed(0)
                return tile_ready, transposed, after

            def column_units(n, group, parts, width, xh, xl, tts, b0, off=0, tile_ready=None, next_tile=None,
                             after=0):
                for tt in tts:
                    for g, part in enumerate(group):
                        if tile_ready:
                            tile_ready(tt, part)
                        if tt == tts[0]:
                            pe.wait_ge(hi_done, n + g + 1 + off)
                        slot = (n + g) % NH
                        nk = KT // parts
                        wh = w_hi[:, slot, :].rearrange("p (k n) -> p k n", k=nk)
                        wl = w_lo[:, slot, :].rearrange("p (k n) -> p k n", k=nk)
                        t = slice(tt * P, (tt + 1) * P)
                        o = bank[:, b0 + tt, 0:width]
                        for k in range(nk):
                            kt = part * nk + k
                            with_hi(o, xh[:, kt, t], xl[:, kt, t], wh[:, k, :], kt == 0)
                        if tt == tts[0]:
                            pe.wait_ge(lo_done, n + g + 1 + off)
                        for k in range(nk):
                            kt = part * nk + k
                            ins = nc.tensor.matmul(o, xh[:, kt, t], wl[:, k, :], start=False, stop=kt == KT - 1)
                        if tt == tts[-1]:
                            ins.then_inc(unit_used, 1)
                        if next_tile and g == after and tt != tts[-1]:
                            next_tile(tt + 1)

            def row_units(n, group, last, xh, xl, tts, b0, off=0, tile_ready=None, next_tile=None,
                          after=0):
                for tt in tts:
                    for g, i in enumerate(group):
                        if tile_ready:
                            tile_ready(tt, i * 4 // KT)
                        if tt == tts[0]:
                            pe.wait_ge(hi_done, n + g + 1 + off)
                        slot = (n + g) % NH
                        wh = w_hi[:, slot, :].rearrange("p (k n) -> p k n", k=4)
                        wl = w_lo[:, slot, :].rearrange("p (k n) -> p k n", k=4)
                        t = slice(tt * P, (tt + 1) * P)
                        for ch in range(2):
                            for k in range(2):
                                with_hi(bank[:, b0 + 2 * tt + ch, :], xh[:, 2 * i + k, t], xl[:, 2 * i + k, t],
                                        wh[:, 2 * k + ch, :], i == 0 and k == 0)
                        if tt == tts[0]:
                            pe.wait_ge(lo_done, n + g + 1 + off)
                        for ch in range(2):
                            for k in range(2):
                                ins = nc.tensor.matmul(bank[:, b0 + 2 * tt + ch, :], xh[:, 2 * i + k, t],
                                                       wl[:, 2 * k + ch, :], start=False, stop=i == last and k == 1)
                            if i == last and (tt, ch) != (tts[-1], 1):
                                ins.then_inc(bank_done, 1)
                        if tt == tts[-1]:
                            ins.then_inc(unit_used, 1)
                        if next_tile and g == after and tt != tts[-1]:
                            next_tile(tt + 1)

            def feed_forward(ub, w, w_col, cb, xh, xl, tts, off=0, off_c=0, first=None, gathering=None, last_added=None):
                def transposes(c):
                    pe.wait_ge(hid_done, cb + c + 1 + off_c)
                    if cb + c > 0:
                        pe.wait_ge(h_lo, cb + c + off_c)
                    for tt in tts:
                        b = 4 + tt if len(tts) > 1 else 4 + c % 2
                        for k in range(w[c] // P):
                            ins = nc.tensor.transpose(bank[:, b, k * P:(k + 1) * P], hid[:, tt, k * P:(k + 1) * P], ident)
                    ins.then_inc(h_psum, 1)

                at = 0
                for c, parts in enumerate(w_col):
                    for kind in ("gate", "up"):
                        if cb + c > 0:
                            pe.wait_ge(silu_done if kind == "gate" else hid_done, cb + c + off_c)
                        if c == 0 and kind == "up" and last_added is not None:
                            pe.wait_ge(added, last_added)
                        b0 = 0 if kind == "gate" else len(tts)
                        if at == 0 and first:
                            column_units(ub, range(parts), parts, w[c], xh, xl, tts, b0, off, *first)
                        else:
                            for part in range(parts):
                                column_units(ub + at + part, [part], parts, w[c], xh, xl, tts, b0, off)
                        at += parts
                        if kind == "gate" and c > 0:
                            transposes(c - 1)
                n_rows = sum(w) // 256
                y0 = 0 if len(tts) > 1 else 2

                def bank_free(tt, _):
                    if tt == 1:
                        pe.wait_ge(hid_done, cb + len(w) + off_c)

                for group in row_groups(n_rows, tts):
                    i = group[0]
                    if i == 0 and y0 == 0:
                        pe.wait_ge(silu_done, cb + len(w) + off_c)
                    if i in (0, n_rows - 1 - (n_rows - 1) % 2):
                        pe.wait_ge(h_lo, cb + (len(w) - 1 if i == 0 else len(w)) + off_c)
                    row_units(ub + at + i, group, n_rows - 1, hT_hi, hT_lo, tts, y0, off,
                              bank_free if i == 0 else None)
                    if i == 0:
                        transposes(len(w) - 1)
                    if gathering and i == GATHER_AT:
                        gathering()

            def row_groups(n, tts):
                return [[i] for i in range(n)] if len(tts) == 1 else [[i] for i in range(n - 2)] + [[n - 2, n - 1]]

            def qk_group(l, k):
                g, tt = k // 2, k % 2
                if k >= 6:
                    pe.wait_ge(qk_lo_in, 8 * l + k - 3)
                for j in range(4):
                    c0 = QK_TILES[4 * g + j]
                    ins = nc.tensor.transpose(bank[:, qk_bank(k), j * P:(j + 1) * P], proj[:, tt, c0:c0 + P], ident)
                ins.then_inc(qk_psum, 1)

            def qk_ready(l, k):
                pe.wait_ge(qk_hi_in, 8 * l + k)
                pe.wait_ge(qk_lo_in, 8 * l + k)

            def scores(l, a):
                seg, kind, qt, heads = GROUPS[a]
                ga = l * NG + a
                if a >= 2:
                    pe.wait_ge(exp_done if GROUPS[a - 2][1] == "a" else max_done, ga - 1)
                for i, h in enumerate(heads):
                    q0, k0, base, size = {"a": (0, 2, (h % 2) * HD + i * DIFF, DIFF),
                                          "b": (4, 7, (h % 2) * HD, HD),
                                          "c": (10, 13, (h % 2) * HD, HD)}[kind]
                    part = slice(base, base + size)
                    qtile, ktile = q0 + h // 2, k0 + h // 2
                    qh, ql = ((qk_hi, qk_lo), (xT_hi, xT_lo))[qtile // KT]
                    kh, kl = ((qk_hi, qk_lo), (xT_hi, xT_lo))[ktile // KT]
                    q, k = (qtile % KT, slice(qt * P, (qt + 1) * P)), ktile % KT
                    ins = three(bank[:, 2 * (ga % 2) + i, 0:SEQ], qh[part, q[0], q[1]], ql[part, q[0], q[1]],
                                kh[part, k, :], kl[part, k, :], True, True)
                ins.then_inc(s_psum, 1)

            def prob_transposes(l, a):
                ga = l * NG + a
                kind = GROUPS[a][1]
                if kind == "a":
                    pe.wait_ge(mixed, l * SEG_END[1] + a + 1)
                else:
                    pe.wait_ge(exp_done, ga + 1)
                if ga >= 1:
                    pe.wait_ge(p_in, ga)
                for j in range(NT * prob_matrices(kind)):
                    i, kt = j // NT, j % NT
                    ins = nc.tensor.transpose(bank[:, 4, j * P:(j + 1) * P], prob[:, ga % 2, i, kt * P:(kt + 1) * P], ident)
                ins.then_inc(p_psum, 1)

            def weigh_values(l, a):
                seg, kind, qt, heads = GROUPS[a]
                ga = l * NG + a
                pe.wait_ge(p_in, ga + 1)
                if O_FREE[seg] and GROUPS[a - 1][0] != seg:
                    pe.wait_ge(o_read, l * NSEG + O_FREE[seg])
                v0 = {"a": VA, "b": VB, "c": VC}[kind]
                for i, h in enumerate(heads[0:prob_matrices(kind)]):
                    col = h * HD
                    for kt in range(NT):
                        ins = nc.tensor.matmul(bank[:, O_BANK[seg], col:col + HD], probT[:, ga % 2, i * NT + kt, :],
                                               proj[:, kt, v0 + h * HD:v0 + (h + 1) * HD],
                                               start=(kt == 0), stop=(kt == NT - 1))
                ins.then_inc(pv_done, 1)

            def token_tile(tt, kt):
                return xtok[:, tt, kt * P:(kt + 1) * P]

            pe.wait_ge(ident_in, 16)
            for l in range(DEPTH):
                making = operand(3 * l, token_tile,
                                 lambda tt: pe.wait_ge(ln_done, 2 * NT * l + tt + 1 - NT) if l else pe.wait_ge(x_in[tt], 16),
                                 1 if l else 0)
                for u in range(U_IN):
                    j = u // 2
                    if u % 2 == 0 and j >= 2:
                        pe.wait_ge(proj_in, (l * IN_CHUNKS + (1 if j == 2 else j)) * NT)
                    if u == 0:
                        column_units(BASE_IN[l], range(2), 2, CW, xT_hi, xT_lo, range(NT), proj_banks(j), 0, *making)
                    elif u > 1:
                        column_units(BASE_IN[l] + u, [u % 2], 2, CW, xT_hi, xT_lo, range(NT), proj_banks(j))
                    if u == 3:
                        pe.wait_ge(roped, 2 * l + 1)
                        for k in range(2):
                            qk_group(l, k)
                    if u == FIRST_SLOT - 1:
                        qk_ready(l, 2)
                        pe.wait_ge(proj_in, (l * IN_CHUNKS + 2) * NT)
                        scores(l, 0)
                        scores(l, 1)
                    if u in SLOTS:
                        a = SLOTS[u]
                        if a + 2 < SEG_END[1]:
                            scores(l, a + 2)
                        prob_transposes(l, a)
                        if a >= 1:
                            weigh_values(l, a - 1)
                a = SEG_END[1] - 1
                pe.wait_ge(roped, 2 * (l + 1))
                for k in range(2, 4):
                    qk_group(l, k)
                prob_transposes(l, a)
                weigh_values(l, a - 1)
                pe.wait_ge(proj_in, (l + 1) * IN_CHUNKS * NT)
                for k in range(4, 8):
                    qk_group(l, k)
                weigh_values(l, a)
                qk_ready(l, 8)
                scores(l, a + 1)
                scores(l, a + 2)
                for a in range(SEG_END[1], NG):
                    if a + 2 < NG:
                        scores(l, a + 2)
                    prob_transposes(l, a)
                    if a > SEG_END[1]:
                        weigh_values(l, a - 1)
                making = operand(3 * l + 1, lambda tt, kt: proj[:, tt, MERGED_TILES[kt]:MERGED_TILES[kt] + P],
                                 lambda tt: pe.wait_ge(merged, NSEG * l + NSEG - 1 + tt))
                weigh_values(l, NG - 1)
                row_units(BASE_OUT[l], [0, 1], U_OUT - 1, xT_hi, xT_lo, range(NT), 4, 0, *making)
                row_units(BASE_OUT[l] + 2, [2, 3], U_OUT - 1, xT_hi, xT_lo, range(NT), 4, 0, making[0])
                making = operand(3 * l + 2, token_tile, lambda tt: pe.wait_ge(ln_done, 2 * NT * l + tt + 1), 1)
                if l == 0:
                    feed_forward(BASE_FFN, FFN_W, U_FFN_COL, 0, xT_hi, xT_lo, range(NT), first=making)

            pe.wait_ge(wr_split, 2)
            tile_ready, next_tile, _ = making
            for tt in range(NT):
                if tt:
                    next_tile(tt)
                logits = bank[:, 6, tt * 2 * NE:(tt + 1) * 2 * NE]
                for kt in range(KT):
                    if kt % (KT // 2) == 0:
                        tile_ready(tt, kt // (KT // 2))
                    t = slice(tt * P, (tt + 1) * P)
                    nc.tensor.matmul(logits, xT_hi[:, kt, t], router_parts[:, kt, :], start=kt == 0, stop=False)
                    ins = nc.tensor.matmul(logits[:, 0:NE], xT_lo[:, kt, t], router_parts[:, kt, 0:NE], start=False,
                                           stop=kt == KT - 1)
            ins.then_inc(logit_psum, 1)
            pe.wait_ge(chosen_ready, 1)
            pe.wait_ge(consts_in, 16)
            before, ones = const("before"), const("ones")
            o = bank[:, 7, :]
            nc.tensor.matmul(o[:, 0:NE], before, chosen[:, 0, :], start=True, stop=True)
            nc.tensor.matmul(o[:, NE:2 * NE], ones, chosen[:, 0, :], start=True, stop=False)
            nc.tensor.matmul(o[:, NE:2 * NE], before, chosen[:, 1, :], start=False, stop=True)
            nc.tensor.matmul(o[:, 2 * NE:3 * NE], ones, chosen[:, 0, :], start=True, stop=False)
            nc.tensor.matmul(o[:, 2 * NE:3 * NE], ones, chosen[:, 1, :], start=False, stop=True).then_inc(pos_psum, 1)

            pe.wait_ge(routed, 1)
            n_large = pe.value_load(work[0:1, AT_LARGE:AT_LARGE + 1], min_val=0, max_val=MAX_LARGE)
            n_small = pe.value_load(work[0:1, AT_SMALL:AT_SMALL + 1], min_val=0, max_val=NE)

            def gather(i):
                pe.wait_ge(sel_ready, i + 1)
                for q in range(2):
                    for k in range(4):
                        kt = 4 * q + k
                        for tt in range(NT):
                            ins = nc.tensor.matmul(bank[:, 6 + q, k * P:(k + 1) * P], xtok[:, tt, kt * P:(kt + 1) * P],
                                                   sel[:, tt, :], start=(tt == 0), stop=(tt == NT - 1))
                    ins.then_inc(gather_psum, 1)

            with pe.If(n_small > 0):
                gather(0)
            with pe.If(n_large > 0):
                with pe.Fori(0, n_large) as r:
                    pe.wait_ge(added, r * 4 + 2)
                    feed_forward(BASE_MOE, MOE_W, MOE_COL, len(FFN_W), xT_hi, xT_lo, range(NT),
                                 r * U_MOE, r * len(MOE_W), last_added=r * 4 + 4)

            with pe.If(n_small > 0):
                with pe.Fori(0, n_small) as i:
                    r = pe.snap(n_large + i)
                    pe.wait_ge(added, r * 4 + 2)
                    pe.wait_ge(g_hi, i * 2 + 2)
                    pe.wait_ge(g_lo, i * 2 + 2)
                    for tt in range(NT):
                        ins = nc.tensor.transpose(bank[:, 6, tt * P:(tt + 1) * P], sel[:, tt, :], ident)
                    ins.then_inc(selT_psum, 1)

                    def gather_next():
                        with pe.If(i + 1 < n_small):
                            pe.wait_ge(selT_in, i + 1)
                            gather(i + 1)

                    feed_forward(BASE_MOE, MOE_W, MOE_COL, len(FFN_W), xg_hi, xg_lo, [0],
                                 r * U_MOE, r * len(MOE_W), gathering=gather_next,
                                 last_added=r * 4 + 4)
                    pe.wait_ge(selT_in, i + 1)
                    for q in range(4):
                        ch, tt = q // 2, q % 2
                        if tt == 0:
                            pe.wait_ge(y_lo, i * 2 + (ch + 1))
                        for y, stop in ((yo_hi, False), (yo_lo, True)):
                            ins = nc.tensor.matmul(bank[:, SCATTER_BANKS[q], :], selT[:, tt, :], y[:, 4 * ch:4 * ch + 4, :],
                                                   start=not stop, stop=stop)
                        ins.then_inc(scatter_psum, 1)


_INS = ["x", "w_in", "w_out", "beta_mix", "diff_lambda", "diff_norm_g", "na_rpb", "ln1_g", "ln1_b", "ln2_g", "ln2_b",
        "ffn_w_gate", "ffn_w_up", "ffn_w_down", "moe_w_router", "moe_w_gate", "moe_w_up", "moe_w_down"]


def kernel(**inputs):
    import concourse.bacc as bacc
    from concourse.bass_utils import run_bass_kernel_spmd

    nc = bacc.Bacc("TRN2", target_bir_lowering=False, num_devices=1)
    arrays, args = {}, []
    for name in _INS + ["table"]:
        a = np.ascontiguousarray(inputs[name]) if name != "table" else shape_table()
        arrays[f"in_{name}"] = a
        args.append(nc.dram_tensor(f"in_{name}", a.shape, F32, kind="ExternalInput").ap())
    args.append(nc.dram_tensor("out_x", (1, SEQ, D), F32, kind="ExternalOutput").ap())
    encoder(nc, *args)
    r = run_bass_kernel_spmd(nc, [arrays], core_ids=[0])
    return r.results[0]["out_x"]
```
